# Optimizing a Trainium2 kernel written in Bass

```python
import math
import jax, jax.numpy as jnp
from jax import lax
import numpy as np

D_MODEL = 1024
BATCH = 1
SEQ = 256
DEPTH = 2

GRID_W = 64
CTX_LEN = 256
N_HEADS = D_MODEL // 128
HEAD_DIM = 64
V_DIM = 2 * HEAD_DIM
QK_WIDTH = N_HEADS * 2 * HEAD_DIM
V_WIDTH = N_HEADS * V_DIM
F_GROUPS = 4
F_WIDTH = D_MODEL // 2
F_GROUP_DIM = F_WIDTH // F_GROUPS
IN_WIDTH = 2 * QK_WIDTH + V_WIDTH + F_WIDTH
Q_BLOCK = 128
ROPE_THETA = 10000.0
ROPE_AXIS_DIM = HEAD_DIM // 2
ROPE_HALF = ROPE_AXIS_DIM // 2
ATTN_SCALE = HEAD_DIM ** -0.5
N_EXPERTS = 16
N_GROUPS = 4
EXPERTS_PER_GROUP = N_EXPERTS // N_GROUPS
TOP_K = 2
D_EXPERT = D_MODEL // 2
EPS = 1e-6

kernel_name = "hybrid_diffattn_fourier_groupmoe_dit"

def rmsnorm(x, g):
    xf = x.astype(jnp.float32)
    y = xf * lax.rsqrt(jnp.mean(xf * xf, axis=-1, keepdims=True) + EPS)
    return (y * g.astype(jnp.float32)).astype(x.dtype)

def ada_chunks(cond, w, b):
    m = jax.nn.silu(cond) @ w + b
    return jnp.split(m, 6, axis=-1)

def modulate(h, shift, scale):
    return h * (1 + scale) + shift

def axial_rope_tables(n_tokens):
    rows = n_tokens // GRID_W
    row = jnp.broadcast_to(jnp.arange(rows)[:, None], (rows, GRID_W)).reshape(-1)
    col = jnp.broadcast_to(jnp.arange(GRID_W)[None, :], (rows, GRID_W)).reshape(-1)
    inv = ROPE_THETA ** (-jnp.arange(ROPE_HALF, dtype=jnp.float32) / ROPE_HALF)
    ang = jnp.concatenate([row[:, None] * inv, col[:, None] * inv], axis=-1)
    return jnp.cos(ang), jnp.sin(ang)

def apply_axial_rope(x, cos, sin):
    S = x.shape[1]
    xs = x.astype(jnp.float32).reshape(*x.shape[:-1], 2, 2, ROPE_HALF)
    x1, x2 = xs[..., 0, :], xs[..., 1, :]
    c = cos.reshape(S, 2, ROPE_HALF)[None, :, None, None]
    s = sin.reshape(S, 2, ROPE_HALF)[None, :, None, None]
    out = jnp.stack([x1 * c - x2 * s, x1 * s + x2 * c], axis=-2)
    return out.reshape(x.shape).astype(x.dtype)

def diff_attend(q, k, v, lam):
    s = jnp.einsum('bqhmd,bkhmd->bhmqk', q, k, preferred_element_type=jnp.float32) * ATTN_SCALE
    p = jax.nn.softmax(s, axis=-1)
    a = p[:, :, 0] - lam * p[:, :, 1]
    o = jnp.einsum('bhqk,bkhe->bqhe', a.astype(v.dtype), v, preferred_element_type=jnp.float32)
    return o.astype(v.dtype)

def fourier_mix(f):
    B, L, _ = f.shape
    fg = f.astype(jnp.float32).reshape(B, L, F_GROUPS, F_GROUP_DIM)
    z = jnp.fft.fftn(fg, axes=(1, 3), norm="ortho").real
    return z.reshape(B, L, F_WIDTH).astype(f.dtype)

def split_proj(u):
    lead = u.shape[:-1]
    q = u[..., :QK_WIDTH].reshape(*lead, N_HEADS, 2, HEAD_DIM)
    k = u[..., QK_WIDTH:2 * QK_WIDTH].reshape(*lead, N_HEADS, 2, HEAD_DIM)
    v = u[..., 2 * QK_WIDTH:2 * QK_WIDTH + V_WIDTH].reshape(*lead, N_HEADS, V_DIM)
    f = u[..., 2 * QK_WIDTH + V_WIDTH:]
    return q, k, v, f

def merge_branches(h, o, f, lam_init, g_subln, w_attn_out, w_four_out, w_gate, b_gate, w_out):
    o = rmsnorm(o, g_subln) * (1.0 - lam_init)
    y_attn = o.reshape(*o.shape[:-2], V_WIDTH) @ w_attn_out
    y_four = fourier_mix(f) @ w_four_out
    gates = jax.nn.sigmoid((h @ w_gate + b_gate).astype(jnp.float32)).astype(h.dtype)
    g_attn, g_four = gates[..., :D_MODEL], gates[..., D_MODEL:]
    return (g_attn * y_attn + g_four * y_four) @ w_out

def token_mixer(h_lat, h_ctx, w_in, lam, lam_init, g_subln, w_attn_out, w_four_out,
                w_gate, b_gate, w_out, cos, sin, with_ctx_out):
    B, S, _ = h_lat.shape
    q_l, k_l, v_l, f_l = split_proj(h_lat @ w_in)
    q_l = apply_axial_rope(q_l, cos, sin)
    k_l = apply_axial_rope(k_l, cos, sin)
    if with_ctx_out:
        q_c, k_c, v_c, f_c = split_proj(h_ctx @ w_in)
    else:
        u_kv = h_ctx @ w_in[:, QK_WIDTH:2 * QK_WIDTH + V_WIDTH]
        k_c = u_kv[..., :QK_WIDTH].reshape(*u_kv.shape[:-1], N_HEADS, 2, HEAD_DIM)
        v_c = u_kv[..., QK_WIDTH:].reshape(*u_kv.shape[:-1], N_HEADS, V_DIM)
    k_all = jnp.concatenate([k_c, k_l], axis=1)
    v_all = jnp.concatenate([v_c, v_l], axis=1)
    n_blk = S // Q_BLOCK
    qb = q_l.reshape(B, n_blk, Q_BLOCK, N_HEADS, 2, HEAD_DIM).swapaxes(0, 1)
    o_l = lax.map(lambda qq: diff_attend(qq, k_all, v_all, lam), qb)
    o_l = o_l.swapaxes(0, 1).reshape(B, S, N_HEADS, V_DIM)
    out_l = merge_branches(h_lat, o_l, f_l, lam_init, g_subln, w_attn_out, w_four_out,
                           w_gate, b_gate, w_out)
    if with_ctx_out:
        o_c = diff_attend(q_c, k_c, v_c, lam)
        out_c = merge_branches(h_ctx, o_c, f_c, lam_init, g_subln, w_attn_out, w_four_out,
                               w_gate, b_gate, w_out)
        return out_l, out_c
    return out_l, None

def moe(h, w_router, b_router, w_e_gate, w_e_up, w_e_down):
    aff = jax.nn.sigmoid(jnp.matmul(h, w_router, preferred_element_type=jnp.float32))
    sel = aff + b_router.astype(jnp.float32)
    group_score = lax.top_k(sel.reshape(-1, N_GROUPS, EXPERTS_PER_GROUP), TOP_K)[0].sum(-1)
    g_idx = jnp.argmax(group_score, axis=-1)
    in_group = (jnp.arange(N_EXPERTS) // EXPERTS_PER_GROUP)[None, :] == g_idx[:, None]
    _, top_idx = lax.top_k(jnp.where(in_group, sel, -jnp.inf), TOP_K)
    w_top = jnp.take_along_axis(aff, top_idx, axis=-1)
    w_top = w_top / jnp.sum(w_top, axis=-1, keepdims=True)
    gates = jnp.einsum('nk,nke->ne', w_top,
                       jax.nn.one_hot(top_idx, N_EXPERTS, dtype=jnp.float32)).astype(h.dtype)
    y = jnp.zeros_like(h)
    for e in range(N_EXPERTS):
        he = jax.nn.silu(h @ w_e_gate[e]) * (h @ w_e_up[e])
        y = y + gates[:, e:e + 1] * (he @ w_e_down[e])
    return y

def setup_inputs(seed: int = 0) -> dict:
    key = jax.random.key(seed)
    ks = jax.random.split(key, 24)
    f32 = jnp.float32
    L, D = DEPTH, D_MODEL
    nrm = lambda k, shape, s: jax.random.normal(k, shape, f32) * s
    return {
        "x": nrm(ks[0], (BATCH, SEQ, D), 1.0),
        "c": nrm(ks[1], (BATCH, D), 1.0),
        "ctx": nrm(ks[2], (BATCH, CTX_LEN, D), 1.0),
        "c_ctx": nrm(ks[3], (D,), 1.0),
        "w_ada": nrm(ks[4], (L, D, 6 * D), 0.5 * D ** -0.5),
        "b_ada": nrm(ks[5], (L, 6 * D), 0.02),
        "g_norm1": 1.0 + nrm(ks[6], (L, D), 0.02),
        "w_in": nrm(ks[7], (L, D, IN_WIDTH), D ** -0.5),
        "lam_qk": nrm(ks[8], (L, 4, HEAD_DIM), 0.1),
        "g_subln": 1.0 + nrm(ks[9], (L, V_DIM), 0.02),
        "w_attn_out": nrm(ks[10], (L, V_WIDTH, D), V_WIDTH ** -0.5),
        "w_four_out": nrm(ks[11], (L, F_WIDTH, D), F_WIDTH ** -0.5),
        "w_gate": nrm(ks[12], (L, D, 2 * D), D ** -0.5),
        "b_gate": nrm(ks[13], (L, 2 * D), 0.02),
        "w_out": nrm(ks[14], (L, D, D), D ** -0.5),
        "g_norm2": 1.0 + nrm(ks[15], (L, D), 0.02),
        "w_router": nrm(ks[16], (D, N_EXPERTS), D ** -0.5),
        "b_router": nrm(ks[17], (N_EXPERTS,), 0.01),
        "w_e_gate": nrm(ks[18], (L, N_EXPERTS, D, D_EXPERT), D ** -0.5),
        "w_e_up": nrm(ks[19], (L, N_EXPERTS, D, D_EXPERT), D ** -0.5),
        "w_e_down": nrm(ks[20], (L, N_EXPERTS, D_EXPERT, D), D_EXPERT ** -0.5),
        "g_final": 1.0 + nrm(ks[21], (D,), 0.02),
    }

def reference(x, c, ctx, c_ctx, w_ada, b_ada, g_norm1, w_in, lam_qk, g_subln, w_attn_out,
              w_four_out, w_gate, b_gate, w_out, g_norm2, w_router, b_router,
              w_e_gate, w_e_up, w_e_down, g_final):
    B, S, D = x.shape
    cos, sin = axial_rope_tables(S)
    for i in range(DEPTH):
        last = i == DEPTH - 1
        lam_init = 0.8 - 0.6 * math.exp(-0.3 * i)
        lp = lam_qk[i].astype(jnp.float32)
        lam = jnp.exp(jnp.sum(lp[0] * lp[1])) - jnp.exp(jnp.sum(lp[2] * lp[3])) + lam_init
        sh1, sc1, ga1, sh2, sc2, ga2 = [m[:, None, :] for m in ada_chunks(c, w_ada[i], b_ada[i])]
        csh1, csc1, cga1, csh2, csc2, cga2 = ada_chunks(c_ctx, w_ada[i], b_ada[i])
        h_l = modulate(rmsnorm(x, g_norm1[i]), sh1, sc1)
        h_c = modulate(rmsnorm(ctx, g_norm1[i]), csh1, csc1)
        out_l, out_c = token_mixer(h_l, h_c, w_in[i], lam, lam_init, g_subln[i], w_attn_out[i],
                                   w_four_out[i], w_gate[i], b_gate[i], w_out[i], cos, sin,
                                   not last)
        x = x + ga1 * out_l
        h2_l = modulate(rmsnorm(x, g_norm2[i]), sh2, sc2)
        if last:
            y = moe(h2_l.reshape(-1, D), w_router, b_router, w_e_gate[i], w_e_up[i], w_e_down[i])
            x = x + ga2 * y.reshape(B, S, D)
        else:
            ctx = ctx + cga1 * out_c
            h2_c = modulate(rmsnorm(ctx, g_norm2[i]), csh2, csc2)
            toks = jnp.concatenate([h2_c, h2_l], axis=1)
            y = moe(toks.reshape(-1, D), w_router, b_router, w_e_gate[i], w_e_up[i],
                    w_e_down[i]).reshape(B, CTX_LEN + S, D)
            ctx = ctx + cga2 * y[:, :CTX_LEN]
            x = x + ga2 * y[:, CTX_LEN:]
    return rmsnorm(x, g_final)


_drawn_inputs = setup_inputs


def setup_inputs(seed=0):
    import zlib

    import numpy as np

    out = dict(_drawn_inputs(seed))
    spreads = {}
    factors = {'g_norm1': 4.028, 'lam_qk': 3.019, 'g_subln': 3.098, 'b_gate': 4.179, 'g_final': 2.75}
    for name, (base, spread) in spreads.items():
        noise = np.random.default_rng([zlib.crc32(name.encode()), seed]).standard_normal(out[name].shape)
        drawn = base * np.exp(spread * noise) if base else spread * noise
        out[name] = __import__('jax').numpy.asarray(drawn.astype(out[name].dtype))
    for name, factor in factors.items():
        out[name] = (out[name] * factor).astype(out[name].dtype)
    return out
```

```python
import math
from contextlib import ExitStack

import numpy as np
import concourse.bass as bass
from concourse import mybir

F32 = mybir.dt.float32
F32R = mybir.dt.float32r
I32 = mybir.dt.int32
U32 = mybir.dt.uint32
ACT = mybir.ActivationFunctionType
ALU = mybir.AluOpType
AX = mybir.AxisListType

P = 128
D = 1024
KT = D // P
T = 512
SEQ = 256
DEPTH = 2
HEADS = 8
HD = 64
FW = D // 2
FG = FW // P
NE = 16
DE = D // 2
KE = DE // P
EPS = 1e-6
ATT_SCALE = HD ** -0.5
BIG = 3.0e38

CK = 2
CW = 512
RAW = 8
SPL = 4
BANKS = 7
EXP_CHUNKS = 12

V_BADA, V_G1, V_G2, V_BG, V_SUB, V_GF, V_C = 0, 48, 56, 64, 80, 81, 89
V_ROWS = 105

C_ID, C_ONE, C_TRI = 0, 128, 256
C_RC, C_RS = 384, 640
C_CD = 896
C_CL, C_SL = 1152, 1664
C_KG, C_KE = 2176, 2180
C_COLS = 2196


def constants():
    t = np.zeros((P, C_COLS), np.float64)
    p = np.arange(P)
    t[:, C_ID:C_ID + P] = np.eye(P)
    t[:, C_ONE:C_ONE + P] = 1.0
    t[:, C_TRI:C_TRI + P] = p[:, None] < p[None, :]
    tok = np.arange(SEQ)
    d = p % HD
    axis, half, j = d // 32, (d % 32) // 16, d % 16
    inv = 10000.0 ** (-j / 16.0)
    pos = np.where(axis[:, None] == 0, tok[None, :] // 64, tok[None, :] % 64)
    ang = pos * inv[:, None]
    t[:, C_RC:C_RC + SEQ] = np.cos(ang)
    t[:, C_RS:C_RS + SEQ] = np.sin(ang) * np.where(half == 0, -1.0, 1.0)[:, None]
    a = 2 * np.pi * np.outer(p, p) / P
    t[:, C_CD:C_CD + P] = np.cos(a) / np.sqrt(P)
    t[:, C_CD + P:C_CD + 2 * P] = np.sin(a) / np.sqrt(P)
    for k in range(2):
        b = 2 * np.pi * np.outer(k * P + p, tok) / SEQ
        t[:, C_CL + k * SEQ:C_CL + (k + 1) * SEQ] = np.cos(b) / np.sqrt(SEQ)
        t[:, C_SL + k * SEQ:C_SL + (k + 1) * SEQ] = -np.sin(b) / np.sqrt(SEQ)
    t[:, C_KG:C_KG + 4] = 4 - np.arange(4)
    t[:, C_KE:C_KE + NE] = NE - np.arange(NE)
    return t.astype(np.float32)


def steps_of(layer):
    proj = [("F", 0), ("GF", 0), ("GF", 1), ("WF", 0)] + [("QK", g) for g in range(4)]
    proj += [("V", 0), ("V", 1), ("GA", 0), ("GA", 1)]
    out = []
    if layer == 0:
        ada = [("ADA", 0, g) for g in range(4, 12)] + [("ADA", 1, g) for g in range(12)]
        for n, s in enumerate(proj):
            take = 2 if n % 3 else 1
            out.append(s)
            out += ada[:take]
            ada = ada[take:]
        assert not ada
    else:
        out = proj
    return out + [("WA", 0), ("WA", 1), ("WO", 0), ("WO", 1)]


def build(nc, x, c, ctx_tok, c_ctx, w_ada, b_ada, g_norm1, w_in, lam_qk, g_subln, w_attn_out,
          w_four_out, w_gate, b_gate, w_out, g_norm2, w_router, b_router, w_e_gate, w_e_up,
          w_e_down, g_final, consts, out):
    es = ExitStack()

    base = -(-nc.sbuf_base // 64) * 64
    at = [base]

    def place(nbytes):
        o = at[0]
        at[0] += -(-nbytes // 32) * 32
        assert at[0] <= nc.sbuf_usable_end, (at[0], nc.sbuf_usable_end)
        return o

    def view(name, shape, dt, offset):
        return nc.alloc_sbuf_tensor_at(name, shape, dt, offset=offset)

    KB = 1024
    o_raw, o_hi, o_lo = place(RAW * 4 * KB), place(SPL * 4 * KB), place(SPL * 4 * KB)
    raw = view("w_raw", [P, RAW, CK, CW], F32, o_raw)
    whi = view("w_hi", [P, SPL, CK, CW], F32R, o_hi)
    wlo = view("w_lo", [P, SPL, CK, CW], F32R, o_lo)
    cst = view("cst", [P, C_COLS], F32, place(C_COLS * 4))
    rX, rH, rQ, rV, rG = place(16 * KB), place(32 * KB), place(32 * KB), place(16 * KB), place(32 * KB)
    X = view("x_feat", [P, KT, T], F32, rX)
    E = view("att_e", [P, 2, 2, T], F32, rX)
    A = view("att_a", [P, 2, T], F32, rX + 8 * KB)
    AT = view("att_at", [P, 2, T], F32, rX + 12 * KB)
    Hhi = view("h_hi", [P, KT, T], F32R, rH)
    Hlo = view("h_lo", [P, KT, T], F32R, rH + 16 * KB)
    O = view("o_tok", [P, 4, HEADS, P], F32, rH)
    h2T = view("h2_feat", [P, KT, T], F32, rH)
    h2tok = view("h2_tok", [P, 4, D], F32, rH + 16 * KB)
    QK = view("qk", [P, 2 * HEADS, T], F32, rQ)
    Zhi = view("z_hi", [P, FG, T], F32R, rQ)
    Zlo = view("z_lo", [P, FG, T], F32R, rQ + 8 * KB)
    OThi = view("ot_hi", [P, KT, T], F32R, rQ)
    OTlo = view("ot_lo", [P, KT, T], F32R, rQ + 16 * KB)
    sq = view("sq", [P, 2, T], F32, rQ)
    std = view("std", [P, T], F32, rQ + 4 * KB)
    rinv = view("rinv", [P, T], F32, rQ + 6 * KB)
    xn = view("xn", [P, 2, T], F32, rQ + 8 * KB)
    hf = view("hf", [P, 2, T], F32, rQ + 12 * KB)
    xg = view("xg", [P, 2, D], F32, rQ)
    xhi = view("xg_hi", [P, KT, P], F32R, rQ + 8 * KB)
    xlo = view("xg_lo", [P, KT, P], F32R, rQ + 12 * KB)
    ytile = view("ytile", [P, 2, D], F32, rQ + 16 * KB)
    zrow = view("zrow", [P, D], F32, rQ + 28 * KB)
    outt = view("outt", [P, 2, D], F32, rG)
    V = view("v_tok", [P, 4, D], F32, rV)
    FT = view("f_feat", [P, FG, T], F32, rV)
    osq = view("o_sq", [P, 4, HEADS, P], F32, rV)
    ot32 = view("ot32", [P, 2, T], F32, rV)
    sg = view("sg", [P, DE], F32, rV)
    gu = view("gu", [P, DE], F32, rV + 2 * KB)
    he = view("he", [P, DE], F32, rV + 4 * KB)
    hehi = view("he_hi", [P, KE, P], F32R, rV + 6 * KB)
    helo = view("he_lo", [P, KE, P], F32R, rV + 8 * KB)
    hT32 = view("he32", [P, KE, P], F32, rV + 10 * KB)
    G = view("g_four", [P, KT, T], F32, rG)
    GA = view("g_attn", [P, KT, T], F32, rG + 16 * KB)
    Y = view("dft_y", [P, 2, FG, 2, 2 * P], F32, rG + 16 * KB)
    rt = view("rope_t", [P, 2, SEQ], F32, rG + 16 * KB)
    tok0 = view("tok0", [P, 4, D], F32, rG)
    y1 = view("y1", [P, 4, D], F32, rG)
    y2 = view("y2", [P, 4, D], F32, rG + 16 * KB)
    xT32 = view("xT32", [P, KT, P], F32, rG)

    def small(name, shape, dt=F32):
        return view(name, shape, dt, place(int(np.prod(shape[1:])) * 4))

    vrow = view("vrow", [P, P], F32, rV)
    vrow1 = view("vrow1", [P, P], F32, rV + KB)
    vec = [small(f"vec{i}", [P, V_ROWS]) for i in range(DEPTH)]
    mod = [small(f"mod{i}", [P, 48, 2]) for i in range(DEPTH)]
    sc1 = [small(f"sc1_{i}", [P, KT, 2]) for i in range(DEPTH)]
    sc2 = [small(f"sc2_{i}", [P, KT, 2]) for i in range(DEPTH)]
    csig = small("csig", [P, 16])
    csil = small("csil", [P, 16])
    cond = small("cond", [P, KT, 4], F32R)
    zero = small("zero", [P, P])
    wr = small("wr", [P, KT, NE])
    brb = small("brb", [P, NE])
    epst = small("epst", [P, 1])
    lamv = small("lamv", [P, 4, HD])
    lprod = small("lprod", [P, 2, HD])
    lsum = small("lsum", [P, 2])
    lexp = small("lexp", [P, 2])
    nlam = small("nlam", [P, 1])
    gsub = small("gsub", [P, 1])
    amax = small("amax", [P, 2, 2])
    aneg = small("aneg", [P, 2, 2])
    asum = small("asum", [P, 2, 2])
    arec = small("arec", [P, 2, 2])
    arec1 = small("arec1", [P, 2])
    oss = small("oss", [P, 4 * HEADS])
    ostd = small("ostd", [P, 4 * HEADS])
    orin = small("orin", [P, 4 * HEADS])
    r_at = [rV]

    def passing(name, shape, dt=F32):
        o = r_at[0]
        r_at[0] += -(-int(np.prod(shape[1:])) * 4 // 32) * 32
        return view(name, shape, dt, o)

    aff = passing("aff", [P, 4, NE])
    sel = passing("sel", [P, 4, NE])
    pr = passing("pr", [P, 4, 4, 6])
    gsc = passing("gsc", [P, 4, 4])
    gmx = passing("gmx", [P, 4])
    geq = passing("geq", [P, 4, 4])
    ing = passing("ing", [P, 4, 4])
    msk = passing("msk", [P, 4, NE])
    ta = passing("ta", [P, 4, NE])
    tb = passing("tb", [P, 4, NE])
    tm = passing("tm", [P, 4])
    oh1 = passing("oh1", [P, 4, NE])
    oh2 = passing("oh2", [P, 4, NE])
    asg = passing("asg", [P, 4, NE])
    w12 = passing("w12", [P, 2, 4])
    wsum = passing("wsum", [P, 4])
    gates = small("gates", [P, 2, 4])
    rank = passing("rank", [P, 5, NE])
    cum = passing("cum", [P, 2, NE])
    start_f = passing("start_f", [P, NE])
    pos = passing("pos", [P, 4, NE])
    loc_f = passing("loc_f", [P, 2, 4])
    loc = small("loc", [P, 2, 4], U32)
    starts = small("starts", [P, NE], I32)
    most_f = passing("most_f", [P, 1])
    most = small("most", [P, 1], I32)

    ps = es.enter_context(nc.psum_tensor("ps", [P, 8, 512], F32))

    ROWS = 2 * T + 4 * P
    xkeep = nc.dram_tensor("xkeep", (P, KT * T), F32).ap()
    hbuf = nc.dram_tensor("hbuf", (ROWS, D), F32).ap()
    ybuf = nc.dram_tensor("ybuf", (ROWS, D), F32).ap()

    def sem(name):
        return es.enter_context(nc.semaphore(name))

    def per_layer(*names):
        return [[sem(f"{name}_{i}") for i in range(DEPTH)] for name in names]

    raw_in = [sem(f"raw_in{i}") for i in range(RAW)]
    hi_ready, lo_ready, w_used = sem("hi_ready"), sem("lo_ready"), sem("w_used")
    cst_in, tok_in, small_in, vec_in = sem("cst_in"), sem("tok_in"), sem("small_in"), sem("vec_in")
    filled, pad_out = sem("filled"), sem("pad_out")
    tile_done = sem("tile_done")
    free_act, free_dve = sem("free_act"), sem("free_dve")
    dve_chain = sem("dve_chain")
    cond_sig, cond_sil, cond_hi, cond_ready = sem("cond_sig"), sem("cond_sil"), sem("cond_hi"), sem("cond_ready")
    mod_a, mod_b = sem("mod_a"), sem("mod_b")
    n_sq, n_squ, n_xn, n_hf, n_hi, n_lo = (sem(f"n_{k}") for k in ("sq", "squ", "xn", "hf", "hi", "lo"))
    norms = {"n1_0": 0, "n2_0": 1, "n1_1": 2, "n2_1": 3, "nf": 4}
    x_kept, x_back, roped, z_hi = per_layer("x_kept", "x_back", "roped", "z_hi")
    lam_in, lam_s, lam_e = per_layer("lam_in", "lam_s", "lam_e")
    a_s, a_neg, a_exp, a_comb, a_tr, a_trc, a_pv, a_oc = (
        sem(f"a_{k}") for k in ("s", "neg", "exp", "comb", "tr", "trc", "pv", "oc"))
    o_sq, o_ss, o_std, o_nrm, ot_h, ot_l, m_f, m_h, m_l = per_layer(
        "o_sq", "o_ss", "o_std", "o_nrm", "ot_h", "ot_l", "m_f", "m_h", "m_l")
    rt_asg, rt_loc, sc_out, e_out, y_free = per_layer("rt_asg", "rt_loc", "sc_out", "e_out", "y_free")
    e_in = [sem("e_in_a"), sem("e_in_b")]
    e_xt, e_xh, e_xl, e_sig, e_gu, e_he, e_ht, e_hh, e_hl, e_ya, e_yd = (
        sem(f"e_{k}") for k in ("xt", "xh", "xl", "sig", "gu", "he", "ht", "hh", "hl", "ya", "yd"))
    f_go, f_in, f_dn, f_out, f_pe, f_act, f_dve = per_layer("f_go", "f_in", "f_dn", "f_out", "f_pe", "f_act", "f_dve")
    y_in, y_sum = per_layer("y_in", "y_sum")
    out_ready, out_done = sem("out_ready"), sem("out_done")

    cs = lambda a, n: cst[:, a:a + n]
    ident, ones, tri = cs(C_ID, P), cs(C_ONE, P), cs(C_TRI, P)

    col0 = [0, SEQ]
    tiles = [[0, 1, 2, 3], [2, 3]]
    items = [[(h, q) for h in range(HEADS) for q in tiles[i]] for i in range(DEPTH)]
    first_item = [0, len(items[0])]
    keys = lambda q: SEQ if q < 2 else T

    def w_chunk(w, k0, n0):
        return w[k0 * P:(k0 + CK) * P, n0:n0 + CW].rearrange("(k p) n -> p k n", p=P)

    def step_chunks(i, s):
        kind = s[0]
        if kind == "ADA":
            return [w_chunk(w_ada[s[1]], CK * k, CW * s[2]) for k in range(4)]
        if kind == "WF":
            return [w_chunk(w_four_out[i], CK * k, CW * n) for n in range(2) for k in range(2)]
        w, n0 = {"F": (w_in[i], 3 * D), "GF": (w_gate[i], D), "QK": (w_in[i], 0), "V": (w_in[i], 2 * D),
                 "GA": (w_gate[i], 0), "WA": (w_attn_out[i], 0), "WO": (w_out[i], 0)}[kind]
        return [w_chunk(w, CK * k, n0 + CW * s[1]) for k in range(4)]

    ADA_A = 16
    mix0, exp0 = [], []
    n = ADA_A
    for i in range(DEPTH):
        mix0.append(n)
        n += 4 * len(steps_of(i))
        exp0.append(n)
        n += NE * EXP_CHUNKS
    assert all(v % RAW == 0 for v in exp0)

    plan, owner = {}, []

    def add_tile(key, by):
        plan[key] = len(owner)
        owner.append(by)

    dft = [[(s, g) for s in range(i, 2) for g in range(FG)] for i in range(DEPTH)]
    for i in range(DEPTH):
        add_tile(("vec", i), "dve")
    for k in range(KT):
        add_tile(("x0", k), "act" if k % 2 else "dve")
    for i in range(DEPTH):
        add_tile((i, "n1"), "act")
        for s in steps_of(i):
            if s == ("GF", 0):
                for sg_ in dft[i]:
                    add_tile((i, "Y") + sg_, "act")
            if s == ("GF", 1):
                for sg_ in dft[i]:
                    add_tile((i, "Z") + sg_, "dve")
            if s == ("WA", 0):
                for h in range(HEADS):
                    add_tile((i, "OT", h), "dve")
            for t in range({"ADA": 0, "WF": 8}.get(s[0], 4)):
                add_tile((i, s[0], s[1], t), "dve" if s[0] in ("WF", "WA", "WO") else "act")
        add_tile((i, "n2"), "act")
        add_tile((i, "log"), "act")
        for t in tiles[i]:
            for half in range(2):
                add_tile((i, "h2", t, half), "act" if half else "dve")
        add_tile((i, "rank"), "dve")
        for k in range(KT):
            add_tile((i, "yT", k), "dve")
    add_tile(("nf",), "act")
    for t in range(2):
        for half in range(2):
            add_tile(("out", t, half), "act" if half else "dve")

    done_at, signals = {}, 0
    for key, t in sorted(plan.items(), key=lambda kv: kv[1]):
        i = key[0]
        if i in (0, 1) and (i,) + key[1:3] and key[1] in ("F", "GF", "WF", "QK", "V", "GA", "WA", "WO") and key[3] % 4 == 3:
            n_step = mix0[i] + 4 * steps_of(i).index(key[1:3])
            done_at[key] = (w_used, n_step + (4 if key[1] != "WF" else 2 + 2 * (key[3] // 4)))
        else:
            signals += 1
            done_at[key] = (tile_done, signals)

    def bank(key):
        return ps[:, plan[key] % BANKS, :]

    def emptied(t):
        by = owner[t]
        return (free_act if by == "act" else free_dve), sum(1 for o in owner[:t + 1] if o == by)

    def take_tile(eng, key):
        t = plan[key]
        if t >= BANKS:
            s, v = emptied(t - BANKS)
            eng.wait_ge(s, v)

    def wait_tile(eng, key):
        eng.wait_ge(*done_at[key])

    def wait_emptied(eng, key):
        eng.wait_ge(*emptied(plan[key]))

    def wait_all_emptied(eng, key):
        for by, s_ in (("act", free_act), ("dve", free_dve)):
            eng.wait_ge(s_, sum(1 for o in owner[:plan[key] + 1] if o == by))

    def scaled(n, it, per):
        return n if it is None else n + it * per

    def raw_value(n, it, per):
        v = 16 * (n // RAW + 1)
        return v if it is None else v + it * (16 * (per // RAW))

    def load(sp, n, src, it=None, per=0):
        if it is not None or n >= RAW:
            sp.wait_ge(lo_ready, scaled(n - RAW + 1, it, per))
        sp.dma_start(raw[:, n % RAW, :, :], src).then_inc(raw_in[n % RAW], 16)

    def split_hi(act, n, it=None, per=0):
        act.wait_ge(raw_in[n % RAW], raw_value(n, it, per))
        if it is not None or n >= SPL:
            act.wait_ge(w_used, scaled(n - SPL + 1, it, per))
        act.activation(whi[:, n % SPL, :, :], raw[:, n % RAW, :, :], ACT.Copy).then_inc(hi_ready, 1)

    def split_lo(dve, n, it=None, per=0):
        dve.wait_ge(hi_ready, scaled(n + 1, it, per))
        dve.tensor_tensor(wlo[:, n % SPL, :, :], raw[:, n % RAW, :, :],
                          whi[:, n % SPL, :, :].bitcast(F32), ALU.subtract).then_inc(lo_ready, 1)

    def product(pe, acc, sh, sl, mh, ml, first, last):
        pe.matmul(acc, sh, mh, start=first, stop=False, skip_group_check=True)
        pe.matmul(acc, sh, ml, start=False, stop=False, skip_group_check=True)
        return pe.matmul(acc, sl, mh, start=False, stop=last, skip_group_check=True)

    block = es.enter_context(nc.Block())

    @block.sync
    def _(sp):
        sp.dma_start(cst[:, :], consts).then_inc(cst_in, 16)
        for s_, src in enumerate((ctx_tok, x)):
            sp.dma_start(tok0[:, 2 * s_:2 * s_ + 2, :], src[0].rearrange("(t p) n -> p t n", p=P)).then_inc(tok_in, 16)
        for n in range(ADA_A):
            load(sp, n, w_chunk(w_ada[0], CK * (n % 4), CW * (n // 4)))
        for i in range(DEPTH):
            n = mix0[i]
            for s in steps_of(i):
                for src in step_chunks(i, s):
                    load(sp, n, src)
                    n += 1
            with sp.Fori(0, NE // 2) as it:
                for j in range(2):
                    for m, (w, kk, nn) in enumerate([(w_e_gate, 4, 1), (w_e_up, 4, 1), (w_e_down, 2, 2)]):
                        we = w[i, 2 * it + j]
                        for ch in range(4):
                            k, cc = ch % kk, ch // kk
                            load(sp, exp0[i] + 12 * j + 4 * m + ch, w_chunk(we, CK * k, CW * cc), it, 24)
            sp.wait_ge(rt_loc[i], 1)
            over = sp.value_load(most[0:1, 0:1], min_val=0, max_val=T)
            nt = len(tiles[i])
            with sp.If(over > P):
                sp.wait_ge(lo_ready, exp0[i] + NE * EXP_CHUNKS)
                with sp.Fori(0, NE) as e:
                    first = sp.value_load(starts[0:1, bass.ds(e, 1)], min_val=0, max_val=2 * T)
                    for r in range(nt):
                        k = e * nt + r
                        sp.wait_ge(f_go[i], k + 1)
                        sp.dma_start(xg[:, 0, :], hbuf[bass.ds(first + r * P, P), :]).then_inc(f_in[i], 16)
                        for m, w in enumerate((w_e_gate, w_e_up)):
                            sp.dma_start(raw[:, 4 * m:4 * m + 4, :, :].rearrange("p s k n -> p (s k) n"),
                                         w[i, e].rearrange("(k p) n -> p k n", p=P)).then_inc(f_in[i], 16)
                        sp.wait_ge(f_pe[i], k * 4 + 2)
                        sp.dma_start(raw[:, 0:4, :, :].rearrange("p s k n -> p (s k n)").rearrange("p (k n) -> p k n", n=D),
                                     w_e_down[i, e].rearrange("(k p) n -> p k n", p=P)).then_inc(f_dn[i], 16)
                        sp.wait_ge(f_dve[i], k * 5 + 5)
                        sp.dma_start(ybuf[bass.ds(first + r * P, P), :], ytile[:, 0, :]).then_inc(f_out[i], 16)
                        sp.wait_ge(f_out[i], (k + 1) * 16)
                        sp.sem_inc(f_go[i], 1)

        sp.wait_ge(out_ready, 4)
        sp.dma_start(out[0].rearrange("(t p) n -> p t n", p=P), outt[:, :, :]).then_inc(out_done, 16)
        sp.wait_ge(out_done, 16)

    @block.gpsimd
    def _(pool):
        pool.memset(zero[:, :], 0.0).then_inc(filled, 1)
        pool.memset(epst[:, :], EPS).then_inc(filled, 1)
        pool.memset(zrow[:, :], 0.0).then_inc(filled, 1)
        for i, dst in enumerate((vrow, vrow1)):
            rows = [(V_BADA, b_ada[i], 48), (V_G1, g_norm1[i], 8), (V_G2, g_norm2[i], 8), (V_BG, b_gate[i], 16),
                    (V_SUB, g_subln[i], 1), (V_GF, g_final, 8), (V_C, c[0], 8), (V_C + 8, c_ctx, 8)]
            for r, src, k in rows:
                pool.dma_start(dst[r:r + k, :], src.rearrange("(k p) -> k p", p=P)).then_inc(vec_in, 16)
        pool.dma_start(wr[:, :, :], w_router.rearrange("(k p) n -> p k n", p=P)).then_inc(small_in, 16)
        pool.dma_start(brb[:, :], b_router.rearrange("(a n) -> a n", a=1).to_broadcast([P, NE])).then_inc(small_in, 16)
        pool.wait_ge(filled, 3)
        for r in range(2 * T // P, ROWS // P):
            pool.dma_start(hbuf[r * P:(r + 1) * P, :], zrow[:, :]).then_inc(pad_out, 16)
        for i in range(DEPTH):
            wait_all_emptied(pool, ("x0", KT - 1) if i == 0 else (0, "yT", KT - 1))
            pool.dma_start(xkeep, X[:, :, :].rearrange("p k t -> p (k t)")).then_inc(x_kept[i], 16)
            if i:
                pool.wait_ge(lam_e[0], 1)
            pool.dma_start(lamv[:, :, :], lam_qk[i:i + 1].to_broadcast([P, 4, HD])).then_inc(lam_in[i], 16)
            pool.wait_ge(x_kept[i], 16)
            pool.wait_ge(a_oc, first_item[i] + len(items[i]))
            pool.dma_start(X[:, :, :].rearrange("p k t -> p (k t)"), xkeep).then_inc(x_back[i], 16)
            pool.wait_ge(rt_loc[i], 1)
            wait_all_emptied(pool, (i, "rank"))
            if i == 0:
                pool.wait_ge(pad_out, 16 * (ROWS // P - 2 * T // P))
            for s in range(2):
                for t in tiles[i]:
                    pool.indirect_dma_start(hbuf, bass.IndirectOffsetOnAxis(ap=loc[:, s, t:t + 1], axis=0),
                                            h2tok[:, t, :], None).then_inc(sc_out[i], 16)
            pool.wait_ge(sc_out[i], 32 * len(tiles[i]))
            pool.sem_inc(y_free[i], 2)

            def first_row(e):
                return pool.value_load(starts[0:1, bass.ds(e, 1)], min_val=0, max_val=2 * T)

            def fetch(e, j):
                pool.dma_start(xg[:, j, :], hbuf[bass.ds(first_row(e), P), :]).then_inc(e_in[j], 16)

            def store(e, j):
                pool.wait_ge(e_ya, NE * i + e + 1)
                pool.wait_ge(e_yd, NE * i + e + 1)
                pool.dma_start(ybuf[bass.ds(first_row(e), P), :], ytile[:, j, :]).then_inc(e_out[i], 16)
                pool.wait_ge(e_out[i], (e + 1) * 16)
                pool.sem_inc(y_free[i], 1)

            fetch(0, 0)
            fetch(1, 1)
            with pool.Fori(0, NE // 2 - 1) as it:
                for j in range(2):
                    pool.wait_ge(e_xt, NE * i + 2 * it + j + 1)
                    fetch(2 * it + 2 + j, j)
                    store(2 * it + j, j)
            for j in range(2):
                store(NE - 2 + j, j)
            over = pool.value_load(most[0:1, 0:1], min_val=0, max_val=T)
            with pool.If(over > P):
                pool.sem_inc(f_go[i], 1)
                pool.wait_ge(f_out[i], 16 * NE * len(tiles[i]))
            for s, dst in enumerate((y1, y2)):
                for t in tiles[i]:
                    pool.indirect_dma_start(dst[:, t, :], None, ybuf[0:2 * P * len(tiles[i]), :],
                                            bass.IndirectOffsetOnAxis(ap=loc[:, s, t:t + 1], axis=0)).then_inc(y_in[i], 16)

    @block.tensor
    def _(pe):
        pe.wait_ge(cst_in, 16)
        pe.wait_ge(vec_in, 16 * 16)
        for i, src in enumerate((vrow, vrow1)):
            pe.transpose(bank(("vec", i))[:, 0:V_ROWS], src[0:V_ROWS, :], ident[0:V_ROWS, 0:V_ROWS]).then_inc(tile_done, 1)
        pe.wait_ge(tok_in, 32)
        for k in range(KT):
            take_tile(pe, ("x0", k))
            for t in range(4):
                m = pe.transpose(bank(("x0", k))[:, t * P:(t + 1) * P], tok0[:, t, k * P:(k + 1) * P], ident)
            m.then_inc(tile_done, 1)

        def ada_open(cols):
            pe.matmul(ps[:, 7, cols], zero[:, :], cst[:, C_RC:C_RC + (cols.stop - cols.start)], start=True, stop=False,
                      skip_group_check=True)

        def ada_step(n, g, last):
            for ch in range(4):
                pe.wait_ge(lo_ready, n + ch + 1)
                for k in range(CK):
                    for ct in range(4):
                        acc = ps[:, 7, 16 * g + 4 * ct:16 * g + 4 * ct + 4]
                        wcol = slice(ct * P, (ct + 1) * P)
                        kt = CK * ch + k
                        pe.matmul(acc, whi[:, (n + ch) % SPL, k, wcol], cond[:, kt, :], start=False, stop=False,
                                  skip_group_check=True)
                        m = pe.matmul(acc, wlo[:, (n + ch) % SPL, k, wcol], cond[:, kt, :], start=False,
                                      stop=last and kt == KT - 1, skip_group_check=True)
                m.then_inc(w_used, 1)

        def norm_sum(name, key, c0):
            o, os = KT * norms[name], KT * (norms[name] // 2)
            take_tile(pe, key)
            for k in range(KT):
                pe.wait_ge(n_sq, o + k + 1)
                m = pe.matmul(bank(key)[:, c0:T], ones, sq[:, k % 2, c0:T], start=k == 0, stop=k == KT - 1)
                m.then_inc(n_squ if k < KT - 1 else tile_done, 1)

        def by_weights(n, keys_, c0, moving, chunks):
            for ch in range(chunks):
                pe.wait_ge(lo_ready, n + ch + 1)
                for k in range(CK):
                    kt = CK * ch + k
                    for ct in range(4):
                        if kt == 0:
                            take_tile(pe, keys_[ct])
                        wcol = slice(ct * P, (ct + 1) * P)
                        m = product(pe, bank(keys_[ct])[:, c0:T], whi[:, (n + ch) % SPL, k, wcol],
                                    wlo[:, (n + ch) % SPL, k, wcol], moving[0][:, kt, c0:T], moving[1][:, kt, c0:T],
                                    kt == 0, kt == CK * chunks - 1)
                        if kt == CK * chunks - 1 and ct < 3:
                            m.then_inc(tile_done, 1)
                m.then_inc(w_used, 1)

        def by_tokens(n, keys_):
            for ch in range(4):
                pe.wait_ge(lo_ready, n + ch + 1)
                for k in range(CK):
                    kt = CK * ch + k
                    for t in range(4):
                        if kt == 0:
                            take_tile(pe, keys_[t])
                        tc = slice(t * P, (t + 1) * P)
                        m = product(pe, bank(keys_[t])[:, :], Hhi[:, kt, tc], Hlo[:, kt, tc],
                                    whi[:, (n + ch) % SPL, k, :], wlo[:, (n + ch) % SPL, k, :], kt == 0, kt == KT - 1)
                        if kt == KT - 1 and t < 3:
                            m.then_inc(tile_done, 1)
                m.then_inc(w_used, 1)

        def dft_channels(i):
            for s, g in dft[i]:
                key = (i, "Y", s, g)
                take_tile(pe, key)
                wait_emptied(pe, (i, "F", 0, g))
                for t in range(2):
                    c0 = s * SEQ + t * P
                    m = pe.matmul(bank(key)[:, t * 2 * P:(t + 1) * 2 * P], FT[:, g, c0:c0 + P], cs(C_CD, 2 * P),
                                  start=True, stop=True, skip_group_check=True)
                m.then_inc(tile_done, 1)

        def dft_tokens(i):
            for s, g in dft[i]:
                key = (i, "Z", s, g)
                take_tile(pe, key)
                wait_emptied(pe, (i, "Y", s, g))
                for t in range(2):
                    pe.matmul(bank(key)[:, 0:SEQ], Y[:, s, g, t, 0:P], cs(C_CL + t * SEQ, SEQ), start=t == 0, stop=False)
                    m = pe.matmul(bank(key)[:, 0:SEQ], Y[:, s, g, t, P:2 * P], cs(C_SL + t * SEQ, SEQ), start=False,
                                  stop=t == 1)
                m.then_inc(tile_done, 1)

        def attention(i):
            wait_all_emptied(pe, (i, "GA", 1, 3))
            pe.wait_ge(roped[i], 2 * HEADS)
            pe.wait_ge(mod_b, 2)
            its = items[i]
            for j in range(len(its) + 2):
                if j < len(its):
                    h, q = its[j]
                    if j >= 2:
                        pe.wait_ge(a_exp, 2 * first_item[i] + 2 * (j - 2) + 2)
                    for m_ in range(2):
                        d = slice(m_ * HD, (m_ + 1) * HD)
                        m = pe.matmul(ps[:, 2 * (j % 2) + m_, 0:keys(q)], QK[d, h, q * P:(q + 1) * P],
                                      QK[d, HEADS + h, 0:keys(q)], start=True, stop=True)
                    m.then_inc(a_s, 1)
                if 1 <= j <= len(its):
                    h, q = its[j - 1]
                    b = (j - 1) % 2
                    pe.wait_ge(a_comb, first_item[i] + j)
                    if j >= 3:
                        pe.wait_ge(a_trc, first_item[i] + j - 2)
                    for k in range(keys(q) // P):
                        m = pe.transpose(ps[:, 4 + b, k * P:(k + 1) * P], A[:, b, k * P:(k + 1) * P], ident)
                    m.then_inc(a_tr, 1)
                if j >= 2:
                    h, q = its[j - 2]
                    pe.wait_ge(a_trc, first_item[i] + j - 1)
                    if j >= 4:
                        pe.wait_ge(a_oc, first_item[i] + j - 3)
                    nk = keys(q) // P
                    for k in range(nk):
                        m = pe.matmul(ps[:, 6 + j % 2, 0:P], AT[:, (j - 2) % 2, k * P:(k + 1) * P],
                                      V[:, k, h * P:(h + 1) * P], start=k == 0, stop=k == nk - 1, skip_group_check=True)
                    m.then_inc(a_pv, 1)
            pe.wait_ge(o_nrm[i], 1)
            for h in range(HEADS):
                take_tile(pe, (i, "OT", h))
                for q in tiles[i]:
                    m = pe.transpose(bank((i, "OT", h))[:, q * P:(q + 1) * P], O[:, q, h, :], ident)
                m.then_inc(tile_done, 1)

        pe.wait_ge(cond_ready, 1)
        pe.wait_ge(filled, 3)
        ada_open(slice(0, 64))
        for g in range(4):
            ada_step(4 * g, g, g == 3)

        for i in range(DEPTH):
            c0 = col0[i]
            norm_sum(f"n1_{i}", (i, "n1"), 0)
            pe.wait_ge(n_lo, KT * (i + 1))
            n = mix0[i]
            for s in steps_of(i):
                kind = s[0]
                if s == ("GF", 0):
                    dft_channels(i)
                if s == ("GF", 1):
                    dft_tokens(i)
                if kind == "ADA":
                    if s == ("ADA", 0, 4):
                        pe.wait_ge(mod_a, 1)
                        ada_open(slice(64, 192))
                    if s == ("ADA", 1, 0):
                        pe.wait_ge(mod_b, 1)
                        ada_open(slice(0, 192))
                    ada_step(n, s[2], s[2] == 11)
                elif kind == "WF":
                    wait_emptied(pe, (i, "Z") + dft[i][-1])
                    for nn in range(2):
                        by_weights(n + 2 * nn, [(i, "WF", 0, 4 * nn + t) for t in range(4)], c0, (Zhi, Zlo), 2)
                elif kind == "V":
                    by_tokens(n, [(i, "V", s[1], t) for t in range(4)])
                elif kind == "WA":
                    if s[1] == 0:
                        attention(i)
                        pe.wait_ge(ot_l[i], HEADS)
                    by_weights(n, [(i, "WA", s[1], t) for t in range(4)], c0, (OThi, OTlo), 4)
                elif kind == "WO":
                    pe.wait_ge(m_l[i], KT)
                    by_weights(n, [(i, "WO", s[1], t) for t in range(4)], c0, (Hhi, Hlo), 4)
                else:
                    by_weights(n, [(i, kind, s[1], t) for t in range(4)], 0 if kind == "QK" and s[1] >= 2 else c0,
                               (Hhi, Hlo), 4)
                n += 4

            norm_sum(f"n2_{i}", (i, "n2"), c0)
            pe.wait_ge(small_in, 32)
            key = (i, "log")
            take_tile(pe, key)
            pe.wait_ge(n_hf, KT * (2 * i + 2))
            for t in tiles[i]:
                for k in range(KT):
                    m = pe.matmul(bank(key)[:, NE * t:NE * t + NE], h2T[:, k, t * P:(t + 1) * P], wr[:, k, :],
                                  start=k == 0, stop=k == KT - 1, skip_group_check=True)
            m.then_inc(tile_done, 1)
            for t in tiles[i]:
                for half in range(2):
                    key = (i, "h2", t, half)
                    take_tile(pe, key)
                    for k in range(4):
                        m = pe.transpose(bank(key)[:, k * P:(k + 1) * P], h2T[:, 4 * half + k, t * P:(t + 1) * P], ident)
                    m.then_inc(tile_done, 1)
            pe.wait_ge(rt_asg[i], 1)
            key = (i, "rank")
            take_tile(pe, key)
            tl = tiles[i]
            for t in tl:
                for u in tl[:tl.index(t) + 1]:
                    pe.matmul(bank(key)[:, NE * t:NE * t + NE], tri if u == t else ones, asg[:, u, :], start=u == tl[0],
                              stop=u == t, skip_group_check=True)
            for u in tl:
                m = pe.matmul(bank(key)[:, 64:64 + NE], ones, asg[:, u, :], start=u == tl[0], stop=u == tl[-1],
                              skip_group_check=True)
            m.then_inc(tile_done, 1)
            wait_all_emptied(pe, key)

            nb = exp0[i]
            with pe.Fori(0, NE // 2) as it:

                def turn_tokens(j):
                    pe.wait_ge(e_in[j], it * 16 + (8 * NE * i + 16))
                    if j == 1:
                        pe.wait_ge(e_xl, NE * i + 2 * it + 1)
                    for k in range(KT):
                        m = pe.transpose(ps[:, 4 + k // 4, (k % 4) * P:(k % 4 + 1) * P], xg[:, j, k * P:(k + 1) * P], ident)
                    m.then_inc(e_xt, 1)

                def gate_up(j):
                    pe.wait_ge(e_xl, NE * i + 2 * it + j + 1)
                    for m_ in range(2):
                        for ch in range(4):
                            n = nb + 12 * j + 4 * m_ + ch
                            pe.wait_ge(lo_ready, it * 24 + (n + 1))
                            for k in range(CK):
                                kt = CK * ch + k
                                m = product(pe, ps[:, m_, :], xhi[:, kt, :], xlo[:, kt, :], whi[:, n % SPL, k, :],
                                            wlo[:, n % SPL, k, :], kt == 0, kt == KT - 1)
                            m.then_inc(w_used, 1)

                def turn_hidden(j):
                    pe.wait_ge(e_he, NE * i + 2 * it + j + 1)
                    for k in range(KE):
                        m = pe.transpose(ps[:, 6, k * P:(k + 1) * P], he[:, k * P:(k + 1) * P], ident)
                    m.then_inc(e_ht, 1)

                def down(j):
                    pe.wait_ge(e_hl, NE * i + 2 * it + j + 1)
                    if j == 1:
                        pe.wait_ge(e_ya, NE * i + 2 * it + 1)
                        pe.wait_ge(e_yd, NE * i + 2 * it + 1)
                    for ch in range(4):
                        n = nb + 12 * j + 8 + ch
                        pe.wait_ge(lo_ready, it * 24 + (n + 1))
                        for k in range(CK):
                            kt = CK * (ch % 2) + k
                            m = product(pe, ps[:, 2 + ch // 2, :], hehi[:, kt, :], helo[:, kt, :], whi[:, n % SPL, k, :],
                                        wlo[:, n % SPL, k, :], kt == 0, kt == KE - 1)
                        m.then_inc(w_used, 1)

                turn_tokens(0)
                gate_up(0)
                turn_tokens(1)
                turn_hidden(0)
                down(0)
                gate_up(1)
                turn_hidden(1)
                down(1)
                pe.wait_ge(e_ya, NE * i + 2 * it + 2)
                pe.wait_ge(e_yd, NE * i + 2 * it + 2)

            over = pe.value_load(most[0:1, 0:1], min_val=0, max_val=T)
            with pe.If(over > P):
                with pe.Fori(0, NE * len(tiles[i])) as r:
                    pe.wait_ge(f_in[i], r * 48 + 48)
                    for k in range(KT):
                        m = pe.transpose(ps[:, 4 + k // 4, (k % 4) * P:(k % 4 + 1) * P], xg[:, 0, k * P:(k + 1) * P], ident)
                    m.then_inc(f_pe[i], 1)
                    pe.wait_ge(f_dve[i], r * 5 + 1)
                    for m_ in range(2):
                        for k in range(KT):
                            m = pe.matmul(ps[:, m_, :], xT32[:, k, :], raw[:, 4 * m_ + k // 2, k % 2, :], start=k == 0,
                                          stop=k == KT - 1)
                    m.then_inc(f_pe[i], 1)
                    pe.wait_ge(f_dve[i], r * 5 + 3)
                    for k in range(KE):
                        m = pe.transpose(ps[:, 6, k * P:(k + 1) * P], he[:, k * P:(k + 1) * P], ident)
                    m.then_inc(f_pe[i], 1)
                    pe.wait_ge(f_dve[i], r * 5 + 4)
                    pe.wait_ge(f_dn[i], r * 16 + 16)
                    for half in range(2):
                        for k in range(KE):
                            m = pe.matmul(ps[:, 2 + half, :], hT32[:, k, :], raw[:, k, half, :], start=k == 0, stop=k == KE - 1)
                    m.then_inc(f_pe[i], 1)
                    pe.wait_ge(f_dve[i], r * 5 + 5)

            pe.wait_ge(y_sum[i], len(tiles[i]))
            for k in range(KT):
                key = (i, "yT", k)
                take_tile(pe, key)
                for t in tiles[i]:
                    m = pe.transpose(bank(key)[:, t * P:(t + 1) * P], y2[:, t, k * P:(k + 1) * P], ident)
                m.then_inc(tile_done, 1)

        norm_sum("nf", ("nf",), SEQ)
        pe.wait_ge(n_hf, KT * 5)
        for t in range(2):
            for half in range(2):
                key = ("out", t, half)
                take_tile(pe, key)
                for k in range(4):
                    cc = SEQ + t * P
                    m = pe.transpose(bank(key)[:, k * P:(k + 1) * P], h2T[:, 4 * half + k, cc:cc + P], ident)
                m.then_inc(tile_done, 1)

    lam_init = [0.8 - 0.6 * math.exp(-0.3 * i) for i in range(DEPTH)]
    streams = [(0, SEQ, 1), (SEQ, T, 0)]

    @block.scalar
    def _(act):
        act.wait_ge(filled, 3)

        def norm(name, c0, scale, bias, split):
            o, os = KT * norms[name], KT * (norms[name] // 2)
            for k in range(KT):
                if k >= 2:
                    act.wait_ge(n_squ, o - norms[name] + k - 1)
                act.activation(sq[:, k % 2, c0:T], X[:, k, c0:T], ACT.Square).then_inc(n_sq, 1)
            key = {"n1_0": (0, "n1"), "n2_0": (0, "n2"), "n1_1": (1, "n1"), "n2_1": (1, "n2"), "nf": ("nf",)}[name]
            wait_tile(act, key)
            act.activation(std[:, c0:T], bank(key)[:, c0:T], ACT.Sqrt, bias=epst[:, 0:1], scale=1.0 / D).then_inc(free_act, 1)
            for k in range(KT):
                act.wait_ge(n_xn, o + k + 1)
                if split and k >= 2:
                    act.wait_ge(n_lo, os + k - 1)
                dst = hf[:, k % 2] if split else h2T[:, k]
                parts = [p for p in streams if p[0] >= c0]
                for a_, b_, s in parts:
                    kw = {"bias": bias(k, s)} if bias else {}
                    m = act.activation(dst[:, a_:b_], xn[:, k % 2, a_:b_], ACT.Identity, scale=scale(k, s), **kw)
                m.then_inc(n_hf, 1)
                if split:
                    act.wait_ge(n_hf, o + k + 1)
                    act.activation(Hhi[:, k, :], hf[:, k % 2, :], ACT.Copy).then_inc(n_hi, 1)

        def empty_step(i, s):
            c0, kind = col0[i], s[0]
            if kind in ("ADA", "WF", "WO"):
                return
            for t in range(4):
                key = (i, kind, s[1], t)
                b = 4 * s[1] + t
                if kind == "WA":
                    act.wait_ge(m_f[i], b + 1)
                    act.activation(Hhi[:, b, c0:T], G[:, b, c0:T], ACT.Copy).then_inc(m_h[i], 1)
                    continue
                wait_tile(act, key)
                if kind == "F":
                    m = act.activation(FT[:, t, c0:T], bank(key)[:, c0:T], ACT.Copy)
                elif kind == "QK":
                    cc = 0 if s[1] >= 2 else c0
                    if i == 0 and b == 0:
                        act.wait_ge(pad_out, 16 * (ROWS // P - 2 * T // P))
                    m = act.activation(QK[:, b, cc:T], bank(key)[:, cc:T], ACT.Copy)
                elif kind == "V":
                    m = act.activation(V[:, t, s[1] * CW:(s[1] + 1) * CW], bank(key)[:, :], ACT.Copy)
                else:
                    off = V_BG + (0 if kind == "GA" else 8) + b
                    if kind == "GA" and b == 0:
                        act.wait_ge(roped[i], 2 * HEADS)
                    m = act.activation((GA if kind == "GA" else G)[:, b, c0:T], bank(key)[:, c0:T], ACT.Sigmoid,
                                       bias=vec[i][:, off:off + 1])
                m.then_inc(free_act, 1)

        def attention(i):
            act.wait_ge(lam_s[i], 1)
            act.activation(lexp[:, :], lsum[:, :], ACT.Exp).then_inc(lam_e[i], 1)
            act.wait_ge(x_kept[i], 16)
            its = items[i]
            for j in range(len(its) + 1):
                if j < len(its):
                    q, b = its[j][1], j % 2
                    act.wait_ge(a_neg, first_item[i] + j + 1)
                    if j >= 2:
                        act.wait_ge(a_comb, first_item[i] + j - 1)
                    for m_ in range(2):
                        act.activation(E[:, b, m_, 0:keys(q)], ps[:, 2 * b + m_, 0:keys(q)], ACT.Exp,
                                       bias=aneg[:, b, m_:m_ + 1], scale=ATT_SCALE,
                                       accum_out=asum[:, b, m_:m_ + 1]).then_inc(a_exp, 1)
                if j >= 1:
                    q, b = its[j - 1][1], (j - 1) % 2
                    act.wait_ge(a_tr, first_item[i] + j)
                    if j >= 3:
                        act.wait_ge(a_pv, first_item[i] + j - 2)
                    act.activation(AT[:, b, 0:keys(q)], ps[:, 4 + b, 0:keys(q)], ACT.Copy).then_inc(a_trc, 1)
            tl = tiles[i]
            act.wait_ge(a_oc, first_item[i] + len(its))
            act.activation(osq[:, tl[0]:, :, :].rearrange("p q h e -> p (q h e)"),
                           O[:, tl[0]:, :, :].rearrange("p q h e -> p (q h e)"), ACT.Square).then_inc(o_sq[i], 1)
            act.wait_ge(o_ss[i], 1)
            no = len(tl) * HEADS
            act.activation(ostd[:, 0:no], oss[:, 0:no], ACT.Sqrt, bias=epst[:, 0:1], scale=1.0 / P).then_inc(o_std[i], 1)
            for h in range(HEADS):
                wait_emptied(act, (i, "OT", h))
                act.activation(OThi[:, h, col0[i]:T], ot32[:, h % 2, col0[i]:T], ACT.Copy).then_inc(ot_h[i], 1)

        def dft_channels(i):
            for s, g in dft[i]:
                key = (i, "Y", s, g)
                wait_tile(act, key)
                act.activation(Y[:, s, g, :, :].rearrange("p t n -> p (t n)"), bank(key), ACT.Copy).then_inc(free_act, 1)

        def dft_tokens(i):
            for s, g in dft[i]:
                key = (i, "Z", s, g)
                wait_tile(act, key)
                act.activation(Zhi[:, g, s * SEQ:(s + 1) * SEQ], bank(key)[:, 0:SEQ], ACT.Copy).then_inc(z_hi[i], 1)

        wait_emptied(act, ("vec", 0))
        act.activation(csig[:, :], vec[0][:, V_C:V_C + 16], ACT.Sigmoid).then_inc(cond_sig, 1)
        act.wait_ge(cond_sil, 1)
        act.activation(cond[:, :, :].rearrange("p k (s u) -> p s k u", u=2)[:, :, :, 0],
                       csil[:, :].rearrange("p (s k) -> p s k", s=2), ACT.Copy).then_inc(cond_hi, 1)
        for k in range(1, KT, 2):
            wait_tile(act, ("x0", k))
            act.activation(X[:, k, :], bank(("x0", k)), ACT.Copy).then_inc(free_act, 1)
        for n in range(ADA_A):
            split_hi(act, n)
        for i in range(DEPTH):
            n = mix0[i]
            for ch in range(3):
                split_hi(act, n + ch)
            wait_all_emptied(act, ("x0", KT - 1) if i == 0 else (0, "yT", KT - 1))
            if i == 0:
                act.wait_ge(mod_a, 1)
            norm(f"n1_{i}", 0, lambda k, s: sc1[i][:, k, s:s + 1], lambda k, s: mod[i][:, k, s:s + 1], True)
            before = None
            for s in steps_of(i):
                for ch in range(4):
                    if ch < 3 and before is not None:
                        split_hi(act, n + ch)
                    if ch == 3:
                        if before is not None:
                            empty_step(i, before)
                        if s == ("GF", 0):
                            dft_channels(i)
                        if s == ("GF", 1):
                            dft_tokens(i)
                        split_hi(act, n + ch)
                if s == ("WA", 0):
                    attention(i)
                before = s
                n += 4
            wait_emptied(act, (i, "WO", 1, 3))
            act.wait_ge(mod_b, 1)
            norm(f"n2_{i}", col0[i], lambda k, s: sc2[i][:, k, s:s + 1], lambda k, s: mod[i][:, 24 + k, s:s + 1], False)
            key = (i, "log")
            t0 = tiles[i][0]
            wait_tile(act, key)
            act.activation(aff[:, t0:, :].rearrange("p t e -> p (t e)"), bank(key)[:, NE * t0:4 * NE],
                           ACT.Sigmoid).then_inc(free_act, 1)
            for t in tiles[i]:
                key = (i, "h2", t, 1)
                wait_tile(act, key)
                act.activation(h2tok[:, t, CW:D], bank(key), ACT.Copy).then_inc(free_act, 1)

            nb = exp0[i]
            with act.Fori(0, NE // 2) as it:
                def tokens(j):
                    act.wait_ge(e_xt, NE * i + 2 * it + j + 1)
                    act.activation(xhi[:, :, :].rearrange("p k t -> p (k t)"),
                                   ps[:, 4:6, :].rearrange("p b n -> p (b n)"), ACT.Copy).then_inc(e_xh, 1)

                def splits(lo_, hi_):
                    for ch in range(lo_, hi_):
                        split_hi(act, nb + ch, it, 24)

                for j in range(2):
                    o = 12 * j
                    if j == 0:
                        splits(0, 3)
                        tokens(0)
                        splits(3, 8)
                    else:
                        splits(o + 3, o + 8)
                    act.wait_ge(w_used, it * 24 + (nb + o + 4))
                    act.activation(sg[:, :], ps[:, 0, :], ACT.Sigmoid).then_inc(e_sig, 1)
                    if j == 0:
                        tokens(1)
                    splits(o + 8, o + 11)
                    act.wait_ge(e_ht, NE * i + 2 * it + j + 1)
                    act.activation(hehi[:, :, :].rearrange("p k t -> p (k t)"), ps[:, 6, :], ACT.Copy).then_inc(e_hh, 1)
                    splits(o + 11, o + 12)
                    if j == 0:
                        splits(12, 15)
                    act.wait_ge(w_used, it * 24 + (nb + o + 12))
                    act.wait_ge(y_free[i], 2 * it + j + 1)
                    act.activation(ytile[:, j, 0:CW], ps[:, 2, :], ACT.Copy).then_inc(e_ya, 1)

            over = act.value_load(most[0:1, 0:1], min_val=0, max_val=T)
            with act.If(over > P):
                with act.Fori(0, NE * len(tiles[i])) as r:
                    act.wait_ge(f_pe[i], r * 4 + 2)
                    act.activation(sg[:, :], ps[:, 0, :], ACT.Sigmoid).then_inc(f_act[i], 1)
                    act.wait_ge(f_dve[i], r * 5 + 5)
        wait_all_emptied(act, (1, "yT", KT - 1))
        norm("nf", SEQ, lambda k, s: vec[0][:, V_GF + k:V_GF + k + 1], None, False)
        for t in range(2):
            wait_tile(act, ("out", t, 1))
            act.activation(outt[:, t, CW:D], bank(("out", t, 1)), ACT.Copy).then_inc(out_ready, 1)

    @block.vector
    def _(dve):
        chain = [0]

        def link(ins):
            chain[0] += 1
            ins.then_inc(dve_chain, 1)
            dve.wait_ge(dve_chain, chain[0])

        def stt(o, a, s, b, op0, op1):
            return dve.scalar_tensor_tensor(out=o, in0=a, scalar=s, in1=b, op0=op0, op1=op1)

        def spread(ap, shape):
            return ap.to_broadcast(shape)

        def norm(name, c0, split):
            o, os = KT * norms[name], KT * (norms[name] // 2)
            key = {"n1_0": (0, "n1"), "n2_0": (0, "n2"), "n1_1": (1, "n1"), "n2_1": (1, "n2"), "nf": ("nf",)}[name]
            wait_emptied(dve, key)
            link(dve.reciprocal(rinv[:, c0:T], std[:, c0:T]))
            for k in range(KT + 1):
                if k < KT:
                    if k >= 2:
                        dve.wait_ge(n_hf, o + k - 1)
                    dve.tensor_tensor(xn[:, k % 2, c0:T], X[:, k, c0:T], rinv[:, c0:T], ALU.mult).then_inc(n_xn, 1)
                if split and k >= 1:
                    dve.wait_ge(n_hi, os + k)
                    dve.tensor_tensor(Hlo[:, k - 1, :], hf[:, (k - 1) % 2, :], Hhi[:, k - 1, :].bitcast(F32),
                                      ALU.subtract).then_inc(n_lo, 1)

        def adaln(i, b0, b1, done):
            m = mod[i][:, b0:b1, :]
            link(dve.tensor_reduce(m, ps[:, 7, 4 * b0:4 * b1].rearrange("p (b s u) -> p b s u", s=2, u=2), AX.X, ALU.add))
            bias = vec[i][:, V_BADA + b0:V_BADA + b1].unsqueeze(2)
            ins = dve.tensor_tensor(m, m, spread(bias, [P, b1 - b0, 2]), ALU.add)
            for sc, blk, g in ((sc1[i], 8, V_G1), (sc2[i], 32, V_G2)):
                if b0 <= blk < b1:
                    link(ins)
                    ins = stt(sc[:, :, :], mod[i][:, blk:blk + 8, :], 1.0,
                              spread(vec[i][:, g:g + 8].unsqueeze(2), [P, KT, 2]), ALU.add, ALU.mult)
            ins.then_inc(done, 1)

        def empty_step(i, s, half=1):
            c0, kind = col0[i], s[0]
            parts = [p for p in streams if p[0] >= c0]
            if kind == "ADA" and s[2] == 11:
                n_end = mix0[0] + 4 * steps_of(0).index(s) + 4
                dve.wait_ge(w_used, n_end)
                adaln(s[1], 16 if s[1] == 0 else 0, 48, mod_b)
            elif kind == "QK":
                for t in range(4):
                    b = 4 * s[1] + t
                    wait_emptied(dve, (i, "QK", s[1], t))
                    lat = QK[:, b, SEQ:T]
                    link(dve.stream_shuffle(rt[:, t % 2, :], lat, [(r + 16) % 32 for r in range(32)]))
                    link(dve.tensor_tensor(rt[:, t % 2, :], rt[:, t % 2, :], cs(C_RS, SEQ), ALU.mult))
                    link(dve.tensor_tensor(lat, lat, cs(C_RC, SEQ), ALU.mult))
                    dve.tensor_tensor(lat, lat, rt[:, t % 2, :], ALU.add).then_inc(roped[i], 1)
            elif kind == "WF":
                for t in range(4 * half, 4 * half + 4):
                    key = (i, "WF", 0, t)
                    wait_emptied(dve, (i, "GF", t // 4, t % 4))
                    wait_tile(dve, key)
                    dve.tensor_tensor(G[:, t, c0:T], bank(key)[:, c0:T], G[:, t, c0:T], ALU.mult).then_inc(free_dve, 1)
            elif kind == "WA":
                for t in range(4):
                    b, key = 4 * s[1] + t, (i, "WA", s[1], t)
                    wait_tile(dve, key)
                    ga = GA[:, b, c0:T]
                    dve.tensor_tensor(ga, bank(key)[:, c0:T], ga, ALU.mult).then_inc(free_dve, 1)
                    wait_emptied(dve, key)
                    dve.tensor_tensor(G[:, b, c0:T], G[:, b, c0:T], ga, ALU.add).then_inc(m_f[i], 1)
                for t in range(4):
                    b = 4 * s[1] + t
                    dve.wait_ge(m_h[i], b + 1)
                    dve.tensor_tensor(Hlo[:, b, c0:T], G[:, b, c0:T], Hhi[:, b, c0:T].bitcast(F32),
                                      ALU.subtract).then_inc(m_l[i], 1)
            elif kind == "WO":
                if s[1] == 0:
                    dve.wait_ge(x_back[i], 16)
                for t in range(4):
                    b, key = 4 * s[1] + t, (i, "WO", s[1], t)
                    wait_tile(dve, key)
                    for a_, b_, cd in parts:
                        m = stt(X[:, b, a_:b_], bank(key)[:, a_:b_], mod[i][:, 16 + b, cd:cd + 1], X[:, b, a_:b_],
                                ALU.mult, ALU.add)
                    m.then_inc(free_dve, 1)

        def attention(i):
            dve.wait_ge(lam_in[i], 16)
            pairs = lamv[:, :, :].rearrange("p (a b) d -> p a b d", b=2)
            link(dve.tensor_tensor(lprod[:, :, :], pairs[:, :, 0, :], pairs[:, :, 1, :], ALU.mult))
            dve.tensor_reduce(lsum[:, :], lprod[:, :, :], AX.X, ALU.add).then_inc(lam_s[i], 1)
            dve.wait_ge(lam_e[i], 1)
            link(dve.tensor_tensor(nlam[:, :], lexp[:, 1:2], lexp[:, 0:1], ALU.subtract))
            link(dve.tensor_scalar(nlam[:, :], nlam[:, :], -lam_init[i], None, ALU.add))
            link(dve.tensor_scalar(gsub[:, :], vec[i][:, V_SUB:V_SUB + 1], 1.0 - lam_init[i], None, ALU.mult))
            its = items[i]
            for j in range(len(its) + 2):
                if j < len(its):
                    q, b = its[j][1], j % 2
                    dve.wait_ge(a_s, first_item[i] + j + 1)
                    link(dve.tensor_reduce(amax[:, b, :], ps[:, 2 * b:2 * b + 2, 0:keys(q)], AX.X, ALU.max))
                    dve.tensor_scalar(aneg[:, b, :], amax[:, b, :], -ATT_SCALE, None, ALU.mult).then_inc(a_neg, 1)
                if 1 <= j <= len(its):
                    q, b = its[j - 1][1], (j - 1) % 2
                    dve.wait_ge(a_exp, 2 * first_item[i] + 2 * j)
                    link(dve.reciprocal(arec[:, b, :], asum[:, b, :]))
                    link(dve.tensor_tensor(arec1[:, b:b + 1], arec[:, b, 1:2], nlam[:, :], ALU.mult))
                    e0, e1 = E[:, b, 0, 0:keys(q)], E[:, b, 1, 0:keys(q)]
                    link(dve.tensor_scalar(e1, e1, arec1[:, b:b + 1], None, ALU.mult))
                    if j >= 3:
                        dve.wait_ge(a_tr, first_item[i] + j - 2)
                    stt(A[:, b, 0:keys(q)], e0, arec[:, b, 0:1], e1, ALU.mult, ALU.add).then_inc(a_comb, 1)
                if j >= 2:
                    h, q = its[j - 2]
                    dve.wait_ge(a_pv, first_item[i] + j - 1)
                    dve.tensor_copy(O[:, q, h, :], ps[:, 6 + j % 2, 0:P]).then_inc(a_oc, 1)
            tl = tiles[i]
            no = len(tl) * HEADS
            dve.wait_ge(o_sq[i], 1)
            heads = lambda t_: t_[:, tl[0]:, :, :].rearrange("p q h e -> p (q h) e")
            dve.tensor_reduce(oss[:, 0:no], heads(osq), AX.X, ALU.add).then_inc(o_ss[i], 1)
            dve.wait_ge(o_std[i], 1)
            link(dve.reciprocal(orin[:, 0:no], ostd[:, 0:no]))
            dve.tensor_tensor(heads(O), heads(O), spread(orin[:, 0:no].unsqueeze(2), [P, no, P]), ALU.mult).then_inc(o_nrm[i], 1)
            c0 = col0[i]
            for h in range(HEADS + 1):
                if h < HEADS:
                    key = (i, "OT", h)
                    wait_tile(dve, key)
                    if h >= 2:
                        dve.wait_ge(ot_l[i], h - 1)
                    dve.tensor_scalar(ot32[:, h % 2, c0:T], bank(key)[:, c0:T], gsub[:, 0:1], None, ALU.mult).then_inc(free_dve, 1)
                if h >= 1:
                    dve.wait_ge(ot_h[i], h)
                    dve.tensor_tensor(OTlo[:, h - 1, c0:T], ot32[:, (h - 1) % 2, c0:T], OThi[:, h - 1, c0:T].bitcast(F32),
                                      ALU.subtract).then_inc(ot_l[i], 1)

        def dft_tokens(i):
            for m_, (s, g) in enumerate(dft[i]):
                key = (i, "Z", s, g)
                cols = slice(s * SEQ, (s + 1) * SEQ)
                dve.wait_ge(z_hi[i], m_ + 1)
                dve.tensor_tensor(Zlo[:, g, cols], bank(key)[:, 0:SEQ], Zhi[:, g, cols].bitcast(F32),
                                  ALU.subtract).then_inc(free_dve, 1)

        def route(i):
            t0, nt = tiles[i][0], len(tiles[i])
            v = lambda t_: t_[:, t0:]
            g4 = lambda t_: v(t_).rearrange("p t (g e) -> p t g e", g=4)
            key_e = cs(C_KE, NE).unsqueeze(1)
            key_g = cs(C_KG, 4).unsqueeze(1)
            row = lambda t_, n_: spread(v(t_).unsqueeze(2), [P, nt, n_])

            def first_max(src, n_, keys_, work, onehot):
                link(dve.tensor_reduce(v(tm), v(src), AX.X, ALU.max))
                link(dve.tensor_tensor(v(work), v(src), row(tm, n_), ALU.is_equal))
                link(dve.tensor_tensor(v(work), v(work), spread(keys_, [P, nt, n_]), ALU.mult))
                link(dve.tensor_reduce(v(tm), v(work), AX.X, ALU.max))
                link(dve.tensor_tensor(v(onehot), v(work), row(tm, n_), ALU.is_equal))

            wait_emptied(dve, (i, "log"))
            link(dve.tensor_tensor(v(sel), v(aff), spread(brb[:, :].unsqueeze(1), [P, nt, NE]), ALU.add))
            s4 = g4(sel)
            for m_, (a_, b_) in enumerate([(0, 1), (0, 2), (0, 3), (1, 2), (1, 3), (2, 3)]):
                ins = dve.tensor_tensor(v(pr)[:, :, :, m_], s4[:, :, :, a_], s4[:, :, :, b_], ALU.add)
            link(ins)
            link(dve.tensor_reduce(v(gsc), v(pr), AX.X, ALU.max))
            first_max(gsc, 4, key_g, geq, ing)
            inb = spread(v(ing).unsqueeze(3), [P, nt, 4, 4])
            link(dve.tensor_scalar(v(geq), v(ing), BIG, -BIG, ALU.mult, ALU.add))
            link(dve.tensor_tensor(g4(msk), s4, inb, ALU.mult))
            link(dve.tensor_tensor(g4(msk), g4(msk), spread(v(geq).unsqueeze(3), [P, nt, 4, 4]), ALU.add))
            first_max(msk, NE, key_e, ta, oh1)
            link(dve.tensor_scalar(v(tb), v(oh1), -BIG, None, ALU.mult))
            link(dve.tensor_tensor(v(msk), v(msk), v(tb), ALU.add))
            first_max(msk, NE, key_e, ta, oh2)
            dve.tensor_tensor(v(asg), v(oh1), v(oh2), ALU.add).then_inc(rt_asg[i], 1)
            for s, oh in enumerate((oh1, oh2)):
                link(dve.tensor_tensor(v(ta), v(oh), v(aff), ALU.mult))
                link(dve.tensor_reduce(w12[:, s, t0:], v(ta), AX.X, ALU.add))
            link(dve.tensor_tensor(v(wsum), w12[:, 0, t0:], w12[:, 1, t0:], ALU.add))
            link(dve.reciprocal(v(wsum), v(wsum)))
            for s in range(2):
                link(dve.tensor_tensor(gates[:, s, t0:], w12[:, s, t0:], v(wsum), ALU.mult))

        def places(i):
            t0, nt = tiles[i][0], len(tiles[i])
            v = lambda t_: t_[:, t0:]
            key = (i, "rank")
            wait_tile(dve, key)
            dve.tensor_copy(rank[:, t0:5, :].rearrange("p t e -> p (t e)"), bank(key)[:, NE * t0:5 * NE]).then_inc(free_dve, 1)
            wait_emptied(dve, key)
            count = rank[:, 4, :]
            link(dve.tensor_reduce(most_f[:, :], count, AX.X, ALU.max))
            link(dve.tensor_copy(cum[:, 0, :], count))
            for m_, sh in enumerate((1, 2, 4, 8)):
                a_, b_ = cum[:, m_ % 2, :], cum[:, (m_ + 1) % 2, :]
                link(dve.tensor_copy(b_[:, 0:sh], a_[:, 0:sh]))
                link(dve.tensor_tensor(b_[:, sh:NE], a_[:, sh:NE], a_[:, 0:NE - sh], ALU.add))
            link(dve.tensor_tensor(start_f[:, :], cum[:, 0, :], count, ALU.subtract))
            link(dve.tensor_tensor(v(pos), rank[:, t0:4, :], spread(start_f[:, :].unsqueeze(1), [P, nt, NE]), ALU.add))
            for s, oh in enumerate((oh1, oh2)):
                link(dve.tensor_tensor(v(ta), v(oh), v(pos), ALU.mult))
                link(dve.tensor_reduce(loc_f[:, s, t0:], v(ta), AX.X, ALU.add))
            dve.tensor_copy(loc[:, :, t0:], loc_f[:, :, t0:])
            dve.tensor_copy(starts[:, :], start_f[:, :])
            dve.tensor_copy(most[:, :], most_f[:, :]).then_inc(rt_loc[i], 1)

        for i in range(DEPTH):
            wait_tile(dve, ("vec", i))
            dve.tensor_copy(vec[i][:, :], bank(("vec", i))[:, 0:V_ROWS]).then_inc(free_dve, 1)
        wait_emptied(dve, ("vec", 1))
        dve.wait_ge(cond_sig, 1)
        dve.tensor_tensor(csil[:, :], csig[:, :], vec[0][:, V_C:V_C + 16], ALU.mult).then_inc(cond_sil, 1)
        dve.wait_ge(cond_hi, 1)
        cond4 = cond[:, :, :].rearrange("p k (s u) -> p s k u", u=2)
        dve.tensor_tensor(cond4[:, :, :, 1], csil[:, :].rearrange("p (s k) -> p s k", s=2),
                          cond4[:, :, :, 0].bitcast(F32), ALU.subtract).then_inc(cond_ready, 1)
        for k in range(0, KT, 2):
            wait_tile(dve, ("x0", k))
            dve.tensor_copy(X[:, k, :], bank(("x0", k))).then_inc(free_dve, 1)
        for n in range(ADA_A):
            split_lo(dve, n)
        dve.wait_ge(w_used, ADA_A)
        adaln(0, 0, 16, mod_a)

        for i in range(DEPTH):
            n = mix0[i]
            for ch in range(3):
                split_lo(dve, n + ch)
            norm(f"n1_{i}", 0, True)
            before = None
            for s in steps_of(i):
                for ch in range(4):
                    if ch < 3 and before is not None:
                        split_lo(dve, n + ch)
                    if ch == 3:
                        if before is not None:
                            empty_step(i, before)
                        if s == ("GF", 1):
                            dft_tokens(i)
                        split_lo(dve, n + ch)
                        if s == ("WF", 0):
                            empty_step(i, s, 0)
                if s == ("WA", 0):
                    attention(i)
                before = s
                n += 4
            empty_step(i, before)
            norm(f"n2_{i}", col0[i], False)
            for t in tiles[i]:
                key = (i, "h2", t, 0)
                if t == tiles[i][0]:
                    route(i)
                wait_tile(dve, key)
                dve.tensor_copy(h2tok[:, t, 0:CW], bank(key)).then_inc(free_dve, 1)
            places(i)

            nb = exp0[i]
            with dve.Fori(0, NE // 2) as it:
                def tokens(j):
                    dve.wait_ge(e_xh, NE * i + 2 * it + j + 1)
                    dve.tensor_tensor(xlo[:, :, :].rearrange("p k t -> p (k t)"), ps[:, 4:6, :].rearrange("p b n -> p (b n)"),
                                      xhi[:, :, :].rearrange("p k t -> p (k t)").bitcast(F32), ALU.subtract).then_inc(e_xl, 1)

                def splits(lo_, hi_):
                    for ch in range(lo_, hi_):
                        split_lo(dve, nb + ch, it, 24)

                for j in range(2):
                    o = 12 * j
                    if j == 0:
                        splits(0, 3)
                        tokens(0)
                    splits(o + 3, o + 8)
                    dve.wait_ge(e_sig, NE * i + 2 * it + j + 1)
                    dve.tensor_tensor(gu[:, :], ps[:, 0, :], sg[:, :], ALU.mult).then_inc(e_gu, 1)
                    if j == 0:
                        tokens(1)
                    splits(o + 8, o + 9)
                    dve.wait_ge(w_used, it * 24 + (nb + o + 8))
                    dve.wait_ge(e_gu, NE * i + 2 * it + j + 1)
                    dve.tensor_tensor(he[:, :], ps[:, 1, :], gu[:, :], ALU.mult).then_inc(e_he, 1)
                    splits(o + 9, o + 11)
                    dve.wait_ge(e_hh, NE * i + 2 * it + j + 1)
                    dve.tensor_tensor(helo[:, :, :].rearrange("p k t -> p (k t)"), ps[:, 6, :],
                                      hehi[:, :, :].rearrange("p k t -> p (k t)").bitcast(F32), ALU.subtract).then_inc(e_hl, 1)
                    splits(o + 11, o + 12)
                    if j == 0:
                        splits(12, 15)
                    dve.wait_ge(w_used, it * 24 + (nb + o + 12))
                    dve.wait_ge(y_free[i], 2 * it + j + 1)
                    dve.tensor_copy(ytile[:, j, CW:D], ps[:, 3, :]).then_inc(e_yd, 1)

            over = dve.value_load(most[0:1, 0:1], min_val=0, max_val=T)
            with dve.If(over > P):
                with dve.Fori(0, NE * len(tiles[i])) as r:
                    dve.wait_ge(f_pe[i], r * 4 + 1)
                    dve.tensor_copy(xT32[:, :, :].rearrange("p k t -> p (k t)"),
                                    ps[:, 4:6, :].rearrange("p b n -> p (b n)")).then_inc(f_dve[i], 1)
                    dve.wait_ge(f_act[i], r + 1)
                    dve.tensor_tensor(gu[:, :], ps[:, 0, :], sg[:, :], ALU.mult).then_inc(f_dve[i], 1)
                    dve.wait_ge(f_dve[i], r * 5 + 2)
                    dve.tensor_tensor(he[:, :], ps[:, 1, :], gu[:, :], ALU.mult).then_inc(f_dve[i], 1)
                    dve.wait_ge(f_pe[i], r * 4 + 3)
                    dve.tensor_copy(hT32[:, :, :].rearrange("p k t -> p (k t)"), ps[:, 6, :]).then_inc(f_dve[i], 1)
                    dve.wait_ge(f_pe[i], r * 4 + 4)
                    dve.tensor_copy(ytile[:, 0, :], ps[:, 2:4, :].rearrange("p b n -> p (b n)")).then_inc(f_dve[i], 1)

            dve.wait_ge(y_in[i], 32 * len(tiles[i]))
            for t in tiles[i]:
                link(dve.tensor_scalar(y1[:, t, :], y1[:, t, :], gates[:, 0, t:t + 1], None, ALU.mult))
                stt(y2[:, t, :], y2[:, t, :], gates[:, 1, t:t + 1], y1[:, t, :], ALU.mult, ALU.add).then_inc(y_sum[i], 1)
            parts = [p for p in streams if p[0] >= col0[i]]
            for k in range(KT):
                key = (i, "yT", k)
                wait_tile(dve, key)
                for a_, b_, cd in parts:
                    m = stt(X[:, k, a_:b_], bank(key)[:, a_:b_], mod[i][:, 40 + k, cd:cd + 1], X[:, k, a_:b_],
                            ALU.mult, ALU.add)
                m.then_inc(free_dve, 1)
        norm("nf", SEQ, False)
        for t in range(2):
            wait_tile(dve, ("out", t, 0))
            dve.tensor_copy(outt[:, t, 0:CW], bank(("out", t, 0))).then_inc(out_ready, 1)

    es.close()


_INS = ["x", "c", "ctx", "c_ctx", "w_ada", "b_ada", "g_norm1", "w_in", "lam_qk", "g_subln", "w_attn_out",
        "w_four_out", "w_gate", "b_gate", "w_out", "g_norm2", "w_router", "b_router", "w_e_gate", "w_e_up",
        "w_e_down", "g_final"]


def kernel(**inputs):
    import concourse.bacc as bacc
    from concourse.bass_utils import run_bass_kernel_spmd

    nc = bacc.Bacc("TRN2", target_bir_lowering=False, num_devices=1)
    arrays, args = {}, []
    for name in _INS:
        a = np.ascontiguousarray(inputs[name])
        arrays[f"in_{name}"] = a
        args.append(nc.dram_tensor(f"in_{name}", a.shape, mybir.dt.from_np(a.dtype), kind="ExternalInput").ap())
    arrays["in_consts"] = constants()
    args.append(nc.dram_tensor("in_consts", (P, C_COLS), F32, kind="ExternalInput").ap())
    o = nc.dram_tensor("out_x", (1, SEQ, D), F32, kind="ExternalOutput").ap()
    build(nc, *args, o)
    r = run_bass_kernel_spmd(nc, [arrays], core_ids=[0])
    return r.results[0]["out_x"]
```

```python
import math
from contextlib import ExitStack

import numpy as np
import concourse.bass as bass
from concourse import mybir

F32 = mybir.dt.float32
F32R = mybir.dt.float32r
I32 = mybir.dt.int32
U32 = mybir.dt.uint32
ACT = mybir.ActivationFunctionType
ALU = mybir.AluOpType
AX = mybir.AxisListType

P = 128
D = 1024
KT = D // P
T = 512
SEQ = 256
DEPTH = 2
HEADS = 8
HD = 64
FW = D // 2
FG = FW // P
NE = 16
DE = D // 2
KE = DE // P
EPS = 1e-6
ATT_SCALE = HD ** -0.5
BIG = 3.0e38

CK = 2
CW = 512
RAW = 8
SPL = 4
AG = 6 * D // CW
AR = 4 * AG
CPAD = 2 * AR - 4
BANKS = 7
EXP_CHUNKS = 12

V_BADA, V_G1, V_G2, V_BG, V_SUB, V_GF, V_C = 0, 48, 56, 64, 80, 81, 89
V_ROWS = 105

C_ID, C_ONE, C_TRI = 0, 128, 256
C_RC, C_RS = 384, 640
C_CD = 896
C_CL, C_SL = 1152, 1664
C_KG, C_KE = 2176, 2180
C_COLS = 2196


def constants():
    t = np.zeros((P, C_COLS), np.float64)
    p = np.arange(P)
    t[:, C_ID:C_ID + P] = np.eye(P)
    t[:, C_ONE:C_ONE + P] = 1.0
    t[:, C_TRI:C_TRI + P] = p[:, None] < p[None, :]
    tok = np.arange(SEQ)
    d = p % HD
    axis, half, j = d // 32, (d % 32) // 16, d % 16
    inv = 10000.0 ** (-j / 16.0)
    pos = np.where(axis[:, None] == 0, tok[None, :] // 64, tok[None, :] % 64)
    ang = pos * inv[:, None]
    t[:, C_RC:C_RC + SEQ] = np.cos(ang)
    t[:, C_RS:C_RS + SEQ] = np.sin(ang) * np.where(half == 0, -1.0, 1.0)[:, None]
    a = 2 * np.pi * np.outer(p, p) / P
    t[:, C_CD:C_CD + P] = np.cos(a) / np.sqrt(P)
    t[:, C_CD + P:C_CD + 2 * P] = np.sin(a) / np.sqrt(P)
    for k in range(2):
        b = 2 * np.pi * np.outer(k * P + p, tok) / SEQ
        t[:, C_CL + k * SEQ:C_CL + (k + 1) * SEQ] = np.cos(b) / np.sqrt(SEQ)
        t[:, C_SL + k * SEQ:C_SL + (k + 1) * SEQ] = -np.sin(b) / np.sqrt(SEQ)
    t[:, C_KG:C_KG + 4] = 4 - np.arange(4)
    t[:, C_KE:C_KE + NE] = NE - np.arange(NE)
    return t.astype(np.float32)


def steps_of(layer):
    return ([("F", 0), ("GF", 0), ("GF", 1), ("WF", 0)] + [("QK", g) for g in range(4)]
            + [("V", 0), ("V", 1), ("GA", 0), ("GA", 1), ("WA", 0), ("WA", 1), ("WO", 0), ("WO", 1)])


def stream_of(layer):
    ada = [(("ADA", 0, g), ch) for g in range(4, 12) for ch in range(4)]
    ada += [(("ADA", 1, g), ch) for g in range(12) for ch in range(4)]
    out = []
    for n, s in enumerate(steps_of(layer)):
        for ch in range(4):
            out.append((s, ch))
            if layer == 0:
                take = 1 if n % 3 == 0 else 2
                out += ada[:take]
                ada = ada[take:]
    assert layer or not ada
    return out


def build(nc, x, c, ctx_tok, c_ctx, w_ada, b_ada, g_norm1, w_in, lam_qk, g_subln, w_attn_out,
          w_four_out, w_gate, b_gate, w_out, g_norm2, w_router, b_router, w_e_gate, w_e_up,
          w_e_down, g_final, consts, out):
    es = ExitStack()

    base = -(-nc.sbuf_base // 64) * 64
    at = [base]

    def place(nbytes):
        o = at[0]
        at[0] += -(-nbytes // 32) * 32
        assert at[0] <= nc.sbuf_usable_end, (at[0], nc.sbuf_usable_end)
        return o

    def view(name, shape, dt, offset):
        return nc.alloc_sbuf_tensor_at(name, shape, dt, offset=offset)

    KB = 1024
    o_raw, o_hi, o_lo = place(RAW * 4 * KB), place(SPL * 4 * KB), place(SPL * 4 * KB)
    raw = view("w_raw", [P, RAW, CK, CW], F32, o_raw)
    whi4 = view("w_hi", [P, SPL, CK, CW], F32R, o_hi)
    wlo4 = view("w_lo", [P, SPL, CK, CW], F32R, o_lo)
    cst = view("cst", [P, C_COLS], F32, place(C_COLS * 4))
    rX, rH, rQ, rV, rG = place(16 * KB), place(32 * KB), place(32 * KB), place(16 * KB), place(32 * KB)
    X = view("x_feat", [P, KT, T], F32, rX)
    E = view("att_e", [P, 2, 2, T], F32, rX)
    A = view("att_a", [P, 2, T], F32, rX + 8 * KB)
    AT = view("att_at", [P, 2, T], F32, rX + 12 * KB)
    Hhi = view("h_hi", [P, KT, T], F32R, rH)
    Hlo = view("h_lo", [P, KT, T], F32R, rH + 16 * KB)
    O = view("o_tok", [P, 4, HEADS, P], F32, rH)
    whi8 = view("w_hi_more", [P, SPL, CK, CW], F32R, rH)
    wlo8 = view("w_lo_more", [P, SPL, CK, CW], F32R, rH + 16 * KB)
    h2T = view("h2_feat", [P, KT, T], F32, rH)
    h2tok = view("h2_tok", [P, 4, D], F32, rH + 16 * KB)
    QK = view("qk", [P, 2 * HEADS, T], F32, rQ)
    Zhi = view("z_hi", [P, FG, T], F32R, rQ)
    Zlo = view("z_lo", [P, FG, T], F32R, rQ + 8 * KB)
    OThi = view("ot_hi", [P, KT, T], F32R, rQ)
    OTlo = view("ot_lo", [P, KT, T], F32R, rQ + 16 * KB)
    sq = view("sq", [P, 2, T], F32, rQ)
    std = view("std", [P, T], F32, rQ + 4 * KB)
    rinv = view("rinv", [P, T], F32, rQ + 6 * KB)
    xn = view("xn", [P, 2, T], F32, rQ + 8 * KB)
    hf = view("hf", [P, 2, T], F32, rQ + 12 * KB)
    xg = view("xg", [P, 2, D], F32, rQ)
    xhi = view("xg_hi", [P, KT, P], F32R, rQ + 8 * KB)
    xlo = view("xg_lo", [P, KT, P], F32R, rQ + 12 * KB)
    ytile = view("ytile", [P, 2, D], F32, rQ + 16 * KB)
    zrow = view("zrow", [P, D], F32, rQ + 28 * KB)
    outt = view("outt", [P, 2, D], F32, rG)
    V = view("v_tok", [P, 4, D], F32, rV)
    FT = view("f_feat", [P, FG, T], F32, rV)
    osq = view("o_sq", [P, 4, HEADS, P], F32, rV)
    ot32 = view("ot32", [P, 2, T], F32, rV)
    sg = view("sg", [P, DE], F32, rV)
    gu = view("gu", [P, DE], F32, rV + 2 * KB)
    he = view("he", [P, DE], F32, rV + 4 * KB)
    hehi = view("he_hi", [P, KE, P], F32R, rV + 6 * KB)
    helo = view("he_lo", [P, KE, P], F32R, rV + 8 * KB)
    hT32 = view("he32", [P, KE, P], F32, rV + 10 * KB)
    G = view("g_four", [P, KT, T], F32, rG)
    GA = view("g_attn", [P, KT, T], F32, rG + 16 * KB)
    Y = view("dft_y", [P, 2, FG, 2, 2 * P], F32, rG + 16 * KB)
    rt = view("rope_t", [P, 2, SEQ], F32, rG + 16 * KB)
    tok0 = view("tok0", [P, 4, D], F32, rG)
    y1 = view("y1", [P, 4, D], F32, rG)
    y2 = view("y2", [P, 4, D], F32, rG + 16 * KB)
    ada_row = [view("ada_row_h", [P, CW], F32, rH + 30 * KB), view("ada_row_v", [P, CW], F32, rV + 8 * KB)]
    ada_row.append(ada_row[0])
    xT32 = view("xT32", [P, KT, P], F32, rG)

    def small(name, shape, dt=F32):
        return view(name, shape, dt, place(int(np.prod(shape[1:])) * 4))

    vrow = view("vrow", [P, P], F32, rV)
    vrow1 = view("vrow1", [P, P], F32, rV + KB)
    vec = [small(f"vec{i}", [P, V_ROWS]) for i in range(DEPTH)]
    mod = [small(f"mod{i}", [P, 48, 2]) for i in range(DEPTH)]
    sc1 = [small(f"sc1_{i}", [P, KT, 2]) for i in range(DEPTH)]
    sc2 = [small(f"sc2_{i}", [P, KT, 2]) for i in range(DEPTH)]
    csig = small("csig", [P, 16])
    csil = small("csil", [P, 16])
    cond = small("cond", [P, KT, CPAD], F32R)
    wr = small("wr", [P, KT, NE])
    brb = small("brb", [P, NE])
    epst = small("epst", [P, 1])
    lamv = view("lamv", [P, 4 * DEPTH, HD], F32, rV + 2 * KB)
    lprod = view("lprod", [P, 2 * DEPTH, HD], F32, rV + 4 * KB)
    lsum = small("lsum", [P, 2 * DEPTH])
    lexp = small("lexp", [P, 2 * DEPTH])
    nlam = small("nlam", [P, DEPTH])
    gsub = small("gsub", [P, 1])
    amax = small("amax", [P, 2, 2])
    aneg = small("aneg", [P, 2, 2])
    asum = small("asum", [P, 2, 2])
    arec = small("arec", [P, 2, 2])
    arec1 = small("arec1", [P, 2])
    oss = small("oss", [P, 4 * HEADS])
    ostd = small("ostd", [P, 4 * HEADS])
    orin = small("orin", [P, 4 * HEADS])
    r_at = [rV]

    def passing(name, shape, dt=F32):
        o = r_at[0]
        r_at[0] += -(-int(np.prod(shape[1:])) * 4 // 32) * 32
        return view(name, shape, dt, o)

    aff = passing("aff", [P, 4, NE])
    sel = passing("sel", [P, 4, NE])
    pr = passing("pr", [P, 4, 4, 6])
    gsc = passing("gsc", [P, 4, 4])
    gmx = passing("gmx", [P, 4])
    geq = passing("geq", [P, 4, 4])
    ing = passing("ing", [P, 4, 4])
    msk = passing("msk", [P, 4, NE])
    ta = passing("ta", [P, 4, NE])
    tb = passing("tb", [P, 4, NE])
    tm = passing("tm", [P, 4])
    oh1 = passing("oh1", [P, 4, NE])
    oh2 = passing("oh2", [P, 4, NE])
    asg = passing("asg", [P, 4, NE])
    w12 = passing("w12", [P, 2, 4])
    wsum = passing("wsum", [P, 4])
    gates = small("gates", [P, 2, 4])
    rank = passing("rank", [P, 5, NE])
    cum = passing("cum", [P, 2, NE])
    start_f = passing("start_f", [P, NE])
    pos = passing("pos", [P, 4, NE])
    loc_f = passing("loc_f", [P, 2, 4])
    loc = small("loc", [P, 2, 4], U32)
    starts = small("starts", [P, NE], I32)
    most_f = passing("most_f", [P, 1])
    most = small("most", [P, 1], I32)

    ps = es.enter_context(nc.psum_tensor("ps", [P, 8, 512], F32))

    ROWS = 2 * T + 4 * P
    xkeep = nc.dram_tensor("xkeep", (P, KT * T), F32).ap()
    hbuf = nc.dram_tensor("hbuf", (ROWS, D), F32).ap()
    ybuf = nc.dram_tensor("ybuf", (ROWS, D), F32).ap()

    def sem(name):
        return es.enter_context(nc.semaphore(name))

    def per_layer(*names):
        return [[sem(f"{name}_{i}") for i in range(DEPTH)] for name in names]

    raw_in = [sem(f"raw_in{i}") for i in range(RAW)]
    hi_ready, lo_ready, w_used = sem("hi_ready"), sem("lo_ready"), sem("w_used")
    cst_in, tok_in, small_in, vec_in = sem("cst_in"), sem("tok_in"), sem("small_in"), sem("vec_in")
    filled, pad_out = sem("filled"), sem("pad_out")
    tile_done = sem("tile_done")
    free_act, free_dve = sem("free_act"), sem("free_dve")
    dve_chain = sem("dve_chain")
    cond_sig, cond_sil, cond_hi, cond_ready = sem("cond_sig"), sem("cond_sil"), sem("cond_hi"), sem("cond_ready")
    ada_rows = sem("ada_rows")
    mod_a, mod_b = sem("mod_a"), sem("mod_b")
    n_sq, n_squ, n_xn, n_hf, n_hi, n_lo = (sem(f"n_{k}") for k in ("sq", "squ", "xn", "hf", "hi", "lo"))
    norms = {"n1_0": 0, "n2_0": 1, "n1_1": 2, "n2_1": 3, "nf": 4}
    x_kept, x_back, roped, z_hi = per_layer("x_kept", "x_back", "roped", "z_hi")
    lam_in, lam_s, lam_e = sem("lam_in"), sem("lam_s"), sem("lam_e")
    a_s, a_neg, a_exp, a_comb, a_tr, a_trc, a_pv, a_oc = (
        sem(f"a_{k}") for k in ("s", "neg", "exp", "comb", "tr", "trc", "pv", "oc"))
    o_sq, o_ss, o_std, o_nrm, ot_h, ot_l, m_f, m_h, m_l = per_layer(
        "o_sq", "o_ss", "o_std", "o_nrm", "ot_h", "ot_l", "m_f", "m_h", "m_l")
    rt_asg, rt_loc, sc_out, e_out, y_free = per_layer("rt_asg", "rt_loc", "sc_out", "e_out", "y_free")
    e_in = [sem("e_in_a"), sem("e_in_b")]
    e_xt, e_xh, e_xl, e_sig, e_gu, e_he, e_ht, e_hh, e_hl, e_ya, e_yd = (
        sem(f"e_{k}") for k in ("xt", "xh", "xl", "sig", "gu", "he", "ht", "hh", "hl", "ya", "yd"))
    f_go, f_in, f_dn, f_out, f_pe, f_act, f_dve = per_layer("f_go", "f_in", "f_dn", "f_out", "f_pe", "f_act", "f_dve")
    y_in, y_sum = per_layer("y_in", "y_sum")
    out_ready, out_done = sem("out_ready"), sem("out_done")

    cs = lambda a, n: cst[:, a:a + n]
    ident, ones, tri = cs(C_ID, P), cs(C_ONE, P), cs(C_TRI, P)

    col0 = [0, SEQ]
    tiles = [[0, 1, 2, 3], [2, 3]]
    items = [[(h, q) for h in range(HEADS) for q in tiles[i]] for i in range(DEPTH)]
    first_item = [0, len(items[0])]
    keys = lambda q: SEQ if q < 2 else T

    def w_chunk(w, k0, n0):
        return w[k0 * P:(k0 + CK) * P, n0:n0 + CW].rearrange("(k p) n -> p k n", p=P)

    def chunk_of(i, s, ch):
        kind = s[0]
        if kind == "ADA":
            return w_chunk(w_ada[s[1]], CK * ch, CW * s[2])
        if kind == "WF":
            return w_chunk(w_four_out[i], CK * (ch % 2), CW * (ch // 2))
        w, n0 = {"F": (w_in[i], 3 * D), "GF": (w_gate[i], D), "QK": (w_in[i], 0), "V": (w_in[i], 2 * D),
                 "GA": (w_gate[i], 0), "WA": (w_attn_out[i], 0), "WO": (w_out[i], 0)}[kind]
        return w_chunk(w, CK * ch, n0 + CW * s[1])

    ADA_A = 16
    mix0, exp0 = [], []
    n = ADA_A
    for i in range(DEPTH):
        mix0.append(n)
        n += len(stream_of(i))
        exp0.append(n)
        n += NE * EXP_CHUNKS
    assert all(v % RAW == 0 for v in exp0)

    place_of = [{sc: mix0[i] + n for n, sc in enumerate(stream_of(i))} for i in range(DEPTH)]

    ADA_TURN = {("V", 0): 1, ("WA", 1): 2}
    ada_last = [ADA_A - 1] + [place_of[0][(("ADA", i, AG - 1), 3)] for i in range(DEPTH)]
    assert all(ada_last[p_] < place_of[0][(s, 0)] for s, p_ in ADA_TURN.items())

    plan, owner = {}, []

    def add_tile(key, by):
        plan[key] = len(owner)
        owner.append(by)

    dft = [[(s, g) for s in range(i, 2) for g in range(FG)] for i in range(DEPTH)]
    for i in range(DEPTH):
        add_tile(("vec", i), "dve")
    for k in range(KT):
        add_tile(("x0", k), "act" if k % 2 else "dve")
    for i in range(DEPTH):
        add_tile((i, "n1"), "act")
        if i == 0:
            add_tile(("ada", 0), "dve")
        for s in steps_of(i):
            if i == 0 and s in ADA_TURN:
                add_tile(("ada", ADA_TURN[s]), "dve")
            if s == ("GF", 0):
                for sg_ in dft[i]:
                    add_tile((i, "Y") + sg_, "act")
            if s == ("GF", 1):
                for sg_ in dft[i]:
                    add_tile((i, "Z") + sg_, "dve")
            if s == ("WA", 0):
                for h in range(HEADS):
                    add_tile((i, "OT", h), "dve")
            for t in range(8 if s[0] == "WF" else 4):
                add_tile((i, s[0], s[1], t), "dve" if s[0] in ("WF", "WA", "WO") else "act")
        add_tile((i, "n2"), "act")
        add_tile((i, "log"), "act")
        for t in tiles[i]:
            for half in range(2):
                add_tile((i, "h2", t, half), "act" if half else "dve")
        add_tile((i, "rank"), "dve")
        for k in range(KT):
            add_tile((i, "yT", k), "dve")
    add_tile(("nf",), "act")
    for t in range(2):
        for half in range(2):
            add_tile(("out", t, half), "act" if half else "dve")

    done_at, signals = {}, 0
    for key, t in sorted(plan.items(), key=lambda kv: kv[1]):
        i = key[0]
        if key[1:] and key[1] in ("F", "GF", "WF", "QK", "V", "GA", "WA", "WO") and key[3] % 4 == 3:
            last = 3 if key[1] != "WF" else 1 + 2 * (key[3] // 4)
            done_at[key] = (w_used, place_of[i][(key[1:3], last)] + 1)
        else:
            signals += 1
            done_at[key] = (tile_done, signals)

    def bank(key):
        return ps[:, plan[key] % BANKS, :]

    def emptied(t):
        by = owner[t]
        return (free_act if by == "act" else free_dve), sum(1 for o in owner[:t + 1] if o == by)

    def take_tile(eng, key):
        t = plan[key]
        if t >= BANKS:
            s, v = emptied(t - BANKS)
            eng.wait_ge(s, v)

    def wait_tile(eng, key):
        eng.wait_ge(*done_at[key])

    def wait_emptied(eng, key):
        eng.wait_ge(*emptied(plan[key]))

    def wait_all_emptied(eng, key):
        for by, s_ in (("act", free_act), ("dve", free_dve)):
            eng.wait_ge(s_, sum(1 for o in owner[:plan[key] + 1] if o == by))

    def scaled(n, it, per):
        return n if it is None else n + it * per

    def raw_value(n, it, per):
        v = 16 * (n // RAW + 1)
        return v if it is None else v + it * (16 * (per // RAW))

    def load(sp, n, src, it=None, per=0):
        if it is not None or n >= RAW:
            sp.wait_ge(lo_ready, scaled(n - RAW + 1, it, per))
        sp.dma_start(raw[:, n % RAW, :, :], src).then_inc(raw_in[n % RAW], 16)

    def in_experts(n):
        return any(exp0[i] <= n < exp0[i] + NE * EXP_CHUNKS for i in range(DEPTH))

    def ring(n):
        return 2 * SPL if in_experts(n) else SPL

    def whi(n):
        r = n % ring(n)
        return (whi4 if r < SPL else whi8)[:, r % SPL, :, :]

    def wlo(n):
        r = n % ring(n)
        return (wlo4 if r < SPL else wlo8)[:, r % SPL, :, :]

    def split_hi(act, n, it=None, per=0):
        act.wait_ge(raw_in[n % RAW], raw_value(n, it, per))
        if it is not None or n >= SPL:
            act.wait_ge(w_used, scaled(n - ring(n) + 1, it, per))
        act.activation(whi(n), raw[:, n % RAW, :, :], ACT.Copy).then_inc(hi_ready, 1)

    def split_lo(dve, n, it=None, per=0):
        dve.wait_ge(hi_ready, scaled(n + 1, it, per))
        dve.tensor_tensor(wlo(n), raw[:, n % RAW, :, :], whi(n).bitcast(F32), ALU.subtract).then_inc(lo_ready, 1)

    def product(pe, acc, sh, sl, mh, ml, first, last):
        pe.matmul(acc, sh, mh, start=first, stop=False, skip_group_check=True)
        pe.matmul(acc, sh, ml, start=False, stop=False, skip_group_check=True)
        return pe.matmul(acc, sl, mh, start=False, stop=last, skip_group_check=True)

    block = es.enter_context(nc.Block())

    @block.sync
    def _(sp):
        sp.dma_start(cst[:, :], consts).then_inc(cst_in, 16)
        for s_, src in enumerate((ctx_tok, x)):
            sp.dma_start(tok0[:, 2 * s_:2 * s_ + 2, :], src[0].rearrange("(t p) n -> p t n", p=P)).then_inc(tok_in, 16)
        for n in range(ADA_A):
            load(sp, n, w_chunk(w_ada[0], CK * (n % 4), CW * (n // 4)))
        for i in range(DEPTH):
            for n, (s, ch) in enumerate(stream_of(i)):
                load(sp, mix0[i] + n, chunk_of(i, s, ch))
            nb = exp0[i]

            def weights(n, w, e, it=None):
                for ch in range(4):
                    k, cc = (ch % 2, ch // 2) if w is w_e_down else (ch, 0)
                    load(sp, n + ch, w_chunk(w[i, e], CK * k, CW * cc), it, 24)

            for e in range(2):
                weights(nb + 8 * e, w_e_gate, e)
                weights(nb + 8 * e + 4, w_e_up, e)
            with sp.Fori(0, NE // 2 - 1) as it:
                for j in range(2):
                    weights(nb + 16 + 12 * j, w_e_down, 2 * it + j, it)
                    weights(nb + 20 + 12 * j, w_e_gate, 2 * it + j + 2, it)
                    weights(nb + 24 + 12 * j, w_e_up, 2 * it + j + 2, it)
            for e in (NE - 2, NE - 1):
                weights(nb + EXP_CHUNKS * NE - 4 * (NE - e), w_e_down, e)
            sp.wait_ge(rt_loc[i], 1)
            over = sp.value_load(most[0:1, 0:1], min_val=0, max_val=T)
            nt = len(tiles[i])
            with sp.If(over > P):
                sp.wait_ge(lo_ready, exp0[i] + NE * EXP_CHUNKS)
                with sp.Fori(0, NE) as e:
                    first = sp.value_load(starts[0:1, bass.ds(e, 1)], min_val=0, max_val=2 * T)
                    for r in range(nt):
                        k = e * nt + r
                        sp.wait_ge(f_go[i], k + 1)
                        sp.dma_start(xg[:, 0, :], hbuf[bass.ds(first + r * P, P), :]).then_inc(f_in[i], 16)
                        for m, w in enumerate((w_e_gate, w_e_up)):
                            sp.dma_start(raw[:, 4 * m:4 * m + 4, :, :].rearrange("p s k n -> p (s k) n"),
                                         w[i, e].rearrange("(k p) n -> p k n", p=P)).then_inc(f_in[i], 16)
                        sp.wait_ge(f_pe[i], k * 4 + 2)
                        sp.dma_start(raw[:, 0:4, :, :].rearrange("p s k n -> p (s k n)").rearrange("p (k n) -> p k n", n=D),
                                     w_e_down[i, e].rearrange("(k p) n -> p k n", p=P)).then_inc(f_dn[i], 16)
                        sp.wait_ge(f_dve[i], k * 5 + 5)
                        sp.dma_start(ybuf[bass.ds(first + r * P, P), :], ytile[:, 0, :]).then_inc(f_out[i], 16)
                        sp.wait_ge(f_out[i], (k + 1) * 16)
                        sp.sem_inc(f_go[i], 1)

        sp.wait_ge(out_ready, 4)
        sp.dma_start(out[0].rearrange("(t p) n -> p t n", p=P), outt[:, :, :]).then_inc(out_done, 16)
        sp.wait_ge(out_done, 16)

    @block.gpsimd
    def _(pool):
        pool.memset(cond[:, :, :].bitcast(F32), 0.0).then_inc(filled, 1)
        pool.memset(epst[:, :], EPS).then_inc(filled, 1)
        pool.memset(zrow[:, :], 0.0).then_inc(filled, 1)
        for i, dst in enumerate((vrow, vrow1)):
            rows = [(V_BADA, b_ada[i], 48), (V_G1, g_norm1[i], 8), (V_G2, g_norm2[i], 8), (V_BG, b_gate[i], 16),
                    (V_SUB, g_subln[i], 1), (V_GF, g_final, 8), (V_C, c[0], 8), (V_C + 8, c_ctx, 8)]
            for r, src, k in rows:
                pool.dma_start(dst[r:r + k, :], src.rearrange("(k p) -> k p", p=P)).then_inc(vec_in, 16)
        pool.dma_start(lamv[:, :, :], lam_qk.rearrange("(a l) m d -> a (l m) d", a=1).to_broadcast([P, 4 * DEPTH, HD])).then_inc(lam_in, 16)
        pool.dma_start(wr[:, :, :], w_router.rearrange("(k p) n -> p k n", p=P)).then_inc(small_in, 16)
        pool.dma_start(brb[:, :], b_router.rearrange("(a n) -> a n", a=1).to_broadcast([P, NE])).then_inc(small_in, 16)
        pool.wait_ge(filled, 3)
        for r in range(2 * T // P, ROWS // P):
            pool.dma_start(hbuf[r * P:(r + 1) * P, :], zrow[:, :]).then_inc(pad_out, 16)
        for i in range(DEPTH):
            wait_all_emptied(pool, ("x0", KT - 1) if i == 0 else (0, "yT", KT - 1))
            pool.dma_start(xkeep, X[:, :, :].rearrange("p k t -> p (k t)")).then_inc(x_kept[i], 16)
            pool.wait_ge(x_kept[i], 16)
            pool.wait_ge(a_oc, first_item[i] + len(items[i]))
            pool.dma_start(X[:, :, :].rearrange("p k t -> p (k t)"), xkeep).then_inc(x_back[i], 16)
            pool.wait_ge(rt_loc[i], 1)
            wait_all_emptied(pool, (i, "rank"))
            if i == 0:
                pool.wait_ge(pad_out, 16 * (ROWS // P - 2 * T // P))
            for s in range(2):
                for t in tiles[i]:
                    pool.indirect_dma_start(hbuf, bass.IndirectOffsetOnAxis(ap=loc[:, s, t:t + 1], axis=0),
                                            h2tok[:, t, :], None).then_inc(sc_out[i], 16)
            pool.wait_ge(sc_out[i], 32 * len(tiles[i]))
            pool.sem_inc(y_free[i], 2)

            def first_row(e):
                return pool.value_load(starts[0:1, bass.ds(e, 1)], min_val=0, max_val=2 * T)

            def fetch(e, j):
                pool.dma_start(xg[:, j, :], hbuf[bass.ds(first_row(e), P), :]).then_inc(e_in[j], 16)

            def store(e, j, first=False):
                pool.wait_ge(e_ya, NE * i + e + 1)
                pool.wait_ge(e_yd, NE * i + e + 1)
                if not first:
                    pool.wait_ge(e_out[i], e * 16)
                    pool.sem_inc(y_free[i], 1)
                pool.dma_start(ybuf[bass.ds(first_row(e), P), :], ytile[:, j, :]).then_inc(e_out[i], 16)

            def refetch(e, j):
                pool.wait_ge(e_xt, NE * i + e - 1)
                fetch(e, j)

            fetch(0, 0)
            fetch(1, 1)
            refetch(2, 0)
            refetch(3, 1)
            store(0, 0, first=True)
            with pool.Fori(0, NE // 2 - 2) as it:
                for j in range(2):
                    refetch(2 * it + 4 + j, j)
                    store(2 * it + 1 + j, 1 - j)
            for e in range(NE - 3, NE):
                store(e, e % 2)
            pool.wait_ge(e_out[i], NE * 16)
            over = pool.value_load(most[0:1, 0:1], min_val=0, max_val=T)
            with pool.If(over > P):
                pool.sem_inc(f_go[i], 1)
                pool.wait_ge(f_out[i], 16 * NE * len(tiles[i]))
            for s, dst in enumerate((y1, y2)):
                for t in tiles[i]:
                    pool.indirect_dma_start(dst[:, t, :], None, ybuf[0:2 * P * len(tiles[i]), :],
                                            bass.IndirectOffsetOnAxis(ap=loc[:, s, t:t + 1], axis=0)).then_inc(y_in[i], 16)

    @block.tensor
    def _(pe):
        pe.wait_ge(cst_in, 16)
        pe.wait_ge(vec_in, 16 * 16)
        for i, src in enumerate((vrow, vrow1)):
            pe.transpose(bank(("vec", i))[:, 0:V_ROWS], src[0:V_ROWS, :], ident[0:V_ROWS, 0:V_ROWS]).then_inc(tile_done, 1)
        pe.wait_ge(tok_in, 32)
        for k in range(KT):
            take_tile(pe, ("x0", k))
            for t in range(4):
                m = pe.transpose(bank(("x0", k))[:, t * P:(t + 1) * P], tok0[:, t, k * P:(k + 1) * P], ident)
            m.then_inc(tile_done, 1)

        def ada_chunk(n, g, ch, first, last):
            pe.wait_ge(lo_ready, n + 1)
            for k in range(CK):
                kt = CK * ch + k
                at_g = cond[:, kt, AR - 4 - 4 * g:2 * AR - 4 - 4 * g]
                pe.matmul(ps[0:AR, 7, :], at_g, whi(n)[:, k, :], start=first and k == 0, stop=False, skip_group_check=True)
                m = pe.matmul(ps[0:AR, 7, :], at_g, wlo(n)[:, k, :], start=False, stop=last and k == CK - 1,
                              skip_group_check=True)
            m.then_inc(w_used, 1)

        def ada_turn(part):
            take_tile(pe, ("ada", part))
            pe.wait_ge(ada_rows, part + 1)
            for ct in range(4):
                m = pe.transpose(bank(("ada", part))[:, ct * AR:(ct + 1) * AR], ada_row[part][0:AR, ct * P:(ct + 1) * P],
                                 ident[0:AR, 0:AR])
            m.then_inc(tile_done, 1)

        def norm_sum(name, key, c0):
            o, os = KT * norms[name], KT * (norms[name] // 2)
            take_tile(pe, key)
            for k in range(KT):
                pe.wait_ge(n_sq, o + k + 1)
                m = pe.matmul(bank(key)[:, c0:T], ones, sq[:, k % 2, c0:T], start=k == 0, stop=k == KT - 1)
                m.then_inc(n_squ if k < KT - 1 else tile_done, 1)

        def by_weights(n, ch, keys_, c0, moving, chunks):
            pe.wait_ge(lo_ready, n + 1)
            for k in range(CK):
                kt = CK * ch + k
                for ct in range(4):
                    if kt == 0:
                        take_tile(pe, keys_[ct])
                    wcol = slice(ct * P, (ct + 1) * P)
                    m = product(pe, bank(keys_[ct])[:, c0:T], whi(n)[:, k, wcol], wlo(n)[:, k, wcol],
                                moving[0][:, kt, c0:T], moving[1][:, kt, c0:T], kt == 0, kt == CK * chunks - 1)
                    if kt == CK * chunks - 1 and ct < 3:
                        m.then_inc(tile_done, 1)
            m.then_inc(w_used, 1)

        def by_tokens(n, ch, keys_):
            pe.wait_ge(lo_ready, n + 1)
            for k in range(CK):
                kt = CK * ch + k
                for t in range(4):
                    if kt == 0:
                        take_tile(pe, keys_[t])
                    tc = slice(t * P, (t + 1) * P)
                    m = product(pe, bank(keys_[t])[:, :], Hhi[:, kt, tc], Hlo[:, kt, tc], whi(n)[:, k, :], wlo(n)[:, k, :],
                                kt == 0, kt == KT - 1)
                    if kt == KT - 1 and t < 3:
                        m.then_inc(tile_done, 1)
            m.then_inc(w_used, 1)

        def dft_channels(i):
            for s, g in dft[i]:
                key = (i, "Y", s, g)
                take_tile(pe, key)
                wait_emptied(pe, (i, "F", 0, g))
                for t in range(2):
                    c0 = s * SEQ + t * P
                    m = pe.matmul(bank(key)[:, t * 2 * P:(t + 1) * 2 * P], FT[:, g, c0:c0 + P], cs(C_CD, 2 * P),
                                  start=True, stop=True, skip_group_check=True)
                m.then_inc(tile_done, 1)

        def dft_tokens(i):
            for s, g in dft[i]:
                key = (i, "Z", s, g)
                take_tile(pe, key)
                wait_emptied(pe, (i, "Y", s, g))
                for t in range(2):
                    pe.matmul(bank(key)[:, 0:SEQ], Y[:, s, g, t, 0:P], cs(C_CL + t * SEQ, SEQ), start=t == 0, stop=False)
                    m = pe.matmul(bank(key)[:, 0:SEQ], Y[:, s, g, t, P:2 * P], cs(C_SL + t * SEQ, SEQ), start=False,
                                  stop=t == 1)
                m.then_inc(tile_done, 1)

        def attention(i):
            wait_all_emptied(pe, (i, "GA", 1, 3))
            pe.wait_ge(roped[i], 2 * HEADS)
            pe.wait_ge(ada_rows, 3)
            its, f = items[i], first_item[i]
            for j in range(len(its) + 3):
                if j < len(its):
                    h, q = its[j]
                    if j >= 2:
                        pe.wait_ge(a_exp, 2 * (f + j - 1))
                    for m_ in range(2):
                        d = slice(m_ * HD, (m_ + 1) * HD)
                        m = pe.matmul(ps[:, 2 * (j % 2) + m_, 0:keys(q)], QK[d, h, q * P:(q + 1) * P],
                                      QK[d, HEADS + h, 0:keys(q)], start=True, stop=True)
                    m.then_inc(a_s, 1)
                t = j - 2
                if 0 <= t < len(its):
                    h, q = its[t]
                    pe.wait_ge(a_comb, f + t + 1)
                    if t >= 2:
                        pe.wait_ge(a_trc, f + t - 1)
                    for k in range(keys(q) // P):
                        m = pe.transpose(ps[:, 4 + t % 2, k * P:(k + 1) * P], A[:, t % 2, k * P:(k + 1) * P], ident)
                    m.then_inc(a_tr, 1)
                t = j - 3
                if t >= 0:
                    h, q = its[t]
                    pe.wait_ge(a_trc, f + t + 1)
                    if t >= 2:
                        pe.wait_ge(a_oc, f + t - 1)
                    nk = keys(q) // P
                    for k in range(nk):
                        m = pe.matmul(ps[:, 6 + t % 2, 0:P], AT[:, t % 2, k * P:(k + 1) * P],
                                      V[:, k, h * P:(h + 1) * P], start=k == 0, stop=k == nk - 1, skip_group_check=True)
                    m.then_inc(a_pv, 1)
            pe.wait_ge(o_nrm[i], 1)
            for h in range(HEADS):
                take_tile(pe, (i, "OT", h))
                for q in tiles[i]:
                    m = pe.transpose(bank((i, "OT", h))[:, q * P:(q + 1) * P], O[:, q, h, :], ident)
                m.then_inc(tile_done, 1)

        norm_sum("n1_0", (0, "n1"), 0)
        pe.wait_ge(cond_ready, 1)
        pe.wait_ge(filled, 3)
        for n in range(ADA_A):
            ada_chunk(n, n // 4, n % 4, n == 0, n == ADA_A - 1)
        ada_turn(0)

        for i in range(DEPTH):
            c0 = col0[i]
            if i:
                norm_sum(f"n1_{i}", (i, "n1"), 0)
            pe.wait_ge(n_lo, KT * (i + 1))
            for (s, ch), n in place_of[i].items():
                kind = s[0]
                if (s, ch) == (("GF", 0), 0):
                    dft_channels(i)
                if (s, ch) == (("GF", 1), 0):
                    dft_tokens(i)
                if i == 0 and s in ADA_TURN and ch == 0:
                    ada_turn(ADA_TURN[s])
                if kind == "ADA":
                    first = (s, ch) in ((("ADA", 0, ADA_A // 4), 0), (("ADA", 1, 0), 0))
                    if first:
                        pe.wait_ge(ada_rows, 1 + s[1])
                    ada_chunk(n, s[2], ch, first, n in ada_last)
                elif kind == "WF":
                    if ch == 0:
                        wait_emptied(pe, (i, "Z") + dft[i][-1])
                    by_weights(n, ch % 2, [(i, "WF", 0, 4 * (ch // 2) + t) for t in range(4)], c0, (Zhi, Zlo), 2)
                elif kind == "V":
                    by_tokens(n, ch, [(i, "V", s[1], t) for t in range(4)])
                elif kind == "WA":
                    if (s[1], ch) == (0, 0):
                        attention(i)
                        pe.wait_ge(ot_l[i], HEADS)
                    by_weights(n, ch, [(i, "WA", s[1], t) for t in range(4)], c0, (OThi, OTlo), 4)
                elif kind == "WO":
                    pe.wait_ge(m_l[i], KT)
                    by_weights(n, ch, [(i, "WO", s[1], t) for t in range(4)], c0, (Hhi, Hlo), 4)
                else:
                    by_weights(n, ch, [(i, kind, s[1], t) for t in range(4)], 0 if kind == "QK" and s[1] >= 2 else c0,
                               (Hhi, Hlo), 4)

            norm_sum(f"n2_{i}", (i, "n2"), c0)
            pe.wait_ge(small_in, 32)
            key = (i, "log")
            take_tile(pe, key)
            pe.wait_ge(n_hf, KT * (2 * i + 2))
            for t in tiles[i]:
                for k in range(KT):
                    m = pe.matmul(bank(key)[:, NE * t:NE * t + NE], h2T[:, k, t * P:(t + 1) * P], wr[:, k, :],
                                  start=k == 0, stop=k == KT - 1, skip_group_check=True)
            m.then_inc(tile_done, 1)
            for t in tiles[i]:
                for half in range(2):
                    key = (i, "h2", t, half)
                    take_tile(pe, key)
                    for k in range(4):
                        m = pe.transpose(bank(key)[:, k * P:(k + 1) * P], h2T[:, 4 * half + k, t * P:(t + 1) * P], ident)
                    m.then_inc(tile_done, 1)
            pe.wait_ge(rt_asg[i], 1)
            key = (i, "rank")
            take_tile(pe, key)
            tl = tiles[i]
            for t in tl:
                for u in tl[:tl.index(t) + 1]:
                    pe.matmul(bank(key)[:, NE * t:NE * t + NE], tri if u == t else ones, asg[:, u, :], start=u == tl[0],
                              stop=u == t, skip_group_check=True)
            for u in tl:
                m = pe.matmul(bank(key)[:, 64:64 + NE], ones, asg[:, u, :], start=u == tl[0], stop=u == tl[-1],
                              skip_group_check=True)
            m.then_inc(tile_done, 1)
            wait_all_emptied(pe, key)

            nb, cb = exp0[i], NE * i

            def turn_tokens(e, j):
                pe.wait_ge(e_in[j], (8 * cb + 16) + (e - j) * 8)
                pe.wait_ge(e_xl, cb + e)
                for k in range(KT):
                    m = pe.transpose(ps[:, 4 + k // 4, (k % 4) * P:(k % 4 + 1) * P], xg[:, j, k * P:(k + 1) * P], ident)
                m.then_inc(e_xt, 1)

            def into_hidden(n, e, m_, it=None):
                if m_ == 0:
                    pe.wait_ge(e_xl, cb + e + 1)
                    pe.wait_ge(e_gu, cb + e)
                else:
                    pe.wait_ge(e_he, cb + e)
                for ch in range(4):
                    pe.wait_ge(lo_ready, scaled(n + ch + 1, it, 24))
                    for k in range(CK):
                        kt = CK * ch + k
                        m = product(pe, ps[:, m_, :], xhi[:, kt, :], xlo[:, kt, :], whi(n + ch)[:, k, :],
                                    wlo(n + ch)[:, k, :], kt == 0, kt == KT - 1)
                    m.then_inc(w_used, 1)

            def turn_hidden(e):
                pe.wait_ge(e_he, cb + e + 1)
                for k in range(KE):
                    m = pe.transpose(ps[:, 6, k * P:(k + 1) * P], he[:, k * P:(k + 1) * P], ident)
                m.then_inc(e_ht, 1)

            def down(n, e, it=None):
                pe.wait_ge(e_hl, cb + e + 1)
                pe.wait_ge(e_ya, cb + e)
                pe.wait_ge(e_yd, cb + e)
                for ch in range(4):
                    pe.wait_ge(lo_ready, scaled(n + ch + 1, it, 24))
                    for k in range(CK):
                        kt = CK * (ch % 2) + k
                        m = product(pe, ps[:, 2 + ch // 2, :], hehi[:, kt, :], helo[:, kt, :], whi(n + ch)[:, k, :],
                                    wlo(n + ch)[:, k, :], kt == 0, kt == KE - 1)
                    m.then_inc(w_used, 1)

            for e in range(2):
                turn_tokens(e, e)
                into_hidden(nb + 8 * e, e, 0)
                if e:
                    turn_hidden(0)
                into_hidden(nb + 8 * e + 4, e, 1)
            with pe.Fori(0, NE // 2 - 1) as it:
                for j in range(2):
                    e = 2 * it + (2 + j)
                    n = nb + 16 + 12 * j
                    turn_tokens(e, j)
                    down(n, 2 * it + j, it)
                    into_hidden(n + 4, e, 0, it)
                    turn_hidden(2 * it + (1 + j))
                    into_hidden(n + 8, e, 1, it)
            n = nb + NE * EXP_CHUNKS - 8
            down(n, NE - 2)
            turn_hidden(NE - 1)
            down(n + 4, NE - 1)
            pe.wait_ge(e_ya, cb + NE)
            pe.wait_ge(e_yd, cb + NE)

            over = pe.value_load(most[0:1, 0:1], min_val=0, max_val=T)
            with pe.If(over > P):
                with pe.Fori(0, NE * len(tiles[i])) as r:
                    pe.wait_ge(f_in[i], r * 48 + 48)
                    for k in range(KT):
                        m = pe.transpose(ps[:, 4 + k // 4, (k % 4) * P:(k % 4 + 1) * P], xg[:, 0, k * P:(k + 1) * P], ident)
                    m.then_inc(f_pe[i], 1)
                    pe.wait_ge(f_dve[i], r * 5 + 1)
                    for m_ in range(2):
                        for k in range(KT):
                            m = pe.matmul(ps[:, m_, :], xT32[:, k, :], raw[:, 4 * m_ + k // 2, k % 2, :], start=k == 0,
                                          stop=k == KT - 1)
                    m.then_inc(f_pe[i], 1)
                    pe.wait_ge(f_dve[i], r * 5 + 3)
                    for k in range(KE):
                        m = pe.transpose(ps[:, 6, k * P:(k + 1) * P], he[:, k * P:(k + 1) * P], ident)
                    m.then_inc(f_pe[i], 1)
                    pe.wait_ge(f_dve[i], r * 5 + 4)
                    pe.wait_ge(f_dn[i], r * 16 + 16)
                    for half in range(2):
                        for k in range(KE):
                            m = pe.matmul(ps[:, 2 + half, :], hT32[:, k, :], raw[:, k, half, :], start=k == 0, stop=k == KE - 1)
                    m.then_inc(f_pe[i], 1)
                    pe.wait_ge(f_dve[i], r * 5 + 5)

            pe.wait_ge(y_sum[i], len(tiles[i]))
            for k in range(KT):
                key = (i, "yT", k)
                take_tile(pe, key)
                for t in tiles[i]:
                    m = pe.transpose(bank(key)[:, t * P:(t + 1) * P], y2[:, t, k * P:(k + 1) * P], ident)
                m.then_inc(tile_done, 1)

        norm_sum("nf", ("nf",), SEQ)
        pe.wait_ge(n_hf, KT * 5)
        for t in range(2):
            for half in range(2):
                key = ("out", t, half)
                take_tile(pe, key)
                for k in range(4):
                    cc = SEQ + t * P
                    m = pe.transpose(bank(key)[:, k * P:(k + 1) * P], h2T[:, 4 * half + k, cc:cc + P], ident)
                m.then_inc(tile_done, 1)

    lam_init = [0.8 - 0.6 * math.exp(-0.3 * i) for i in range(DEPTH)]
    streams = [(0, SEQ, 1), (SEQ, T, 0)]

    @block.scalar
    def _(act):
        act.wait_ge(filled, 3)

        norm_tile = {"n1_0": (0, "n1"), "n2_0": (0, "n2"), "n1_1": (1, "n1"), "n2_1": (1, "n2"), "nf": ("nf",)}

        def norm_rms(name, c0):
            o = KT * norms[name]
            for k in range(KT):
                if k >= 2:
                    act.wait_ge(n_squ, o - norms[name] + k - 1)
                act.activation(sq[:, k % 2, c0:T], X[:, k, c0:T], ACT.Square).then_inc(n_sq, 1)
            key = norm_tile[name]
            wait_tile(act, key)
            act.activation(std[:, c0:T], bank(key)[:, c0:T], ACT.Sqrt, bias=epst[:, 0:1], scale=1.0 / D).then_inc(free_act, 1)

        def norm_apply(name, c0, scale, bias, split):
            o, os = KT * norms[name], KT * (norms[name] // 2)
            for k in range(KT):
                act.wait_ge(n_xn, o + k + 1)
                if split and k >= 2:
                    act.wait_ge(n_lo, os + k - 1)
                dst = hf[:, k % 2] if split else h2T[:, k]
                for a_, b_, s in [p for p in streams if p[0] >= c0]:
                    kw = {"bias": bias(k, s)} if bias else {}
                    m = act.activation(dst[:, a_:b_], xn[:, k % 2, a_:b_], ACT.Identity, scale=scale(k, s), **kw)
                m.then_inc(n_hf, 1)
                if split:
                    act.wait_ge(n_hf, o + k + 1)
                    act.activation(Hhi[:, k, :], hf[:, k % 2, :], ACT.Copy).then_inc(n_hi, 1)

        def empty_ada(part):
            act.wait_ge(w_used, ada_last[part] + 1)
            act.activation(ada_row[part][0:AR, :], ps[0:AR, 7, :], ACT.Copy).then_inc(ada_rows, 1)

        def empty_step(i, s):
            c0, kind = col0[i], s[0]
            if kind == "ADA" and s[2] == AG - 1:
                empty_ada(1 + s[1])
            if kind in ("ADA", "WF", "WO"):
                return
            for t in range(4):
                key = (i, kind, s[1], t)
                b = 4 * s[1] + t
                if kind == "WA":
                    act.wait_ge(m_f[i], b + 1)
                    act.activation(Hhi[:, b, c0:T], G[:, b, c0:T], ACT.Copy).then_inc(m_h[i], 1)
                    continue
                wait_tile(act, key)
                if kind == "F":
                    m = act.activation(FT[:, t, c0:T], bank(key)[:, c0:T], ACT.Copy)
                elif kind == "QK":
                    cc = 0 if s[1] >= 2 else c0
                    if i == 0 and b == 0:
                        act.wait_ge(pad_out, 16 * (ROWS // P - 2 * T // P))
                    m = act.activation(QK[:, b, cc:T], bank(key)[:, cc:T], ACT.Copy)
                elif kind == "V":
                    m = act.activation(V[:, t, s[1] * CW:(s[1] + 1) * CW], bank(key)[:, :], ACT.Copy)
                else:
                    off = V_BG + (0 if kind == "GA" else 8) + b
                    if kind == "GA" and b == 0:
                        act.wait_ge(roped[i], 2 * HEADS)
                    m = act.activation((GA if kind == "GA" else G)[:, b, c0:T], bank(key)[:, c0:T], ACT.Sigmoid,
                                       bias=vec[i][:, off:off + 1])
                m.then_inc(free_act, 1)

        def attention(i):
            act.wait_ge(x_kept[i], 16)
            its = items[i]
            for j in range(len(its) + 2):
                if j < len(its):
                    q, b = its[j][1], j % 2
                    act.wait_ge(a_neg, first_item[i] + j + 1)
                    if j >= 2:
                        act.wait_ge(a_comb, first_item[i] + j - 1)
                    for m_ in range(2):
                        act.activation(E[:, b, m_, 0:keys(q)], ps[:, 2 * b + m_, 0:keys(q)], ACT.Exp,
                                       bias=aneg[:, b, m_:m_ + 1], scale=ATT_SCALE,
                                       accum_out=asum[:, b, m_:m_ + 1]).then_inc(a_exp, 1)
                t = j - 2
                if t >= 0:
                    q, b = its[t][1], t % 2
                    act.wait_ge(a_tr, first_item[i] + t + 1)
                    if t >= 2:
                        act.wait_ge(a_pv, first_item[i] + t - 1)
                    act.activation(AT[:, b, 0:keys(q)], ps[:, 4 + b, 0:keys(q)], ACT.Copy).then_inc(a_trc, 1)
            tl = tiles[i]
            act.wait_ge(a_oc, first_item[i] + len(its))
            act.activation(osq[:, tl[0]:, :, :].rearrange("p q h e -> p (q h e)"),
                           O[:, tl[0]:, :, :].rearrange("p q h e -> p (q h e)"), ACT.Square).then_inc(o_sq[i], 1)
            act.wait_ge(o_ss[i], 1)
            no = len(tl) * HEADS
            act.activation(ostd[:, 0:no], oss[:, 0:no], ACT.Sqrt, bias=epst[:, 0:1], scale=1.0 / P).then_inc(o_std[i], 1)
            for h in range(HEADS):
                wait_emptied(act, (i, "OT", h))
                act.activation(OThi[:, h, col0[i]:T], ot32[:, h % 2, col0[i]:T], ACT.Copy).then_inc(ot_h[i], 1)

        def dft_channels(i):
            for s, g in dft[i]:
                key = (i, "Y", s, g)
                wait_tile(act, key)
                act.activation(Y[:, s, g, :, :].rearrange("p t n -> p (t n)"), bank(key), ACT.Copy).then_inc(free_act, 1)

        def dft_tokens(i):
            for s, g in dft[i]:
                key = (i, "Z", s, g)
                wait_tile(act, key)
                act.activation(Zhi[:, g, s * SEQ:(s + 1) * SEQ], bank(key)[:, 0:SEQ], ACT.Copy).then_inc(z_hi[i], 1)

        wait_emptied(act, ("vec", 0))
        act.activation(csig[:, :], vec[0][:, V_C:V_C + 16], ACT.Sigmoid).then_inc(cond_sig, 1)
        act.wait_ge(cond_sil, 1)
        act.activation(cond[:, :, AR - 4:AR].rearrange("p k (s u) -> p s k u", u=2)[:, :, :, 0],
                       csil[:, :].rearrange("p (s k) -> p s k", s=2), ACT.Copy).then_inc(cond_hi, 1)
        for k in range(1, KT, 2):
            wait_tile(act, ("x0", k))
            act.activation(X[:, k, :], bank(("x0", k)), ACT.Copy).then_inc(free_act, 1)
        wait_all_emptied(act, ("x0", KT - 1))
        norm_rms("n1_0", 0)
        act.wait_ge(lam_s, 1)
        act.activation(lexp[:, :], lsum[:, :], ACT.Exp).then_inc(lam_e, 1)
        for n in range(ADA_A):
            split_hi(act, n)
        empty_ada(0)
        for i in range(DEPTH):
            n0 = mix0[i]
            for ch in range(3):
                split_hi(act, n0 + ch)
            if i == 0:
                act.wait_ge(mod_a, 1)
            else:
                wait_all_emptied(act, (0, "yT", KT - 1))
                norm_rms("n1_1", 0)
                act.wait_ge(mod_b, 2)
            norm_apply(f"n1_{i}", 0, lambda k, s: sc1[i][:, k, s:s + 1], lambda k, s: mod[i][:, k, s:s + 1], True)
            at_chunk = {n: sc for sc, n in place_of[i].items()}
            for n in range(n0 + 3, exp0[i] + SPL):
                s, ch = at_chunk.get(n - SPL, (None, 0))
                if ch == 3:
                    empty_step(i, s)
                if n - 3 == place_of[i][(("GF", 0), 0)]:
                    dft_channels(i)
                if n - 3 == place_of[i][(("GF", 1), 0)]:
                    dft_tokens(i)
                if n - SPL == place_of[i][(("WA", 0), 0)]:
                    attention(i)
                if n < exp0[i]:
                    split_hi(act, n)
            wait_emptied(act, (i, "WO", 1, 3))
            act.wait_ge(mod_b, 1)
            norm_rms(f"n2_{i}", col0[i])
            norm_apply(f"n2_{i}", col0[i], lambda k, s: sc2[i][:, k, s:s + 1], lambda k, s: mod[i][:, 24 + k, s:s + 1], False)
            key = (i, "log")
            t0 = tiles[i][0]
            wait_tile(act, key)
            act.activation(aff[:, t0:, :].rearrange("p t e -> p (t e)"), bank(key)[:, NE * t0:4 * NE],
                           ACT.Sigmoid).then_inc(free_act, 1)
            for t in tiles[i]:
                key = (i, "h2", t, 1)
                wait_tile(act, key)
                act.activation(h2tok[:, t, CW:D], bank(key), ACT.Copy).then_inc(free_act, 1)

            nb, cb = exp0[i], NE * i

            def tokens_hi(e):
                act.wait_ge(e_xt, cb + e + 1)
                act.activation(xhi[:, :, :].rearrange("p k t -> p (k t)"), ps[:, 4:6, :].rearrange("p b n -> p (b n)"),
                               ACT.Copy).then_inc(e_xh, 1)

            def splits(n, count, it=None):
                for ch in range(count):
                    split_hi(act, n + ch, it, 24)

            def sigmoid(n, it=None):
                act.wait_ge(w_used, scaled(n, it, 24))
                act.activation(sg[:, :], ps[:, 0, :], ACT.Sigmoid).then_inc(e_sig, 1)

            def hidden_hi(e):
                act.wait_ge(e_ht, cb + e + 1)
                act.activation(hehi[:, :, :].rearrange("p k t -> p (k t)"), ps[:, 6, :], ACT.Copy).then_inc(e_hh, 1)

            def result(n, e, j, it=None):
                act.wait_ge(w_used, scaled(n, it, 24))
                act.wait_ge(y_free[i], e + 1)
                act.activation(ytile[:, j, 0:CW], ps[:, 2, :], ACT.Copy).then_inc(e_ya, 1)

            act.wait_ge(w_used, nb)
            splits(nb, 4)
            act.wait_ge(sc_out[i], 32 * len(tiles[i]))
            tokens_hi(0)
            splits(nb + 4, 8)
            sigmoid(nb + 4)
            splits(nb + 12, 4)
            tokens_hi(1)
            with act.Fori(0, NE // 2 - 1) as it:
                for j in range(2):
                    n = nb + 16 + 12 * j
                    splits(n, 4, it)
                    sigmoid(n - 4, it)
                    hidden_hi(2 * it + j)
                    splits(n + 4, 4, it)
                    tokens_hi(2 * it + 2 + j)
                    splits(n + 8, 3, it)
                    result(n + 4, 2 * it + j, j, it)
                    splits(n + 11, 1, it)
            n = nb + NE * EXP_CHUNKS - 8
            splits(n, 4)
            sigmoid(n - 4)
            hidden_hi(NE - 2)
            splits(n + 4, 4)
            result(n + 4, NE - 2, 0)
            hidden_hi(NE - 1)
            result(n + 8, NE - 1, 1)

            over = act.value_load(most[0:1, 0:1], min_val=0, max_val=T)
            with act.If(over > P):
                with act.Fori(0, NE * len(tiles[i])) as r:
                    act.wait_ge(f_pe[i], r * 4 + 2)
                    act.activation(sg[:, :], ps[:, 0, :], ACT.Sigmoid).then_inc(f_act[i], 1)
                    act.wait_ge(f_dve[i], r * 5 + 5)
        wait_all_emptied(act, (1, "yT", KT - 1))
        norm_rms("nf", SEQ)
        norm_apply("nf", SEQ, lambda k, s: vec[0][:, V_GF + k:V_GF + k + 1], None, False)
        for t in range(2):
            wait_tile(act, ("out", t, 1))
            act.activation(outt[:, t, CW:D], bank(("out", t, 1)), ACT.Copy).then_inc(out_ready, 1)

    @block.vector
    def _(dve):
        chain = [0]

        def link(ins):
            chain[0] += 1
            ins.then_inc(dve_chain, 1)
            dve.wait_ge(dve_chain, chain[0])

        def stt(o, a, s, b, op0, op1):
            return dve.scalar_tensor_tensor(out=o, in0=a, scalar=s, in1=b, op0=op0, op1=op1)

        def spread(ap, shape):
            return ap.to_broadcast(shape)

        def norm(name, c0, split):
            o, os = KT * norms[name], KT * (norms[name] // 2)
            key = {"n1_0": (0, "n1"), "n2_0": (0, "n2"), "n1_1": (1, "n1"), "n2_1": (1, "n2"), "nf": ("nf",)}[name]
            wait_emptied(dve, key)
            link(dve.reciprocal(rinv[:, c0:T], std[:, c0:T]))
            for k in range(KT + 1):
                if k < KT:
                    if k >= 2:
                        dve.wait_ge(n_hf, o + k - 1)
                    dve.tensor_tensor(xn[:, k % 2, c0:T], X[:, k, c0:T], rinv[:, c0:T], ALU.mult).then_inc(n_xn, 1)
                if split and k >= 1:
                    dve.wait_ge(n_hi, os + k)
                    dve.tensor_tensor(Hlo[:, k - 1, :], hf[:, (k - 1) % 2, :], Hhi[:, k - 1, :].bitcast(F32),
                                      ALU.subtract).then_inc(n_lo, 1)

        def adaln(part, i, g0, g1, done):
            b0, b1 = 4 * g0, 4 * g1
            m = mod[i][:, b0:b1, :]
            key = ("ada", part)
            wait_tile(dve, key)
            for ct in range(4):
                sums = bank(key)[:, ct * AR + 4 * g0:ct * AR + 4 * g1].rearrange("p (g s u) -> p g s u", s=2, u=2)
                ins = dve.tensor_reduce(m.rearrange("p (g c) s -> p g c s", c=4)[:, :, ct, :], sums, AX.X, ALU.add)
            ins.then_inc(free_dve, 1)
            wait_emptied(dve, key)
            bias = vec[i][:, V_BADA + b0:V_BADA + b1].unsqueeze(2)
            ins = dve.tensor_tensor(m, m, spread(bias, [P, b1 - b0, 2]), ALU.add)
            for sc, blk, g in ((sc1[i], 8, V_G1), (sc2[i], 32, V_G2)):
                if b0 <= blk < b1:
                    link(ins)
                    ins = stt(sc[:, :, :], mod[i][:, blk:blk + 8, :], 1.0,
                              spread(vec[i][:, g:g + 8].unsqueeze(2), [P, KT, 2]), ALU.add, ALU.mult)
            ins.then_inc(done, 1)

        def empty_step(i, s, half=1):
            c0, kind = col0[i], s[0]
            parts = [p for p in streams if p[0] >= c0]
            if kind == "QK":
                for t in range(4):
                    b = 4 * s[1] + t
                    wait_emptied(dve, (i, "QK", s[1], t))
                    lat = QK[:, b, SEQ:T]
                    link(dve.stream_shuffle(rt[:, t % 2, :], lat, [(r + 16) % 32 for r in range(32)]))
                    link(dve.tensor_tensor(rt[:, t % 2, :], rt[:, t % 2, :], cs(C_RS, SEQ), ALU.mult))
                    link(dve.tensor_tensor(lat, lat, cs(C_RC, SEQ), ALU.mult))
                    dve.tensor_tensor(lat, lat, rt[:, t % 2, :], ALU.add).then_inc(roped[i], 1)
            elif kind == "WF":
                for t in range(4 * half, 4 * half + 4):
                    key = (i, "WF", 0, t)
                    wait_emptied(dve, (i, "GF", t // 4, t % 4))
                    wait_tile(dve, key)
                    dve.tensor_tensor(G[:, t, c0:T], bank(key)[:, c0:T], G[:, t, c0:T], ALU.mult).then_inc(free_dve, 1)
            elif kind == "WA":
                for t in range(4):
                    b, key = 4 * s[1] + t, (i, "WA", s[1], t)
                    wait_tile(dve, key)
                    ga = GA[:, b, c0:T]
                    dve.tensor_tensor(ga, bank(key)[:, c0:T], ga, ALU.mult).then_inc(free_dve, 1)
                    wait_emptied(dve, key)
                    dve.tensor_tensor(G[:, b, c0:T], G[:, b, c0:T], ga, ALU.add).then_inc(m_f[i], 1)
                for t in range(4):
                    b = 4 * s[1] + t
                    dve.wait_ge(m_h[i], b + 1)
                    dve.tensor_tensor(Hlo[:, b, c0:T], G[:, b, c0:T], Hhi[:, b, c0:T].bitcast(F32),
                                      ALU.subtract).then_inc(m_l[i], 1)
            elif kind == "WO":
                if s[1] == 0:
                    dve.wait_ge(x_back[i], 16)
                for t in range(4):
                    b, key = 4 * s[1] + t, (i, "WO", s[1], t)
                    wait_tile(dve, key)
                    for a_, b_, cd in parts:
                        m = stt(X[:, b, a_:b_], bank(key)[:, a_:b_], mod[i][:, 16 + b, cd:cd + 1], X[:, b, a_:b_],
                                ALU.mult, ALU.add)
                    m.then_inc(free_dve, 1)

        def attention(i):
            link(dve.tensor_scalar(gsub[:, :], vec[i][:, V_SUB:V_SUB + 1], 1.0 - lam_init[i], None, ALU.mult))
            its = items[i]
            for j in range(len(its) + 3):
                if j < len(its):
                    q, b = its[j][1], j % 2
                    dve.wait_ge(a_s, first_item[i] + j + 1)
                    link(dve.tensor_reduce(amax[:, b, :], ps[:, 2 * b:2 * b + 2, 0:keys(q)], AX.X, ALU.max))
                    dve.tensor_scalar(aneg[:, b, :], amax[:, b, :], -ATT_SCALE, None, ALU.mult).then_inc(a_neg, 1)
                if 1 <= j <= len(its):
                    q, b = its[j - 1][1], (j - 1) % 2
                    dve.wait_ge(a_exp, 2 * first_item[i] + 2 * j)
                    link(dve.reciprocal(arec[:, b, :], asum[:, b, :]))
                    link(dve.tensor_tensor(arec1[:, b:b + 1], arec[:, b, 1:2], nlam[:, i:i + 1], ALU.mult))
                    e0, e1 = E[:, b, 0, 0:keys(q)], E[:, b, 1, 0:keys(q)]
                    link(dve.tensor_scalar(e1, e1, arec1[:, b:b + 1], None, ALU.mult))
                    if j >= 3:
                        dve.wait_ge(a_tr, first_item[i] + j - 2)
                    stt(A[:, b, 0:keys(q)], e0, arec[:, b, 0:1], e1, ALU.mult, ALU.add).then_inc(a_comb, 1)
                t = j - 3
                if t >= 0:
                    h, q = its[t]
                    dve.wait_ge(a_pv, first_item[i] + t + 1)
                    dve.tensor_copy(O[:, q, h, :], ps[:, 6 + t % 2, 0:P]).then_inc(a_oc, 1)
            tl = tiles[i]
            no = len(tl) * HEADS
            dve.wait_ge(o_sq[i], 1)
            heads = lambda t_: t_[:, tl[0]:, :, :].rearrange("p q h e -> p (q h) e")
            dve.tensor_reduce(oss[:, 0:no], heads(osq), AX.X, ALU.add).then_inc(o_ss[i], 1)
            dve.wait_ge(o_std[i], 1)
            link(dve.reciprocal(orin[:, 0:no], ostd[:, 0:no]))
            dve.tensor_tensor(heads(O), heads(O), spread(orin[:, 0:no].unsqueeze(2), [P, no, P]), ALU.mult).then_inc(o_nrm[i], 1)
            c0 = col0[i]
            for h in range(HEADS + 1):
                if h < HEADS:
                    key = (i, "OT", h)
                    wait_tile(dve, key)
                    if h >= 2:
                        dve.wait_ge(ot_l[i], h - 1)
                    dve.tensor_scalar(ot32[:, h % 2, c0:T], bank(key)[:, c0:T], gsub[:, 0:1], None, ALU.mult).then_inc(free_dve, 1)
                if h >= 1:
                    dve.wait_ge(ot_h[i], h)
                    dve.tensor_tensor(OTlo[:, h - 1, c0:T], ot32[:, (h - 1) % 2, c0:T], OThi[:, h - 1, c0:T].bitcast(F32),
                                      ALU.subtract).then_inc(ot_l[i], 1)

        def dft_tokens(i):
            for m_, (s, g) in enumerate(dft[i]):
                key = (i, "Z", s, g)
                cols = slice(s * SEQ, (s + 1) * SEQ)
                dve.wait_ge(z_hi[i], m_ + 1)
                dve.tensor_tensor(Zlo[:, g, cols], bank(key)[:, 0:SEQ], Zhi[:, g, cols].bitcast(F32),
                                  ALU.subtract).then_inc(free_dve, 1)

        def route(i):
            t0, nt = tiles[i][0], len(tiles[i])
            v = lambda t_: t_[:, t0:]
            g4 = lambda t_: v(t_).rearrange("p t (g e) -> p t g e", g=4)
            key_e = cs(C_KE, NE).unsqueeze(1)
            key_g = cs(C_KG, 4).unsqueeze(1)
            row = lambda t_, n_: spread(v(t_).unsqueeze(2), [P, nt, n_])

            def first_max(src, n_, keys_, work, onehot):
                link(dve.tensor_reduce(v(tm), v(src), AX.X, ALU.max))
                link(dve.tensor_tensor(v(work), v(src), row(tm, n_), ALU.is_equal))
                link(dve.tensor_tensor(v(work), v(work), spread(keys_, [P, nt, n_]), ALU.mult))
                link(dve.tensor_reduce(v(tm), v(work), AX.X, ALU.max))
                link(dve.tensor_tensor(v(onehot), v(work), row(tm, n_), ALU.is_equal))

            wait_emptied(dve, (i, "log"))
            link(dve.tensor_tensor(v(sel), v(aff), spread(brb[:, :].unsqueeze(1), [P, nt, NE]), ALU.add))
            s4 = g4(sel)
            for m_, (a_, b_) in enumerate([(0, 1), (0, 2), (0, 3), (1, 2), (1, 3), (2, 3)]):
                ins = dve.tensor_tensor(v(pr)[:, :, :, m_], s4[:, :, :, a_], s4[:, :, :, b_], ALU.add)
            link(ins)
            link(dve.tensor_reduce(v(gsc), v(pr), AX.X, ALU.max))
            first_max(gsc, 4, key_g, geq, ing)
            inb = spread(v(ing).unsqueeze(3), [P, nt, 4, 4])
            link(dve.tensor_scalar(v(geq), v(ing), BIG, -BIG, ALU.mult, ALU.add))
            link(dve.tensor_tensor(g4(msk), s4, inb, ALU.mult))
            link(dve.tensor_tensor(g4(msk), g4(msk), spread(v(geq).unsqueeze(3), [P, nt, 4, 4]), ALU.add))
            first_max(msk, NE, key_e, ta, oh1)
            link(dve.tensor_scalar(v(tb), v(oh1), -BIG, None, ALU.mult))
            link(dve.tensor_tensor(v(msk), v(msk), v(tb), ALU.add))
            first_max(msk, NE, key_e, ta, oh2)
            dve.tensor_tensor(v(asg), v(oh1), v(oh2), ALU.add).then_inc(rt_asg[i], 1)
            for s, oh in enumerate((oh1, oh2)):
                link(dve.tensor_tensor(v(ta), v(oh), v(aff), ALU.mult))
                link(dve.tensor_reduce(w12[:, s, t0:], v(ta), AX.X, ALU.add))
            link(dve.tensor_tensor(v(wsum), w12[:, 0, t0:], w12[:, 1, t0:], ALU.add))
            link(dve.reciprocal(v(wsum), v(wsum)))
            for s in range(2):
                link(dve.tensor_tensor(gates[:, s, t0:], w12[:, s, t0:], v(wsum), ALU.mult))

        def places(i):
            t0, nt = tiles[i][0], len(tiles[i])
            v = lambda t_: t_[:, t0:]
            key = (i, "rank")
            wait_tile(dve, key)
            dve.tensor_copy(rank[:, t0:5, :].rearrange("p t e -> p (t e)"), bank(key)[:, NE * t0:5 * NE]).then_inc(free_dve, 1)
            wait_emptied(dve, key)
            count = rank[:, 4, :]
            link(dve.tensor_reduce(most_f[:, :], count, AX.X, ALU.max))
            link(dve.tensor_copy(cum[:, 0, :], count))
            for m_, sh in enumerate((1, 2, 4, 8)):
                a_, b_ = cum[:, m_ % 2, :], cum[:, (m_ + 1) % 2, :]
                link(dve.tensor_copy(b_[:, 0:sh], a_[:, 0:sh]))
                link(dve.tensor_tensor(b_[:, sh:NE], a_[:, sh:NE], a_[:, 0:NE - sh], ALU.add))
            link(dve.tensor_tensor(start_f[:, :], cum[:, 0, :], count, ALU.subtract))
            link(dve.tensor_tensor(v(pos), rank[:, t0:4, :], spread(start_f[:, :].unsqueeze(1), [P, nt, NE]), ALU.add))
            for s, oh in enumerate((oh1, oh2)):
                link(dve.tensor_tensor(v(ta), v(oh), v(pos), ALU.mult))
                link(dve.tensor_reduce(loc_f[:, s, t0:], v(ta), AX.X, ALU.add))
            dve.tensor_copy(loc[:, :, t0:], loc_f[:, :, t0:])
            dve.tensor_copy(starts[:, :], start_f[:, :])
            dve.tensor_copy(most[:, :], most_f[:, :]).then_inc(rt_loc[i], 1)

        for i in range(DEPTH):
            wait_tile(dve, ("vec", i))
            dve.tensor_copy(vec[i][:, :], bank(("vec", i))[:, 0:V_ROWS]).then_inc(free_dve, 1)
        wait_emptied(dve, ("vec", 1))
        dve.wait_ge(cond_sig, 1)
        dve.tensor_tensor(csil[:, :], csig[:, :], vec[0][:, V_C:V_C + 16], ALU.mult).then_inc(cond_sil, 1)
        dve.wait_ge(cond_hi, 1)
        cond4 = cond[:, :, AR - 4:AR].rearrange("p k (s u) -> p s k u", u=2)
        dve.tensor_tensor(cond4[:, :, :, 1], csil[:, :].rearrange("p (s k) -> p s k", s=2),
                          cond4[:, :, :, 0].bitcast(F32), ALU.subtract).then_inc(cond_ready, 1)
        for k in range(0, KT, 2):
            wait_tile(dve, ("x0", k))
            dve.tensor_copy(X[:, k, :], bank(("x0", k))).then_inc(free_dve, 1)
        dve.wait_ge(lam_in, 16)
        pairs = lamv[:, :, :].rearrange("p (a b) d -> p a b d", b=2)
        link(dve.tensor_tensor(lprod[:, :, :], pairs[:, :, 0, :], pairs[:, :, 1, :], ALU.mult))
        dve.tensor_reduce(lsum[:, :], lprod[:, :, :], AX.X, ALU.add).then_inc(lam_s, 1)
        for n in range(ADA_A):
            split_lo(dve, n)
        dve.wait_ge(lam_e, 1)
        link(dve.tensor_tensor(nlam[:, :], lexp[:, 1::2], lexp[:, 0::2], ALU.subtract))
        for i in range(DEPTH):
            link(dve.tensor_scalar(nlam[:, i:i + 1], nlam[:, i:i + 1], -lam_init[i], None, ALU.add))
        adaln(0, 0, 0, ADA_A // 4, mod_a)

        for i in range(DEPTH):
            n0 = mix0[i]
            for ch in range(3):
                split_lo(dve, n0 + ch)
            norm(f"n1_{i}", 0, True)
            at_chunk = {n: sc for sc, n in place_of[i].items()}
            for n in range(n0 + 3, exp0[i] + SPL):
                s, ch = at_chunk.get(n - SPL, (None, 0))
                if ch == 3:
                    empty_step(i, s)
                elif ch == 1 and s == ("WF", 0):
                    empty_step(i, s, 0)
                if n - 3 == place_of[i][(("GF", 1), 0)]:
                    dft_tokens(i)
                if n - SPL == place_of[i][(("WA", 0), 0)]:
                    attention(i)
                for s_, part in ADA_TURN.items():
                    if i == 0 and n - SPL == place_of[0][(s_, 0)]:
                        adaln(part, part - 1, 0 if part == 2 else ADA_A // 4, AG, mod_b)
                if n < exp0[i]:
                    split_lo(dve, n)
            norm(f"n2_{i}", col0[i], False)
            for t in tiles[i]:
                key = (i, "h2", t, 0)
                if t == tiles[i][0]:
                    route(i)
                wait_tile(dve, key)
                dve.tensor_copy(h2tok[:, t, 0:CW], bank(key)).then_inc(free_dve, 1)
            places(i)

            nb, cb = exp0[i], NE * i

            def tokens_lo(e):
                dve.wait_ge(e_xh, cb + e + 1)
                dve.tensor_tensor(xlo[:, :, :].rearrange("p k t -> p (k t)"), ps[:, 4:6, :].rearrange("p b n -> p (b n)"),
                                  xhi[:, :, :].rearrange("p k t -> p (k t)").bitcast(F32), ALU.subtract).then_inc(e_xl, 1)

            def splits(n, count, it=None):
                for ch in range(count):
                    split_lo(dve, n + ch, it, 24)

            def gated(e):
                dve.wait_ge(e_sig, cb + e + 1)
                dve.tensor_tensor(gu[:, :], ps[:, 0, :], sg[:, :], ALU.mult).then_inc(e_gu, 1)

            def hidden(n, e, it=None):
                dve.wait_ge(w_used, scaled(n, it, 24))
                dve.wait_ge(e_gu, cb + e + 1)
                dve.tensor_tensor(he[:, :], ps[:, 1, :], gu[:, :], ALU.mult).then_inc(e_he, 1)

            def hidden_lo(e):
                dve.wait_ge(e_hh, cb + e + 1)
                dve.tensor_tensor(helo[:, :, :].rearrange("p k t -> p (k t)"), ps[:, 6, :],
                                  hehi[:, :, :].rearrange("p k t -> p (k t)").bitcast(F32), ALU.subtract).then_inc(e_hl, 1)

            def result(n, e, j, it=None):
                dve.wait_ge(w_used, scaled(n, it, 24))
                dve.wait_ge(y_free[i], e + 1)
                dve.tensor_copy(ytile[:, j, CW:D], ps[:, 3, :]).then_inc(e_yd, 1)

            splits(nb, 4)
            tokens_lo(0)
            splits(nb + 4, 8)
            gated(0)
            splits(nb + 12, 4)
            hidden(nb + 8, 0)
            tokens_lo(1)
            with dve.Fori(0, NE // 2 - 1) as it:
                for j in range(2):
                    n = nb + 16 + 12 * j
                    splits(n, 4, it)
                    gated(2 * it + 1 + j)
                    hidden_lo(2 * it + j)
                    splits(n + 4, 4, it)
                    hidden(n, 2 * it + 1 + j, it)
                    tokens_lo(2 * it + 2 + j)
                    splits(n + 8, 3, it)
                    result(n + 4, 2 * it + j, j, it)
                    splits(n + 11, 1, it)
            n = nb + NE * EXP_CHUNKS - 8
            splits(n, 4)
            gated(NE - 1)
            hidden_lo(NE - 2)
            splits(n + 4, 4)
            hidden(n, NE - 1)
            result(n + 4, NE - 2, 0)
            hidden_lo(NE - 1)
            result(n + 8, NE - 1, 1)

            over = dve.value_load(most[0:1, 0:1], min_val=0, max_val=T)
            with dve.If(over > P):
                with dve.Fori(0, NE * len(tiles[i])) as r:
                    dve.wait_ge(f_pe[i], r * 4 + 1)
                    dve.tensor_copy(xT32[:, :, :].rearrange("p k t -> p (k t)"),
                                    ps[:, 4:6, :].rearrange("p b n -> p (b n)")).then_inc(f_dve[i], 1)
                    dve.wait_ge(f_act[i], r + 1)
                    dve.tensor_tensor(gu[:, :], ps[:, 0, :], sg[:, :], ALU.mult).then_inc(f_dve[i], 1)
                    dve.wait_ge(f_dve[i], r * 5 + 2)
                    dve.tensor_tensor(he[:, :], ps[:, 1, :], gu[:, :], ALU.mult).then_inc(f_dve[i], 1)
                    dve.wait_ge(f_pe[i], r * 4 + 3)
                    dve.tensor_copy(hT32[:, :, :].rearrange("p k t -> p (k t)"), ps[:, 6, :]).then_inc(f_dve[i], 1)
                    dve.wait_ge(f_pe[i], r * 4 + 4)
                    dve.tensor_copy(ytile[:, 0, :], ps[:, 2:4, :].rearrange("p b n -> p (b n)")).then_inc(f_dve[i], 1)

            dve.wait_ge(y_in[i], 32 * len(tiles[i]))
            for t in tiles[i]:
                link(dve.tensor_scalar(y1[:, t, :], y1[:, t, :], gates[:, 0, t:t + 1], None, ALU.mult))
                stt(y2[:, t, :], y2[:, t, :], gates[:, 1, t:t + 1], y1[:, t, :], ALU.mult, ALU.add).then_inc(y_sum[i], 1)
            parts = [p for p in streams if p[0] >= col0[i]]
            for k in range(KT):
                key = (i, "yT", k)
                wait_tile(dve, key)
                for a_, b_, cd in parts:
                    m = stt(X[:, k, a_:b_], bank(key)[:, a_:b_], mod[i][:, 40 + k, cd:cd + 1], X[:, k, a_:b_],
                            ALU.mult, ALU.add)
                m.then_inc(free_dve, 1)
        norm("nf", SEQ, False)
        for t in range(2):
            wait_tile(dve, ("out", t, 0))
            dve.tensor_copy(outt[:, t, 0:CW], bank(("out", t, 0))).then_inc(out_ready, 1)

    es.close()


_INS = ["x", "c", "ctx", "c_ctx", "w_ada", "b_ada", "g_norm1", "w_in", "lam_qk", "g_subln", "w_attn_out",
        "w_four_out", "w_gate", "b_gate", "w_out", "g_norm2", "w_router", "b_router", "w_e_gate", "w_e_up",
        "w_e_down", "g_final"]


def kernel(**inputs):
    import concourse.bacc as bacc
    from concourse.bass_utils import run_bass_kernel_spmd

    nc = bacc.Bacc("TRN2", target_bir_lowering=False, num_devices=1)
    arrays, args = {}, []
    for name in _INS:
        a = np.ascontiguousarray(inputs[name])
        arrays[f"in_{name}"] = a
        args.append(nc.dram_tensor(f"in_{name}", a.shape, mybir.dt.from_np(a.dtype), kind="ExternalInput").ap())
    arrays["in_consts"] = constants()
    args.append(nc.dram_tensor("in_consts", (P, C_COLS), F32, kind="ExternalInput").ap())
    o = nc.dram_tensor("out_x", (1, SEQ, D), F32, kind="ExternalOutput").ap()
    build(nc, *args, o)
    r = run_bass_kernel_spmd(nc, [arrays], core_ids=[0])
    return r.results[0]["out_x"]
```

```python
import math
from contextlib import ExitStack

import numpy as np
import concourse.bass as bass
from concourse import mybir

F32 = mybir.dt.float32
F32R = mybir.dt.float32r
I32 = mybir.dt.int32
U32 = mybir.dt.uint32
ACT = mybir.ActivationFunctionType
ALU = mybir.AluOpType
AX = mybir.AxisListType

P = 128
D = 1024
KT = D // P
T = 512
SEQ = 256
DEPTH = 2
HEADS = 8
HD = 64
FW = D // 2
FG = FW // P
NE = 16
DE = D // 2
KE = DE // P
EPS = 1e-6
ATT_SCALE = HD ** -0.5
BIG = 3.0e38

CK = 2
CW = 512
RAW = 8
SPL = 4
AG = 6 * D // CW
AR = 4 * AG
CPAD = 2 * AR - 4
BANKS = 7
EXP_CHUNKS = 12
CAP = (128, 80)

V_BADA, V_G1, V_G2, V_BG, V_SUB, V_GF, V_C = 0, 48, 56, 64, 80, 81, 89
V_ROWS = 105

C_ID, C_ONE, C_TRI = 0, 128, 256
C_RC, C_RS = 384, 640
C_CD = 896
C_CL, C_SL = 1152, 1664
C_KG, C_KE = 2176, 2180
C_IOTA, C_TOK = 2196, 2324
C_COLS = 2332


def constants():
    t = np.zeros((P, C_COLS), np.float64)
    p = np.arange(P)
    t[:, C_ID:C_ID + P] = np.eye(P)
    t[:, C_ONE:C_ONE + P] = 1.0
    t[:, C_TRI:C_TRI + P] = p[:, None] < p[None, :]
    tok = np.arange(SEQ)
    d = p % HD
    axis, half, j = d // 32, (d % 32) // 16, d % 16
    inv = 10000.0 ** (-j / 16.0)
    pos = np.where(axis[:, None] == 0, tok[None, :] // 64, tok[None, :] % 64)
    ang = pos * inv[:, None]
    t[:, C_RC:C_RC + SEQ] = np.cos(ang)
    t[:, C_RS:C_RS + SEQ] = np.sin(ang) * np.where(half == 0, -1.0, 1.0)[:, None]
    a = 2 * np.pi * np.outer(p, p) / P
    t[:, C_CD:C_CD + P] = np.cos(a) / np.sqrt(P)
    t[:, C_CD + P:C_CD + 2 * P] = np.sin(a) / np.sqrt(P)
    for k in range(2):
        b = 2 * np.pi * np.outer(k * P + p, tok) / SEQ
        t[:, C_CL + k * SEQ:C_CL + (k + 1) * SEQ] = np.cos(b) / np.sqrt(SEQ)
        t[:, C_SL + k * SEQ:C_SL + (k + 1) * SEQ] = -np.sin(b) / np.sqrt(SEQ)
    t[:, C_KG:C_KG + 4] = 4 - np.arange(4)
    t[:, C_KE:C_KE + NE] = NE - np.arange(NE)
    t[:, C_IOTA:C_IOTA + P] = p[None, :]
    for k in range(4):
        t[:, C_TOK + 2 * k:C_TOK + 2 * k + 2] = (k * P + p)[:, None]
    return t.astype(np.float32)


def steps_of(layer):
    return ([("F", 0), ("GF", 0), ("GF", 1), ("WF", 0)] + [("QK", g) for g in range(4)]
            + [("V", 0), ("V", 1), ("GA", 0), ("GA", 1), ("WA", 0), ("WA", 1), ("WO", 0), ("WO", 1)])


def stream_of(layer):
    ada = [(("ADA", 0, g), ch) for g in range(4, 12) for ch in range(4)]
    ada += [(("ADA", 1, g), ch) for g in range(12) for ch in range(4)]
    out = []
    for n, s in enumerate(steps_of(layer)):
        for ch in range(4):
            out.append((s, ch))
            if layer == 0:
                take = 1 if n % 3 == 0 else 2
                out += ada[:take]
                ada = ada[take:]
    assert layer or not ada
    return out


def build(nc, x, c, ctx_tok, c_ctx, w_ada, b_ada, g_norm1, w_in, lam_qk, g_subln, w_attn_out,
          w_four_out, w_gate, b_gate, w_out, g_norm2, w_router, b_router, w_e_gate, w_e_up,
          w_e_down, g_final, consts, out):
    es = ExitStack()

    base = -(-nc.sbuf_base // 64) * 64
    at = [base]

    def place(nbytes):
        o = at[0]
        at[0] += -(-nbytes // 32) * 32
        assert at[0] <= nc.sbuf_usable_end, (at[0], nc.sbuf_usable_end)
        return o

    def view(name, shape, dt, offset):
        return nc.alloc_sbuf_tensor_at(name, shape, dt, offset=offset)

    KB = 1024
    o_raw, o_hi, o_lo = place(RAW * 4 * KB), place(SPL * 4 * KB), place(SPL * 4 * KB)
    raw = view("w_raw", [P, RAW, CK, CW], F32, o_raw)
    whi4 = view("w_hi", [P, SPL, CK, CW], F32R, o_hi)
    wlo4 = view("w_lo", [P, SPL, CK, CW], F32R, o_lo)
    cst = view("cst", [P, C_COLS], F32, place(C_COLS * 4))
    rX, rH, rQ, rV, rG = place(16 * KB), place(32 * KB), place(32 * KB), place(16 * KB), place(32 * KB)
    X = view("x_feat", [P, KT, T], F32, rX)
    E = view("att_e", [P, 2, 2, T], F32, rX)
    A = view("att_a", [P, 2, T], F32, rX + 8 * KB)
    AT = view("att_at", [P, 2, T], F32, rX + 12 * KB)
    Hhi = view("h_hi", [P, KT, T], F32R, rH)
    Hlo = view("h_lo", [P, KT, T], F32R, rH + 16 * KB)
    O = view("o_tok", [P, 4, HEADS, P], F32, rH)
    whi8 = view("w_hi_more", [P, SPL, CK, CW], F32R, rH)
    wlo8 = view("w_lo_more", [P, SPL, CK, CW], F32R, rH + 16 * KB)
    h2T = view("h2_feat", [P, KT, T], F32, rH)
    h2tok = view("h2_tok", [P, 4, D], F32, rH + 16 * KB)
    QK = view("qk", [P, 2 * HEADS, T], F32, rQ)
    Zhi = view("z_hi", [P, FG, T], F32R, rQ)
    Zlo = view("z_lo", [P, FG, T], F32R, rQ + 8 * KB)
    OThi = view("ot_hi", [P, KT, T], F32R, rQ)
    OTlo = view("ot_lo", [P, KT, T], F32R, rQ + 16 * KB)
    sq = view("sq", [P, 2, T], F32, rQ)
    std = view("std", [P, T], F32, rQ + 4 * KB)
    rinv = view("rinv", [P, T], F32, rQ + 6 * KB)
    xn = view("xn", [P, 2, T], F32, rQ + 8 * KB)
    hf = view("hf", [P, 2, T], F32, rQ + 12 * KB)
    xg = view("xg", [P, 2, D], F32, rQ)
    xhi = view("xg_hi", [P, KT, P], F32R, rQ + 8 * KB)
    xlo = view("xg_lo", [P, KT, P], F32R, rQ + 12 * KB)
    ytile = view("ytile", [P, 2, D], F32, rQ + 16 * KB)
    zrow = view("zrow", [P, D], F32, rQ + 28 * KB)
    pick = view("pick", [P, 4, NE, P], F32R, rG)
    outt = view("outt", [P, 2, D], F32, rG)
    V = view("v_tok", [P, 4, D], F32, rV)
    FT = view("f_feat", [P, FG, T], F32, rV)
    osq = view("o_sq", [P, 4, P], F32, rH + 16 * KB)
    ot32 = view("ot32", [P, 2, T], F32, rV)
    sg = view("sg", [P, DE], F32, rV)
    gu = view("gu", [P, DE], F32, rV + 2 * KB)
    he = view("he", [P, DE], F32, rV + 4 * KB)
    hehi = view("he_hi", [P, KE, P], F32R, rV + 6 * KB)
    helo = view("he_lo", [P, KE, P], F32R, rV + 8 * KB)
    hT32 = view("he32", [P, KE, P], F32, rV + 10 * KB)
    G = view("g_four", [P, KT, T], F32, rG)
    GA = view("g_attn", [P, KT, T], F32, rG + 16 * KB)
    Y = view("dft_y", [P, 2, FG, 2, 2 * P], F32, rG + 16 * KB)
    rt = view("rope_t", [P, 2, SEQ], F32, rG + 16 * KB)
    tok0 = view("tok0", [P, 4, D], F32, rG)
    y1 = view("y1", [P, 4, D], F32, rG)
    token_major = view("token_major", [P, 4, D], F32, rH)
    zsq = view("z_sq", [P, 2, D], F32, rH + 16 * KB)
    y2 = view("y2", [P, 4, D], F32, rG + 16 * KB)
    ada_row = [view("ada_row_h", [P, CW], F32, rH + 30 * KB), view("ada_row_v", [P, CW], F32, rV + 8 * KB)]
    ada_row.append(ada_row[0])
    xT32 = view("xT32", [P, KT, P], F32, rG)

    def small(name, shape, dt=F32):
        return view(name, shape, dt, place(int(np.prod(shape[1:])) * 4))

    vrow = view("vrow", [P, P], F32, rV)
    vrow1 = view("vrow1", [P, P], F32, rV + KB)
    vec = [small(f"vec{i}", [P, V_ROWS]) for i in range(DEPTH)]
    mod = [small(f"mod{i}", [P, 48, 2]) for i in range(DEPTH)]
    sc1 = [small(f"sc1_{i}", [P, KT, 2]) for i in range(DEPTH)]
    sc2 = [small(f"sc2_{i}", [P, KT, 2]) for i in range(DEPTH)]
    csig = small("csig", [P, 16])
    csil = small("csil", [P, 16])
    cond = small("cond", [P, KT, CPAD], F32R)
    wr = small("wr", [P, KT, NE])
    brb = small("brb", [P, NE])
    epst = small("epst", [P, 1])
    warmed = small("warmed", [P, 1])
    lamv = view("lamv", [P, 4 * DEPTH, HD], F32, rV + 2 * KB)
    lprod = view("lprod", [P, 2 * DEPTH, HD], F32, rV + 4 * KB)
    lsum = small("lsum", [P, 2 * DEPTH])
    lexp = small("lexp", [P, 2 * DEPTH])
    nlam = small("nlam", [P, DEPTH])
    gsub = small("gsub", [P, 1])
    amax = small("amax", [P, 2, 2])
    aneg = small("aneg", [P, 2, 2])
    asum = small("asum", [P, 2, 2])
    arec = small("arec", [P, 4, 2])
    arec1 = small("arec1", [P, 2])
    zss = small("zss", [P, 3, 2])
    oss = small("oss", [P, 4 * HEADS])
    ostd = small("ostd", [P, 4 * HEADS])
    orin = small("orin", [P, 4 * HEADS])
    r_at = [rV]

    def passing(name, shape, dt=F32):
        o = r_at[0]
        r_at[0] += -(-int(np.prod(shape[1:])) * 4 // 32) * 32
        return view(name, shape, dt, o)

    affT = passing("affT", [P, T])
    aff = passing("aff", [P, 4, NE])
    sel = passing("sel", [P, 4, NE])
    pr = passing("pr", [P, 4, 4, 6])
    gsc = passing("gsc", [P, 4, 4])
    geq = passing("geq", [P, 4, 4])
    ing = passing("ing", [P, 4, 4])
    msk = passing("msk", [P, 4, NE])
    ta = passing("ta", [P, 4, NE])
    tb = passing("tb", [P, 4, NE])
    tm = passing("tm", [P, 4])
    oh1 = passing("oh1", [P, 4, NE])
    oh2 = passing("oh2", [P, 4, NE])
    asg = passing("asg", [P, 5, NE])
    w12 = passing("w12", [P, 2, 4])
    wsum = passing("wsum", [P, 4])
    gates = small("gates", [P, 2, 4])
    rank = passing("rank", [P, 5, NE])
    cum = passing("cum", [P, 2, NE])
    off = passing("off", [P, 4, NE])
    mrank = passing("mrank", [P, 4, NE])
    start_f = passing("start_f", [P, NE])
    pos = passing("pos", [P, 4, NE])
    loc_f = passing("loc_f", [P, 2, 4])
    loc = small("loc", [P, 2, 4], U32)
    starts = small("starts", [P, NE], I32)
    tokr = small("tokr", [P, 4, 2], F32R)
    ids = small("ids", [P, NE], U32)
    idn = small("idn", [P, 2], U32)
    most_f = passing("most_f", [P, 1])
    most = small("most", [P, 1], I32)

    ps = es.enter_context(nc.psum_tensor("ps", [P, 8, 512], F32))

    ROWS = 2 * T + 4 * P
    xkeep = nc.dram_tensor("xkeep", (P, KT * T), F32).ap()
    hbuf = nc.dram_tensor("hbuf", (T, D), F32).ap()
    hsort = nc.dram_tensor("hsort", (ROWS, D), F32).ap()
    ybuf = nc.dram_tensor("ybuf", (ROWS, D), F32).ap()

    def sem(name):
        return es.enter_context(nc.semaphore(name))

    def per_layer(*names):
        return [[sem(f"{name}_{i}") for i in range(DEPTH)] for name in names]

    raw_in = [sem(f"raw_in{i}") for i in range(RAW)]
    hi_ready, lo_ready, w_used = sem("hi_ready"), sem("lo_ready"), sem("w_used")
    cst_in, cst2_in, tok_in, small_in = sem("cst_in"), sem("cst2_in"), sem("tok_in"), sem("small_in")
    vec_in = [sem("vec0_in"), sem("vec1_in")]
    filled, pad_out = sem("filled"), sem("pad_out")
    tile_done = sem("tile_done")
    free_act, free_dve = sem("free_act"), sem("free_dve")
    dve_chain = sem("dve_chain")
    cond_sig, cond_sil, cond_hi, cond_ready = sem("cond_sig"), sem("cond_sil"), sem("cond_hi"), sem("cond_ready")
    ada_rows = sem("ada_rows")
    mod_a, mod_b = sem("mod_a"), sem("mod_b")
    n_sq, n_squ, n_xn, n_hf, n_hi, n_lo = (sem(f"n_{k}") for k in ("sq", "squ", "xn", "hf", "hi", "lo"))
    norms = {"n1_0": 0, "n2_0": 1, "n1_1": 2, "n2_1": 3}
    x_kept, x_back, roped, z_hi = per_layer("x_kept", "x_back", "roped", "z_hi")
    lam_in, lam_s, lam_e = sem("lam_in"), sem("lam_s"), sem("lam_e")
    a_s, a_neg, a_exp, a_comb, a_tr, a_trc, a_pv, a_oc = (
        sem(f"a_{k}") for k in ("s", "neg", "exp", "comb", "tr", "trc", "pv", "oc"))
    o_ss, o_std, o_nrm, ot_h, ot_l, m_f, m_h, m_l = per_layer(
        "o_ss", "o_std", "o_nrm", "ot_h", "ot_l", "m_f", "m_h", "m_l")
    rt_asg, rt_loc, h_out, e_out, y_free, f_sort = per_layer("rt_asg", "rt_loc", "h_out", "e_out", "y_free", "f_sort")
    picked, e_ids, fetching = sem("picked"), sem("e_ids"), sem("fetching")
    e_in = [sem("e_in_a"), sem("e_in_b")]
    e_xt, e_xh, e_xl, e_sig, e_gu, e_he, e_ht, e_hh, e_hl, e_ya, e_yd = (
        sem(f"e_{k}") for k in ("xt", "xh", "xl", "sig", "gu", "he", "ht", "hh", "hl", "ya", "yd"))
    f_go, f_in, f_dn, f_out, f_pe, f_act, f_dve = per_layer("f_go", "f_in", "f_dn", "f_out", "f_pe", "f_act", "f_dve")
    y_in = [sem(f"y_in{t}") for t in range(4)]
    y_sum = [sem(f"y_sum_{i}") for i in range(DEPTH)]
    z_first, z_sum, z_ss, z_std, out_ready, out_done = (
        sem(k) for k in ("z_first", "z_sum", "z_ss", "z_std", "out_ready", "out_done"))

    ahead = [1, 4]
    cs = lambda a, n: cst[:, a:a + n]
    ident, ones, tri = cs(C_ID, P), cs(C_ONE, P), cs(C_TRI, P)

    col0 = [0, SEQ]
    tiles = [[0, 1, 2, 3], [2, 3]]
    items = [[(h, q) for h in range(HEADS) for q in tiles[i]] for i in range(DEPTH)]
    first_item = [0, len(items[0])]
    keys = lambda q: SEQ if q < 2 else T

    def w_chunk(w, k0, n0):
        return w[k0 * P:(k0 + CK) * P, n0:n0 + CW].rearrange("(k p) n -> p k n", p=P)

    def chunk_of(i, s, ch):
        kind = s[0]
        if kind == "ADA":
            return w_chunk(w_ada[s[1]], CK * ch, CW * s[2])
        if kind == "WF":
            return w_chunk(w_four_out[i], CK * (ch % 2), CW * (ch // 2))
        w, n0 = {"F": (w_in[i], 3 * D), "GF": (w_gate[i], D), "QK": (w_in[i], 0), "V": (w_in[i], 2 * D),
                 "GA": (w_gate[i], 0), "WA": (w_attn_out[i], 0), "WO": (w_out[i], 0)}[kind]
        return w_chunk(w, CK * ch, n0 + CW * s[1])

    ADA_A = 16
    mix0, exp0 = [], []
    n = ADA_A
    for i in range(DEPTH):
        mix0.append(n)
        n += len(stream_of(i))
        exp0.append(n)
        n += NE * EXP_CHUNKS
    assert all(v % RAW == 0 for v in exp0)

    place_of = [{sc: mix0[i] + n for n, sc in enumerate(stream_of(i))} for i in range(DEPTH)]

    ADA_TURN = {("V", 0): 1, ("WA", 1): 2}
    ada_last = [ADA_A - 1] + [place_of[0][(("ADA", i, AG - 1), 3)] for i in range(DEPTH)]
    assert all(ada_last[p_] < place_of[0][(s, 0)] for s, p_ in ADA_TURN.items())

    plan, owner = {}, []

    def add_tile(key, by):
        plan[key] = len(owner)
        owner.append(by)

    dft = [[(s, g) for s in range(i, 2) for g in range(FG)] for i in range(DEPTH)]
    for k in range(KT):
        add_tile(("x0", k), "act" if k % 2 else "dve")
    add_tile(("vec", 0), "dve")
    for i in range(DEPTH):
        add_tile((i, "n1"), "act")
        if i == 0:
            add_tile(("ada", 0), "dve")
            add_tile(("vec", 1), "dve")
        for s in steps_of(i):
            if i == 0 and s in ADA_TURN:
                add_tile(("ada", ADA_TURN[s]), "dve")
            if s == ("GF", 0):
                for sg_ in dft[i]:
                    add_tile((i, "Y") + sg_, "act")
            if s == ("GF", 1):
                for sg_ in dft[i]:
                    add_tile((i, "Z") + sg_, "dve")
            if s == ("WA", 0):
                for h in range(HEADS):
                    add_tile((i, "OT", h), "act")
            if s == ("WO", 1):
                add_tile((i, "n2"), "act")
            for t in range(8 if s[0] == "WF" else 4):
                add_tile((i, s[0], s[1], t), "dve" if s[0] in ("WF", "WA", "WO") else "act")
        add_tile((i, "log"), "act")
        add_tile((i, "aff"), "dve")
        for t in tiles[i]:
            for half in range(2):
                add_tile((i, "h2", t, half), "act")
        add_tile((i, "rank"), "dve")
        for g in range(4):
            add_tile((i, "ids", g), "dve")
        for k in range(KT):
            if i == 0:
                add_tile((i, "yT", k), "dve")
            else:
                add_tile(("last", k), "act" if k % 2 else "dve")

    finish = {key: plan[(key[0], "WO", 1, 3)] + 0.5 if key[1:] == ("n2",) else t for key, t in plan.items()}
    done_at, signals = {}, 0
    for key in sorted(plan, key=finish.get):
        i = key[0]
        if key[1:] and key[1] in ("F", "GF", "WF", "QK", "V", "GA", "WA", "WO") and key[3] % 4 == 3:
            last = 3 if key[1] != "WF" else 1 + 2 * (key[3] // 4)
            done_at[key] = (w_used, place_of[i][(key[1:3], last)] + 1)
        else:
            signals += 1
            done_at[key] = (tile_done, signals)

    def bank(key):
        return ps[:, plan[key] % BANKS, :]

    def emptied(t):
        by = owner[t]
        return (free_act if by == "act" else free_dve), sum(1 for o in owner[:t + 1] if o == by)

    def take_tile(eng, key):
        t = plan[key]
        if t >= BANKS:
            s, v = emptied(t - BANKS)
            eng.wait_ge(s, v)

    def wait_tile(eng, key):
        eng.wait_ge(*done_at[key])

    def wait_emptied(eng, key):
        eng.wait_ge(*emptied(plan[key]))

    def wait_all_emptied(eng, key):
        for by, s_ in (("act", free_act), ("dve", free_dve)):
            eng.wait_ge(s_, sum(1 for o in owner[:plan[key] + 1] if o == by))

    def scaled(n, it, per):
        return n if it is None else n + it * per

    def raw_value(n, it, per):
        v = 16 * (n // RAW + 1)
        return v if it is None else v + it * (16 * (per // RAW))

    def load(sp, n, src, it=None, per=0):
        if it is not None or n >= RAW:
            sp.wait_ge(lo_ready, scaled(n - RAW + 1, it, per))
        sp.dma_start(raw[:, n % RAW, :, :], src).then_inc(raw_in[n % RAW], 16)

    def in_experts(n):
        return any(exp0[i] <= n < exp0[i] + NE * EXP_CHUNKS for i in range(DEPTH))

    def ring(n):
        return 2 * SPL if in_experts(n) else SPL

    def whi(n):
        r = n % ring(n)
        return (whi4 if r < SPL else whi8)[:, r % SPL, :, :]

    def wlo(n):
        r = n % ring(n)
        return (wlo4 if r < SPL else wlo8)[:, r % SPL, :, :]

    def split_hi(act, n, it=None, per=0):
        act.wait_ge(raw_in[n % RAW], raw_value(n, it, per))
        if it is not None or n >= SPL:
            act.wait_ge(w_used, scaled(n - ring(n) + 1, it, per))
        act.activation(whi(n), raw[:, n % RAW, :, :], ACT.Copy).then_inc(hi_ready, 1)

    def split_lo(dve, n, it=None, per=0):
        dve.wait_ge(hi_ready, scaled(n + 1, it, per))
        dve.tensor_tensor(wlo(n), raw[:, n % RAW, :, :], whi(n).bitcast(F32), ALU.subtract).then_inc(lo_ready, 1)

    def product(pe, acc, sh, sl, mh, ml, first, last):
        pe.matmul(acc, sh, mh, start=first, stop=False, skip_group_check=True)
        pe.matmul(acc, sh, ml, start=False, stop=False, skip_group_check=True)
        return pe.matmul(acc, sl, mh, start=False, stop=last, skip_group_check=True)

    def turned(t, cap):
        return t[:, :, :].rearrange("p (b k) t -> p b k t", k=4)[:, :, :, 0:cap]

    def turned_ps(b0, nb, cap):
        return ps[:, b0:b0 + nb, 0:4 * cap].rearrange("p b (k t) -> p b k t", k=4)

    def spread(ap, shape):
        return ap.to_broadcast(shape)

    def load_vectors(eng, i):
        rows = [(V_C, c[0], 8), (V_C + 8, c_ctx, 8), (V_BADA, b_ada[i], 48), (V_G1, g_norm1[i], 8),
                (V_G2, g_norm2[i], 8), (V_BG, b_gate[i], 16), (V_SUB, g_subln[i], 1), (V_GF, g_final, 8)]
        for r, src, k in rows:
            eng.dma_start((vrow, vrow1)[i][r:r + k, :], src.rearrange("(k p) -> k p", p=P)).then_inc(vec_in[i], 16)

    block = es.enter_context(nc.Block())

    @block.sync
    def _(sp):
        sp.dma_start(cst[:, 0:C_TRI], consts[:, 0:C_TRI]).then_inc(cst_in, 16)
        for s_, src in enumerate((ctx_tok, x)):
            sp.dma_start(tok0[:, 2 * s_:2 * s_ + 2, :], src[0].rearrange("(t p) n -> p t n", p=P)).then_inc(tok_in, 16)
        load_vectors(sp, 0)
        for n in range(ADA_A):
            load(sp, n, w_chunk(w_ada[0], CK * (n % 4), CW * (n // 4)))
        sp.dma_start(cst[:, C_TRI:], consts[:, C_TRI:]).then_inc(cst2_in, 16)
        for i in range(DEPTH):
            if i:
                sp.wait_ge(y_in[3], 32 * i)
            for n, (s, ch) in enumerate(stream_of(i)):
                load(sp, mix0[i] + n, chunk_of(i, s, ch))
            nb = exp0[i]

            def weights(n, w, e, it=None):
                for ch in range(4):
                    k, cc = (ch % 2, ch // 2) if w is w_e_down else (ch, 0)
                    load(sp, n + ch, w_chunk(w[i, e], CK * k, CW * cc), it, 24)

            for e in range(2):
                weights(nb + 8 * e, w_e_gate, e)
                weights(nb + 8 * e + 4, w_e_up, e)
            with sp.Fori(0, NE // 2 - 1) as it:
                for j in range(2):
                    weights(nb + 16 + 12 * j, w_e_down, 2 * it + j, it)
                    weights(nb + 20 + 12 * j, w_e_gate, 2 * it + j + 2, it)
                    weights(nb + 24 + 12 * j, w_e_up, 2 * it + j + 2, it)
            for e in (NE - 2, NE - 1):
                weights(nb + EXP_CHUNKS * NE - 4 * (NE - e), w_e_down, e)
            sp.wait_ge(rt_loc[i], 1)
            over = sp.value_load(most[0:1, 0:1], min_val=0, max_val=T)
            nt = len(tiles[i])
            with sp.If(over > CAP[i]):
                sp.wait_ge(lo_ready, exp0[i] + NE * EXP_CHUNKS)
                with sp.Fori(0, NE) as e:
                    first = sp.value_load(starts[0:1, bass.ds(e, 1)], min_val=0, max_val=2 * T)
                    for r in range(nt):
                        k = e * nt + r
                        sp.wait_ge(f_go[i], k + 1)
                        sp.dma_start(xg[:, 0, :], hsort[bass.ds(first + r * P, P), :]).then_inc(f_in[i], 16)
                        for m, w in enumerate((w_e_gate, w_e_up)):
                            sp.dma_start(raw[:, 4 * m:4 * m + 4, :, :].rearrange("p s k n -> p (s k) n"),
                                         w[i, e].rearrange("(k p) n -> p k n", p=P)).then_inc(f_in[i], 16)
                        sp.wait_ge(f_pe[i], k * 4 + 2)
                        sp.dma_start(raw[:, 0:4, :, :].rearrange("p s k n -> p (s k n)").rearrange("p (k n) -> p k n", n=D),
                                     w_e_down[i, e].rearrange("(k p) n -> p k n", p=P)).then_inc(f_dn[i], 16)
                        sp.wait_ge(f_dve[i], k * 5 + 5)
                        sp.dma_start(ybuf[bass.ds(first + r * P, P), :], ytile[:, 0, :]).then_inc(f_out[i], 16)
                        sp.wait_ge(f_out[i], (k + 1) * 16)
                        sp.sem_inc(f_go[i], 1)

        for t in range(2):
            sp.wait_ge(out_ready, t + 1)
            sp.dma_start(out[0, t * P:(t + 1) * P, :], outt[:, t, :]).then_inc(out_done, 16)
        sp.wait_ge(out_done, 32)

    @block.gpsimd
    def _(pool):
        pool.memset(cond[:, :, :].bitcast(F32), 0.0).then_inc(filled, 1)
        pool.memset(epst[:, :], EPS).then_inc(filled, 1)
        pool.memset(zrow[:, :], 0.0).then_inc(filled, 1)
        load_vectors(pool, 1)
        pool.dma_start(lamv[:, :, :], lam_qk.rearrange("(a l) m d -> a (l m) d", a=1)
                       .to_broadcast([P, 4 * DEPTH, HD])).then_inc(lam_in, 16)
        pool.dma_start(wr[:, :, :], w_router.rearrange("(k p) n -> p k n", p=P)).then_inc(small_in, 16)
        pool.dma_start(brb[:, :], b_router.rearrange("(a n) -> a n", a=1).to_broadcast([P, NE])).then_inc(small_in, 16)
        pool.wait_ge(filled, 3)
        pool.wait_ge(n_lo, KT)
        for r in range(T // P, ROWS // P):
            pool.dma_start(hsort[r * P:(r + 1) * P, :], zrow[:, :]).then_inc(pad_out, 16)
        for i in range(DEPTH):
            wait_all_emptied(pool, (i, "n1"))
            pool.wait_ge(roped[i], 1)
            pool.dma_start(xkeep, X[:, :, :].rearrange("p k t -> p (k t)")).then_inc(x_kept[i], 16)
            pool.wait_ge(x_kept[i], 16)
            pool.wait_ge(a_oc, first_item[i] + len(items[i]))
            pool.dma_start(X[:, :, :].rearrange("p k t -> p (k t)"), xkeep).then_inc(x_back[i], 16)
            pool.wait_ge(h_out[i], 16 * len(tiles[i]))
            wait_emptied(pool, (i, "ids", 0))
            pool.sem_inc(y_free[i], 2)

            cap = CAP[i]

            def first_row(e):
                return pool.value_load(starts[0:1, bass.ds(e, 1)], min_val=0, max_val=2 * T)

            def fetch(e, j):
                pool.tensor_copy(idn[0:cap, j:j + 1], ids[0:cap, bass.ds(e, 1)]).then_inc(e_ids, 1)
                pool.wait_ge(e_ids, NE * i + e + 1)
                pool.sem_inc(fetching, 1)
                pool.indirect_dma_start(xg[0:cap, j, :], None, hbuf,
                                        bass.IndirectOffsetOnAxis(ap=idn[0:cap, j:j + 1], axis=0)).then_inc(e_in[j], 16)

            def store(e, j, first=False):
                pool.wait_ge(e_ya, NE * i + e + 1)
                pool.wait_ge(e_yd, NE * i + e + 1)
                if not first:
                    pool.wait_ge(e_out[i], e * 16)
                    pool.sem_inc(y_free[i], 1)
                pool.dma_start(ybuf[bass.ds(first_row(e), cap), :], ytile[0:cap, j, :]).then_inc(e_out[i], 16)

            def refetch(e, j):
                pool.wait_ge(e_xt, NE * i + e - 1)
                fetch(e, j)

            fetch(0, 0)
            fetch(1, 1)
            refetch(2, 0)
            refetch(3, 1)
            wait_emptied(pool, (i, "ids", 3))
            pool.wait_ge(rt_loc[i], 1)
            store(0, 0, first=True)
            with pool.Fori(0, NE // 2 - 2) as it:
                for j in range(2):
                    refetch(2 * it + 4 + j, j)
                    store(2 * it + 1 + j, 1 - j)
            for e in range(NE - 3, NE):
                store(e, e % 2)
            pool.wait_ge(e_out[i], NE * 16)
            over = pool.value_load(most[0:1, 0:1], min_val=0, max_val=T)
            with pool.If(over > CAP[i]):
                if i == 0:
                    pool.wait_ge(pad_out, 16 * (ROWS // P - T // P))
                for t in tiles[i]:
                    pool.dma_start(y1[:, t, :], hbuf[t * P:(t + 1) * P, :]).then_inc(f_sort[i], 16)
                pool.wait_ge(f_sort[i], 16 * len(tiles[i]))
                for s in range(2):
                    for t in tiles[i]:
                        pool.indirect_dma_start(hsort, bass.IndirectOffsetOnAxis(ap=loc[:, s, t:t + 1], axis=0),
                                                y1[:, t, :], None).then_inc(f_sort[i], 16)
                pool.wait_ge(f_sort[i], 48 * len(tiles[i]))
                pool.sem_inc(f_go[i], 1)
                pool.wait_ge(f_out[i], 16 * NE * len(tiles[i]))
            for t in tiles[i]:
                for s, dst in enumerate((y1, y2)):
                    pool.indirect_dma_start(dst[:, t, :], None, ybuf[0:2 * P * len(tiles[i]), :],
                                            bass.IndirectOffsetOnAxis(ap=loc[:, s, t:t + 1], axis=0)).then_inc(y_in[t], 16)

    @block.tensor
    def _(pe):
        def turn_vectors(i, src):
            take_tile(pe, ("vec", i))
            pe.wait_ge(vec_in[i], 16 * 8)
            pe.transpose(bank(("vec", i))[:, 0:V_ROWS], src[0:V_ROWS, :], ident[0:V_ROWS, 0:V_ROWS]).then_inc(tile_done, 1)

        pe.wait_ge(cst_in, 16)
        pe.wait_ge(tok_in, 32)
        for k in range(KT):
            take_tile(pe, ("x0", k))
            for t in range(4):
                m = pe.transpose(bank(("x0", k))[:, t * P:(t + 1) * P], tok0[:, t, k * P:(k + 1) * P], ident)
            m.then_inc(tile_done, 1)
        turn_vectors(0, vrow)

        def ada_chunk(n, g, ch, first, last):
            pe.wait_ge(lo_ready, n + 1)
            for k in range(CK):
                kt = CK * ch + k
                at_g = cond[:, kt, AR - 4 - 4 * g:2 * AR - 4 - 4 * g]
                pe.matmul(ps[0:AR, 7, :], at_g, whi(n)[:, k, :], start=first and k == 0, stop=False, skip_group_check=True)
                m = pe.matmul(ps[0:AR, 7, :], at_g, wlo(n)[:, k, :], start=False, stop=last and k == CK - 1,
                              skip_group_check=True)
            m.then_inc(w_used, 1)

        def ada_turn(part):
            take_tile(pe, ("ada", part))
            pe.wait_ge(ada_rows, part + 1)
            for ct in range(4):
                m = pe.transpose(bank(("ada", part))[:, ct * AR:(ct + 1) * AR], ada_row[part][0:AR, ct * P:(ct + 1) * P],
                                 ident[0:AR, 0:AR])
            m.then_inc(tile_done, 1)

        def norm_sum(name, key, c0, ks=range(KT)):
            o = KT * norms[name]
            if ks[0] == 0:
                take_tile(pe, key)
            for k in ks:
                pe.wait_ge(n_sq, o + k + 1)
                m = pe.matmul(bank(key)[:, c0:T], ones, sq[:, k % 2, c0:T], start=k == 0, stop=k == KT - 1)
                m.then_inc(n_squ if k < KT - 1 else tile_done, 1)

        def by_weights(n, ch, keys_, c0, moving, chunks):
            pe.wait_ge(lo_ready, n + 1)
            for k in range(CK):
                kt = CK * ch + k
                for ct in range(4):
                    if kt == 0:
                        take_tile(pe, keys_[ct])
                    wcol = slice(ct * P, (ct + 1) * P)
                    m = product(pe, bank(keys_[ct])[:, c0:T], whi(n)[:, k, wcol], wlo(n)[:, k, wcol],
                                moving[0][:, kt, c0:T], moving[1][:, kt, c0:T], kt == 0, kt == CK * chunks - 1)
                    if kt == CK * chunks - 1 and ct < 3:
                        m.then_inc(tile_done, 1)
            m.then_inc(w_used, 1)

        def by_tokens(n, ch, keys_):
            pe.wait_ge(lo_ready, n + 1)
            for k in range(CK):
                kt = CK * ch + k
                for t in range(4):
                    if kt == 0:
                        take_tile(pe, keys_[t])
                    tc = slice(t * P, (t + 1) * P)
                    m = product(pe, bank(keys_[t])[:, :], Hhi[:, kt, tc], Hlo[:, kt, tc], whi(n)[:, k, :], wlo(n)[:, k, :],
                                kt == 0, kt == KT - 1)
                    if kt == KT - 1 and t < 3:
                        m.then_inc(tile_done, 1)
            m.then_inc(w_used, 1)

        def dft_channels(i):
            for s, g in dft[i]:
                key = (i, "Y", s, g)
                take_tile(pe, key)
                wait_emptied(pe, (i, "F", 0, g))
                for t in range(2):
                    c0 = s * SEQ + t * P
                    m = pe.matmul(bank(key)[:, t * 2 * P:(t + 1) * 2 * P], FT[:, g, c0:c0 + P], cs(C_CD, 2 * P),
                                  start=True, stop=True, skip_group_check=True)
                m.then_inc(tile_done, 1)

        def dft_tokens(i):
            for s, g in dft[i]:
                key = (i, "Z", s, g)
                take_tile(pe, key)
                wait_emptied(pe, (i, "Y", s, g))
                for t in range(2):
                    pe.matmul(bank(key)[:, 0:SEQ], Y[:, s, g, t, 0:P], cs(C_CL + t * SEQ, SEQ), start=t == 0, stop=False)
                    m = pe.matmul(bank(key)[:, 0:SEQ], Y[:, s, g, t, P:2 * P], cs(C_SL + t * SEQ, SEQ), start=False,
                                  stop=t == 1)
                m.then_inc(tile_done, 1)

        def attention(i):
            wait_all_emptied(pe, (i, "GA", 1, 3))
            pe.wait_ge(roped[i], 2 * HEADS)
            pe.wait_ge(ada_rows, 3)
            its, f = items[i], first_item[i]
            for j in range(len(its) + 3):
                if j < len(its):
                    h, q = its[j]
                    if j >= 2:
                        pe.wait_ge(a_exp, 2 * (f + j - 1))
                    for m_ in range(2):
                        d = slice(m_ * HD, (m_ + 1) * HD)
                        m = pe.matmul(ps[:, 2 * (j % 2) + m_, 0:keys(q)], QK[d, h, q * P:(q + 1) * P],
                                      QK[d, HEADS + h, 0:keys(q)], start=True, stop=True)
                    m.then_inc(a_s, 1)
                t = j - 2
                if 0 <= t < len(its):
                    h, q = its[t]
                    pe.wait_ge(a_comb, f + t + 1)
                    if t >= 2:
                        pe.wait_ge(a_trc, f + t - 1)
                    for k in range(keys(q) // P):
                        m = pe.transpose(ps[:, 4 + t % 2, k * P:(k + 1) * P], A[:, t % 2, k * P:(k + 1) * P], ident)
                    m.then_inc(a_tr, 1)
                t = j - 3
                if t >= 0:
                    h, q = its[t]
                    pe.wait_ge(a_trc, f + t + 1)
                    if t >= 2:
                        pe.wait_ge(a_oc, f + t - 1)
                    nk = keys(q) // P
                    for k in range(nk):
                        m = pe.matmul(ps[:, 6 + t % 2, 0:P], AT[:, t % 2, k * P:(k + 1) * P],
                                      V[:, k, h * P:(h + 1) * P], start=k == 0, stop=k == nk - 1, skip_group_check=True)
                    m.then_inc(a_pv, 1)
            for h in range(HEADS):
                pe.wait_ge(o_nrm[i], h + 1)
                take_tile(pe, (i, "OT", h))
                for q in tiles[i]:
                    m = pe.transpose(bank((i, "OT", h))[:, q * P:(q + 1) * P], O[:, q, h, :], ident)
                m.then_inc(tile_done, 1)

        pe.wait_ge(filled, 3)
        for n in range(ADA_A):
            if n < KT:
                norm_sum("n1_0", (0, "n1"), 0, [n])
            if n == 0:
                pe.wait_ge(cond_ready, 1)
            ada_chunk(n, n // 4, n % 4, n == 0, n == ADA_A - 1)
        ada_turn(0)
        turn_vectors(1, vrow1)

        for i in range(DEPTH):
            c0 = col0[i]
            if i:
                norm_sum(f"n1_{i}", (i, "n1"), 0)
            else:
                pe.wait_ge(cst2_in, 16)
            for (s, ch), n in place_of[i].items():
                kind = s[0]
                if (s, ch) == (("GF", 0), 0):
                    dft_channels(i)
                if (s, ch) == (("GF", 1), 0):
                    dft_tokens(i)
                if (s, ch) == (("WO", 1), 3):
                    norm_sum(f"n2_{i}", (i, "n2"), c0, range(4))
                if i == 0 and s in ADA_TURN and ch == 0:
                    ada_turn(ADA_TURN[s])
                if kind == "ADA":
                    first = (s, ch) in ((("ADA", 0, ADA_A // 4), 0), (("ADA", 1, 0), 0))
                    if first:
                        pe.wait_ge(ada_rows, 1 + s[1])
                    ada_chunk(n, s[2], ch, first, n in ada_last)
                elif kind == "WF":
                    if ch == 0:
                        wait_emptied(pe, (i, "Z") + dft[i][-1])
                    by_weights(n, ch % 2, [(i, "WF", 0, 4 * (ch // 2) + t) for t in range(4)], c0, (Zhi, Zlo), 2)
                elif kind == "V":
                    by_tokens(n, ch, [(i, "V", s[1], t) for t in range(4)])
                elif kind == "WA":
                    if (s[1], ch) == (0, 0):
                        attention(i)
                    if s[1] == 0:
                        pe.wait_ge(ot_l[i], CK * (ch + 1))
                    by_weights(n, ch, [(i, "WA", s[1], t) for t in range(4)], c0, (OThi, OTlo), 4)
                elif kind == "WO":
                    if s[1] == 0:
                        pe.wait_ge(m_l[i], CK * (ch + 1))
                    by_weights(n, ch, [(i, "WO", s[1], t) for t in range(4)], c0, (Hhi, Hlo), 4)
                else:
                    if kind == "F":
                        pe.wait_ge(n_lo, KT * i + CK * (ch + 1))
                    by_weights(n, ch, [(i, kind, s[1], t) for t in range(4)], 0 if kind == "QK" and s[1] >= 2 else c0,
                               (Hhi, Hlo), 4)

            norm_sum(f"n2_{i}", (i, "n2"), c0, range(4, KT))
            pe.wait_ge(small_in, 32)
            key = (i, "log")
            take_tile(pe, key)
            for k in range(KT):
                pe.wait_ge(n_hf, KT * (2 * i + 1) + k + 1)
                m = pe.matmul(bank(key)[0:NE, c0:T], wr[:, k, :], h2T[:, k, c0:T], start=k == 0, stop=k == KT - 1)
            m.then_inc(tile_done, 1)
            wait_emptied(pe, key)
            key = (i, "aff")
            take_tile(pe, key)
            for t in tiles[i]:
                m = pe.transpose(bank(key)[:, NE * t:NE * t + NE], affT[0:NE, t * P:(t + 1) * P], ident[0:NE, 0:NE])
            m.then_inc(tile_done, 1)
            for t in tiles[i]:
                for half in range(2):
                    key = (i, "h2", t, half)
                    take_tile(pe, key)
                    for k in range(4):
                        m = pe.transpose(bank(key)[:, k * P:(k + 1) * P], h2T[:, 4 * half + k, t * P:(t + 1) * P], ident)
                    m.then_inc(tile_done, 1)
            pe.wait_ge(rt_asg[i], 1)
            key = (i, "rank")
            take_tile(pe, key)
            tl = tiles[i]
            pe.matmul(bank(key)[:, NE * tl[0]:5 * NE], tri, asg[:, tl[0]:, :], start=True, stop=False, skip_group_check=True)
            for u in tl:
                m = pe.matmul(bank(key)[:, NE * (u + 1):5 * NE], ones, spread(asg[:, u:u + 1, :], [P, 4 - u, NE]),
                              start=False, stop=u == tl[-1], skip_group_check=True)
            m.then_inc(tile_done, 1)
            for g in range(4):
                key = (i, "ids", g)
                take_tile(pe, key)
                pe.wait_ge(picked, 4 * i + g + 1)
                for e in range(4):
                    for t in tl:
                        m = pe.matmul(bank(key)[0:CAP[i], 2 * e:2 * e + 2], pick[:, t, 4 * g + e, 0:CAP[i]], tokr[:, t, :],
                                      start=t == tl[0], stop=t == tl[-1], skip_group_check=True)
                m.then_inc(tile_done, 1)
            wait_all_emptied(pe, key)

            nb, cb, cap = exp0[i], NE * i, CAP[i]

            def turn_tokens(e, j):
                pe.wait_ge(e_in[j], (8 * cb + 16) + (e - j) * 8)
                pe.wait_ge(e_xl, cb + e)
                for k in range(KT):
                    m = pe.transpose(ps[:, 4 + k // 4, (k % 4) * cap:(k % 4 + 1) * cap], xg[0:cap, j, k * P:(k + 1) * P],
                                     ident[0:cap, 0:cap])
                m.then_inc(e_xt, 1)

            def into_hidden(n, e, m_, it=None):
                if m_ == 0:
                    pe.wait_ge(e_xl, cb + e + 1)
                    pe.wait_ge(e_gu, cb + e)
                else:
                    pe.wait_ge(e_he, cb + e)
                for ch in range(4):
                    pe.wait_ge(lo_ready, scaled(n + ch + 1, it, 24))
                    for k in range(CK):
                        kt = CK * ch + k
                        m = product(pe, ps[0:cap, m_, :], xhi[:, kt, 0:cap], xlo[:, kt, 0:cap], whi(n + ch)[:, k, :],
                                    wlo(n + ch)[:, k, :], kt == 0, kt == KT - 1)
                    m.then_inc(w_used, 1)

            def turn_hidden(e):
                pe.wait_ge(e_he, cb + e + 1)
                for k in range(KE):
                    m = pe.transpose(ps[:, 6, k * cap:(k + 1) * cap], he[0:cap, k * P:(k + 1) * P], ident[0:cap, 0:cap])
                m.then_inc(e_ht, 1)

            def down(n, e, it=None):
                pe.wait_ge(e_hl, cb + e + 1)
                pe.wait_ge(e_ya, cb + e)
                pe.wait_ge(e_yd, cb + e)
                for ch in range(4):
                    pe.wait_ge(lo_ready, scaled(n + ch + 1, it, 24))
                    for k in range(CK):
                        kt = CK * (ch % 2) + k
                        m = product(pe, ps[0:cap, 2 + ch // 2, :], hehi[:, kt, 0:cap], helo[:, kt, 0:cap], whi(n + ch)[:, k, :],
                                    wlo(n + ch)[:, k, :], kt == 0, kt == KE - 1)
                    m.then_inc(w_used, 1)

            for e in range(2):
                turn_tokens(e, e)
                into_hidden(nb + 8 * e, e, 0)
                if e:
                    turn_hidden(0)
                into_hidden(nb + 8 * e + 4, e, 1)
            with pe.Fori(0, NE // 2 - 1) as it:
                for j in range(2):
                    e = 2 * it + (2 + j)
                    n = nb + 16 + 12 * j
                    turn_tokens(e, j)
                    down(n, 2 * it + j, it)
                    into_hidden(n + 4, e, 0, it)
                    turn_hidden(2 * it + (1 + j))
                    into_hidden(n + 8, e, 1, it)
            n = nb + NE * EXP_CHUNKS - 8
            down(n, NE - 2)
            turn_hidden(NE - 1)
            down(n + 4, NE - 1)
            pe.wait_ge(e_ya, cb + NE)
            pe.wait_ge(e_yd, cb + NE)
            if i == DEPTH - 1:
                for k in range(KT):
                    key = ("last", k)
                    take_tile(pe, key)
                    for f in range(4 * (k % 2), 4 * (k % 2) + 4):
                        src = (X[:, f, SEQ:SEQ + P], X[:, f, SEQ + P:T], spread(mod[1][:, 40 + f, 0:1], [P, P]),
                               spread(vec[0][:, V_GF + f:V_GF + f + 1], [P, P]))[k // 2]
                        m = pe.transpose(bank(key)[:, (f % 4) * P:(f % 4 + 1) * P], src, ident)
                    m.then_inc(tile_done, 1)

            over = pe.value_load(most[0:1, 0:1], min_val=0, max_val=T)
            with pe.If(over > CAP[i]):
                if i == DEPTH - 1:
                    wait_all_emptied(pe, ("last", KT - 1))
                with pe.Fori(0, NE * len(tiles[i])) as r:
                    pe.wait_ge(f_in[i], r * 48 + 48)
                    for k in range(KT):
                        m = pe.transpose(ps[:, 4 + k // 4, (k % 4) * P:(k % 4 + 1) * P], xg[:, 0, k * P:(k + 1) * P], ident)
                    m.then_inc(f_pe[i], 1)
                    pe.wait_ge(f_dve[i], r * 5 + 1)
                    for m_ in range(2):
                        for k in range(KT):
                            m = pe.matmul(ps[:, m_, :], xT32[:, k, :], raw[:, 4 * m_ + k // 2, k % 2, :], start=k == 0,
                                          stop=k == KT - 1)
                    m.then_inc(f_pe[i], 1)
                    pe.wait_ge(f_dve[i], r * 5 + 3)
                    for k in range(KE):
                        m = pe.transpose(ps[:, 6, k * P:(k + 1) * P], he[:, k * P:(k + 1) * P], ident)
                    m.then_inc(f_pe[i], 1)
                    pe.wait_ge(f_dve[i], r * 5 + 4)
                    pe.wait_ge(f_dn[i], r * 16 + 16)
                    for half in range(2):
                        for k in range(KE):
                            m = pe.matmul(ps[:, 2 + half, :], hT32[:, k, :], raw[:, k, half, :], start=k == 0, stop=k == KE - 1)
                    m.then_inc(f_pe[i], 1)
                    pe.wait_ge(f_dve[i], r * 5 + 5)

            if i == DEPTH - 1:
                continue
            pe.wait_ge(y_sum[i], len(tiles[i]))
            for k in range(KT):
                key = (i, "yT", k)
                take_tile(pe, key)
                for t in tiles[i]:
                    m = pe.transpose(bank(key)[:, t * P:(t + 1) * P], y2[:, t, k * P:(k + 1) * P], ident)
                m.then_inc(tile_done, 1)

    lam_init = [0.8 - 0.6 * math.exp(-0.3 * i) for i in range(DEPTH)]
    streams = [(0, SEQ, 1), (SEQ, T, 0)]

    @block.scalar
    def _(act):
        act.wait_ge(filled, 3)

        norm_tile = {"n1_0": (0, "n1"), "n2_0": (0, "n2"), "n1_1": (1, "n1"), "n2_1": (1, "n2")}

        def warm(func):
            act.activation(warmed[:, :], epst[:, :], func)

        def norm_squares(name, c0, ready, ks=range(KT)):
            o = KT * norms[name]
            if ks[0] == 0:
                warm(ACT.Sqrt)
            for k in ks:
                wait_emptied(act, ready(k))
                if k >= 2:
                    act.wait_ge(n_squ, o - norms[name] + k - 1)
                act.activation(sq[:, k % 2, c0:T], X[:, k, c0:T], ACT.Square).then_inc(n_sq, 1)

        def norm_rms(name, c0):
            key = norm_tile[name]
            wait_tile(act, key)
            act.activation(std[:, c0:T], bank(key)[:, c0:T], ACT.Sqrt, bias=epst[:, 0:1], scale=1.0 / D).then_inc(free_act, 1)

        def norm_apply(name, c0, scale, bias, split, between={}):
            o, os = KT * norms[name], KT * (norms[name] // 2)
            for k in range(KT):
                act.wait_ge(n_xn, o + k + 1)
                if split and k >= 2:
                    act.wait_ge(n_lo, os + k - 1)
                dst = hf[:, k % 2] if split else h2T[:, k]
                for a_, b_, s in [p for p in streams if p[0] >= c0]:
                    kw = {"bias": bias(k, s)} if bias else {}
                    m = act.activation(dst[:, a_:b_], xn[:, k % 2, a_:b_], ACT.Identity, scale=scale(k, s), **kw)
                m.then_inc(n_hf, 1)
                if split:
                    act.wait_ge(n_hf, o + k + 1)
                    act.activation(Hhi[:, k, :], hf[:, k % 2, :], ACT.Copy).then_inc(n_hi, 1)
                if k in between:
                    split_hi(act, between[k])

        def empty_ada(part):
            act.wait_ge(w_used, ada_last[part] + 1)
            act.activation(ada_row[part][0:AR, :], ps[0:AR, 7, :], ACT.Copy).then_inc(ada_rows, 1)

        def empty_step(i, s):
            c0, kind = col0[i], s[0]
            if kind == "ADA" and s[2] == AG - 1:
                empty_ada(1 + s[1])
            if kind in ("ADA", "WF", "WO"):
                return
            for t in range(4):
                key = (i, kind, s[1], t)
                b = 4 * s[1] + t
                if kind == "WA":
                    act.wait_ge(m_f[i], b + 1)
                    act.activation(Hhi[:, b, c0:T], G[:, b, c0:T], ACT.Copy).then_inc(m_h[i], 1)
                    continue
                wait_tile(act, key)
                if kind == "F":
                    m = act.activation(FT[:, t, c0:T], bank(key)[:, c0:T], ACT.Copy)
                elif kind == "QK":
                    cc = 0 if s[1] >= 2 else c0
                    if i == 0 and b == 0:
                        act.wait_ge(pad_out, 16 * (ROWS // P - T // P))
                    m = act.activation(QK[:, b, cc:T], bank(key)[:, cc:T], ACT.Copy)
                elif kind == "V":
                    m = act.activation(V[:, t, s[1] * CW:(s[1] + 1) * CW], bank(key)[:, :], ACT.Copy)
                else:
                    off = V_BG + (0 if kind == "GA" else 8) + b
                    if kind == "GA" and b == 0:
                        act.wait_ge(roped[i], 2 * HEADS)
                    m = act.activation((GA if kind == "GA" else G)[:, b, c0:T], bank(key)[:, c0:T], ACT.Sigmoid,
                                       bias=vec[i][:, off:off + 1])
                m.then_inc(free_act, 1)

        def attention(i):
            warm(ACT.Exp)
            act.wait_ge(x_kept[i], 16)
            its = items[i]
            for j in range(len(its) + 4):
                if j == len(its):
                    warm(ACT.Sqrt)
                if j < len(its):
                    q, b = its[j][1], j % 2
                    act.wait_ge(a_neg, first_item[i] + j + 1)
                    if j >= 2:
                        act.wait_ge(a_comb, first_item[i] + j - 1)
                    for m_ in range(2):
                        act.activation(E[:, b, m_, 0:keys(q)], ps[:, 2 * b + m_, 0:keys(q)], ACT.Exp,
                                       bias=aneg[:, b, m_:m_ + 1], scale=ATT_SCALE,
                                       accum_out=asum[:, b, m_:m_ + 1]).then_inc(a_exp, 1)
                t = j - 2
                if 0 <= t < len(its):
                    q, b = its[t][1], t % 2
                    act.wait_ge(a_tr, first_item[i] + t + 1)
                    if t >= 2:
                        act.wait_ge(a_pv, first_item[i] + t - 1)
                    act.activation(AT[:, b, 0:keys(q)], ps[:, 4 + b, 0:keys(q)], ACT.Copy).then_inc(a_trc, 1)
                t = j - 4
                if t >= 0:
                    h, q = its[t]
                    c = (q - tiles[i][0]) * HEADS + h
                    act.wait_ge(a_oc, first_item[i] + t + 1)
                    if t >= 4:
                        act.wait_ge(o_ss[i], t - 3)
                    act.activation(osq[:, t % 4, :], O[:, q, h, :], ACT.Square, accum_out=oss[:, c:c + 1]).then_inc(o_ss[i], 1)
            act.wait_ge(o_ss[i], len(its))
            no = len(tiles[i]) * HEADS
            act.activation(ostd[:, 0:no], oss[:, 0:no], ACT.Sqrt, bias=epst[:, 0:1], scale=1.0 / P).then_inc(o_std[i], 1)
            for h in range(HEADS):
                key = (i, "OT", h)
                wait_tile(act, key)
                if h >= 2:
                    act.wait_ge(ot_l[i], h - 1)
                act.activation(ot32[:, h % 2, col0[i]:T], bank(key)[:, col0[i]:T], ACT.Identity,
                               scale=gsub[:, 0:1]).then_inc(free_act, 1)
                wait_emptied(act, key)
                act.activation(OThi[:, h, col0[i]:T], ot32[:, h % 2, col0[i]:T], ACT.Copy).then_inc(ot_h[i], 1)

        def dft_channels(i):
            for s, g in dft[i]:
                key = (i, "Y", s, g)
                wait_tile(act, key)
                act.activation(Y[:, s, g, :, :].rearrange("p t n -> p (t n)"), bank(key), ACT.Copy).then_inc(free_act, 1)

        def dft_tokens(i):
            for s, g in dft[i]:
                key = (i, "Z", s, g)
                wait_tile(act, key)
                act.activation(Zhi[:, g, s * SEQ:(s + 1) * SEQ], bank(key)[:, 0:SEQ], ACT.Copy).then_inc(z_hi[i], 1)

        for k in range(1, KT, 2):
            wait_tile(act, ("x0", k))
            act.activation(X[:, k, :], bank(("x0", k)), ACT.Copy).then_inc(free_act, 1)
        wait_emptied(act, ("vec", 0))
        act.activation(csig[:, :], vec[0][:, V_C:V_C + 16], ACT.Sigmoid).then_inc(cond_sig, 1)
        act.wait_ge(cond_sil, 1)
        act.activation(cond[:, :, AR - 4:AR].rearrange("p k (s u) -> p s k u", u=2)[:, :, :, 0],
                       csil[:, :].rearrange("p (s k) -> p s k", s=2), ACT.Copy).then_inc(cond_hi, 1)
        for n in range(ADA_A):
            if n < KT:
                norm_squares("n1_0", 0, lambda k: ("x0", k), [n])
            if n == KT:
                norm_rms("n1_0", 0)
            split_hi(act, n)
        act.wait_ge(lam_s, 1)
        act.activation(lexp[:, :], lsum[:, :], ACT.Exp).then_inc(lam_e, 1)
        empty_ada(0)
        act.wait_ge(cst2_in, 16)
        act.activation(tokr[:, :, :].rearrange("p t u -> p (t u)"), cs(C_TOK, 8), ACT.Copy)
        for i in range(DEPTH):
            n0 = mix0[i]
            for ch in range(ahead[i]):
                split_hi(act, n0 + ch)
            if i == 0:
                act.wait_ge(mod_a, 1)
            else:
                norm_squares("n1_1", 0, lambda k: (0, "yT", k))
                norm_rms("n1_1", 0)
                act.wait_ge(mod_b, 2)
            norm_apply(f"n1_{i}", 0, lambda k, s: sc1[i][:, k, s:s + 1], lambda k, s: mod[i][:, k, s:s + 1], True,
                       {2 * ch - 1: n0 + ch for ch in range(ahead[i], 4)})
            at_chunk = {n: sc for sc, n in place_of[i].items()}
            for n in range(n0 + 4, exp0[i] + SPL):
                s, ch = at_chunk.get(n - SPL, (None, 0))
                if ch == 3:
                    empty_step(i, s)
                if n - 3 == place_of[i][(("GF", 0), 0)]:
                    dft_channels(i)
                if n - 3 == place_of[i][(("GF", 1), 0)]:
                    dft_tokens(i)
                if n - SPL == place_of[i][(("WA", 0), 0)]:
                    attention(i)
                if n < exp0[i]:
                    split_hi(act, n)
                if n == place_of[i][(("WO", 1), 3)]:
                    norm_squares(f"n2_{i}", col0[i], lambda k: (i, "WO", 0, k), range(4))
            norm_squares(f"n2_{i}", col0[i], lambda k: (i, "WO", k // 4, k % 4), range(4, KT))
            norm_rms(f"n2_{i}", col0[i])
            act.wait_ge(mod_b, 1)
            norm_apply(f"n2_{i}", col0[i], lambda k, s: sc2[i][:, k, s:s + 1], lambda k, s: mod[i][:, 24 + k, s:s + 1], False)
            key = (i, "log")
            warm(ACT.Sigmoid)
            wait_tile(act, key)
            act.activation(affT[0:NE, col0[i]:T], bank(key)[0:NE, col0[i]:T], ACT.Sigmoid).then_inc(free_act, 1)
            for t in tiles[i]:
                for half in range(2):
                    key = (i, "h2", t, half)
                    wait_tile(act, key)
                    act.activation(h2tok[:, t, half * CW:(half + 1) * CW], bank(key), ACT.Copy).then_inc(free_act, 1)
                wait_emptied(act, key)
                act.dma_start(hbuf[t * P:(t + 1) * P, :], h2tok[:, t, :]).then_inc(h_out[i], 16)

            nb, cb, cap = exp0[i], NE * i, CAP[i]

            def tokens_hi(e):
                act.wait_ge(e_xt, cb + e + 1)
                act.activation(turned(xhi, cap), turned_ps(4, 2, cap), ACT.Copy).then_inc(e_xh, 1)

            def splits(n, count, it=None):
                for ch in range(count):
                    split_hi(act, n + ch, it, 24)

            def sigmoid(n, it=None):
                act.wait_ge(w_used, scaled(n, it, 24))
                act.activation(sg[0:cap, :], ps[0:cap, 0, :], ACT.Sigmoid).then_inc(e_sig, 1)

            def hidden_hi(e):
                act.wait_ge(e_ht, cb + e + 1)
                act.activation(turned(hehi, cap), turned_ps(6, 1, cap), ACT.Copy).then_inc(e_hh, 1)

            def result(n, e, j, it=None):
                act.wait_ge(w_used, scaled(n, it, 24))
                act.wait_ge(y_free[i], e + 1)
                act.activation(ytile[0:cap, j, 0:CW], ps[0:cap, 2, :], ACT.Copy).then_inc(e_ya, 1)

            act.wait_ge(w_used, nb)
            splits(nb, 4)
            act.wait_ge(h_out[i], 16 * len(tiles[i]))
            tokens_hi(0)
            splits(nb + 4, 4)
            act.wait_ge(rt_loc[i], 1)
            sigmoid(nb + 4)
            splits(nb + 8, 4)
            tokens_hi(1)
            splits(nb + 12, 4)
            with act.Fori(0, NE // 2 - 1) as it:
                for j in range(2):
                    n = nb + 16 + 12 * j
                    splits(n, 4, it)
                    sigmoid(n - 4, it)
                    hidden_hi(2 * it + j)
                    splits(n + 4, 4, it)
                    tokens_hi(2 * it + 2 + j)
                    splits(n + 8, 3, it)
                    result(n + 4, 2 * it + j, j, it)
                    splits(n + 11, 1, it)
            n = nb + NE * EXP_CHUNKS - 8
            splits(n, 4)
            sigmoid(n - 4)
            hidden_hi(NE - 2)
            splits(n + 4, 4)
            result(n + 4, NE - 2, 0)
            hidden_hi(NE - 1)
            result(n + 8, NE - 1, 1)

            if i == DEPTH - 1:
                for k in range(1, KT, 2):
                    wait_tile(act, ("last", k))
                    act.activation(token_major[:, k // 2, CW:D], bank(("last", k)), ACT.Copy).then_inc(free_act, 1)

            over = act.value_load(most[0:1, 0:1], min_val=0, max_val=T)
            with act.If(over > CAP[i]):
                with act.Fori(0, NE * len(tiles[i])) as r:
                    act.wait_ge(f_pe[i], r * 4 + 2)
                    act.activation(sg[:, :], ps[:, 0, :], ACT.Sigmoid).then_inc(f_act[i], 1)
                    act.wait_ge(f_dve[i], r * 5 + 5)
        warm(ACT.Sqrt)
        for t in range(2):
            act.wait_ge(y_in[2 + t], 32 * DEPTH)
            act.activation(y1[:, 2 + t, :], y1[:, 2 + t, :], ACT.Identity, scale=gates[:, 0, 2 + t:3 + t]).then_inc(z_first, 1)
        for t in range(2):
            act.wait_ge(z_sum, t + 1)
            act.activation(zsq[:, t, :], y2[:, 2 + t, :], ACT.Square, accum_out=zss[:, 0, t:t + 1]).then_inc(z_ss, 1)
            act.wait_ge(z_ss, t + 1)
            act.activation(zss[:, 1, t:t + 1], zss[:, 0, t:t + 1], ACT.Sqrt, bias=epst[:, 0:1], scale=1.0 / D).then_inc(z_std, 1)

    @block.vector
    def _(dve):
        chain = [0]

        def link(ins):
            chain[0] += 1
            ins.then_inc(dve_chain, 1)
            dve.wait_ge(dve_chain, chain[0])

        def stt(o, a, s, b, op0, op1):
            return dve.scalar_tensor_tensor(out=o, in0=a, scalar=s, in1=b, op0=op0, op1=op1)

        def norm_inverse(name, c0):
            key = {"n1_0": (0, "n1"), "n2_0": (0, "n2"), "n1_1": (1, "n1"), "n2_1": (1, "n2")}[name]
            wait_emptied(dve, key)
            link(dve.reciprocal(rinv[:, c0:T], std[:, c0:T]))

        def norm(name, c0, split, between={}):
            o, os = KT * norms[name], KT * (norms[name] // 2)
            for k in range(KT + 1):
                if k < KT:
                    if k >= 2:
                        dve.wait_ge(n_hf, o + k - 1)
                    dve.tensor_tensor(xn[:, k % 2, c0:T], X[:, k, c0:T], rinv[:, c0:T], ALU.mult).then_inc(n_xn, 1)
                if split and k >= 1:
                    dve.wait_ge(n_hi, os + k)
                    dve.tensor_tensor(Hlo[:, k - 1, :], hf[:, (k - 1) % 2, :], Hhi[:, k - 1, :].bitcast(F32),
                                      ALU.subtract).then_inc(n_lo, 1)
                if k - 1 in between:
                    split_lo(dve, between[k - 1])

        def adaln(part, i, g0, g1, done):
            b0, b1 = 4 * g0, 4 * g1
            m = mod[i][:, b0:b1, :]
            key = ("ada", part)
            wait_tile(dve, key)
            for ct in range(4):
                sums = bank(key)[:, ct * AR + 4 * g0:ct * AR + 4 * g1].rearrange("p (g s u) -> p g s u", s=2, u=2)
                ins = dve.tensor_reduce(m.rearrange("p (g c) s -> p g c s", c=4)[:, :, ct, :], sums, AX.X, ALU.add)
            ins.then_inc(free_dve, 1)
            wait_emptied(dve, key)
            bias = vec[i][:, V_BADA + b0:V_BADA + b1].unsqueeze(2)
            ins = dve.tensor_tensor(m, m, spread(bias, [P, b1 - b0, 2]), ALU.add)
            for sc, blk, g in ((sc1[i], 8, V_G1), (sc2[i], 32, V_G2)):
                if b0 <= blk < b1:
                    link(ins)
                    ins = stt(sc[:, :, :], mod[i][:, blk:blk + 8, :], 1.0,
                              spread(vec[i][:, g:g + 8].unsqueeze(2), [P, KT, 2]), ALU.add, ALU.mult)
            ins.then_inc(done, 1)

        def empty_step(i, s, half=1):
            c0, kind = col0[i], s[0]
            parts = [p for p in streams if p[0] >= c0]
            if kind == "QK":
                for t in range(4):
                    b = 4 * s[1] + t
                    wait_emptied(dve, (i, "QK", s[1], t))
                    lat = QK[:, b, SEQ:T]
                    link(dve.stream_shuffle(rt[:, t % 2, :], lat, [(r + 16) % 32 for r in range(32)]))
                    link(dve.tensor_tensor(rt[:, t % 2, :], rt[:, t % 2, :], cs(C_RS, SEQ), ALU.mult))
                    link(dve.tensor_tensor(lat, lat, cs(C_RC, SEQ), ALU.mult))
                    dve.tensor_tensor(lat, lat, rt[:, t % 2, :], ALU.add).then_inc(roped[i], 1)
            elif kind == "WF":
                for t in range(4 * half, 4 * half + 4):
                    key = (i, "WF", 0, t)
                    wait_emptied(dve, (i, "GF", t // 4, t % 4))
                    wait_tile(dve, key)
                    dve.tensor_tensor(G[:, t, c0:T], bank(key)[:, c0:T], G[:, t, c0:T], ALU.mult).then_inc(free_dve, 1)
            elif kind == "WA":
                for t in range(4):
                    b, key = 4 * s[1] + t, (i, "WA", s[1], t)
                    wait_tile(dve, key)
                    ga = GA[:, b, c0:T]
                    dve.tensor_tensor(ga, bank(key)[:, c0:T], ga, ALU.mult).then_inc(free_dve, 1)
                    wait_emptied(dve, key)
                    dve.tensor_tensor(G[:, b, c0:T], G[:, b, c0:T], ga, ALU.add).then_inc(m_f[i], 1)
                for t in range(4):
                    b = 4 * s[1] + t
                    dve.wait_ge(m_h[i], b + 1)
                    dve.tensor_tensor(Hlo[:, b, c0:T], G[:, b, c0:T], Hhi[:, b, c0:T].bitcast(F32),
                                      ALU.subtract).then_inc(m_l[i], 1)
            elif kind == "WO":
                if s[1] == 0:
                    dve.wait_ge(x_back[i], 16)
                for t in range(4):
                    b, key = 4 * s[1] + t, (i, "WO", s[1], t)
                    wait_tile(dve, key)
                    for a_, b_, cd in parts:
                        m = stt(X[:, b, a_:b_], bank(key)[:, a_:b_], mod[i][:, 16 + b, cd:cd + 1], X[:, b, a_:b_],
                                ALU.mult, ALU.add)
                    m.then_inc(free_dve, 1)

        def attention(i):
            link(dve.tensor_scalar(gsub[:, :], vec[i][:, V_SUB:V_SUB + 1], 1.0 - lam_init[i], None, ALU.mult))
            its = items[i]
            for j in range(len(its) + 3):
                if j < len(its):
                    q, b = its[j][1], j % 2
                    dve.wait_ge(a_s, first_item[i] + j + 1)
                    link(dve.tensor_reduce(amax[:, b, :], ps[:, 2 * b:2 * b + 2, 0:keys(q)], AX.X, ALU.max))
                    dve.tensor_scalar(aneg[:, b, :], amax[:, b, :], -ATT_SCALE, None, ALU.mult).then_inc(a_neg, 1)
                if 1 <= j <= len(its):
                    q, b = its[j - 1][1], (j - 1) % 2
                    dve.wait_ge(a_exp, 2 * first_item[i] + 2 * j)
                    r4 = (j - 1) % 4
                    link(dve.reciprocal(arec[:, r4, :], asum[:, b, :]))
                    link(stt(arec1[:, b:b + 1], arec[:, r4, 1:2], nlam[:, i:i + 1], asum[:, b, 0:1], ALU.mult, ALU.mult))
                    e0, e1 = E[:, b, 0, 0:keys(q)], E[:, b, 1, 0:keys(q)]
                    if j >= 3:
                        dve.wait_ge(a_tr, first_item[i] + j - 2)
                    stt(A[:, b, 0:keys(q)], e1, arec1[:, b:b + 1], e0, ALU.mult, ALU.add).then_inc(a_comb, 1)
                t = j - 3
                if t >= 0:
                    h, q = its[t]
                    dve.wait_ge(a_pv, first_item[i] + t + 1)
                    dve.tensor_scalar(O[:, q, h, :], ps[:, 6 + t % 2, 0:P], arec[:, t % 4, 0:1], None,
                                      ALU.mult).then_inc(a_oc, 1)
            tl, c0 = tiles[i], col0[i]
            no = len(tl) * HEADS
            by_head = orin[:, 0:no].rearrange("p (q h) -> p q h", h=HEADS)
            dve.wait_ge(o_std[i], 1)
            link(dve.reciprocal(orin[:, 0:no], ostd[:, 0:no]))
            for h in range(HEADS + 2):
                if h < HEADS:
                    oh = O[:, tl[0]:, h, :]
                    dve.tensor_tensor(oh, oh, spread(by_head[:, :, h].unsqueeze(2), [P, len(tl), P]),
                                      ALU.mult).then_inc(o_nrm[i], 1)
                if h >= 2:
                    dve.wait_ge(ot_h[i], h - 1)
                    dve.tensor_tensor(OTlo[:, h - 2, c0:T], ot32[:, h % 2, c0:T], OThi[:, h - 2, c0:T].bitcast(F32),
                                      ALU.subtract).then_inc(ot_l[i], 1)

        def dft_tokens(i):
            for m_, (s, g) in enumerate(dft[i]):
                key = (i, "Z", s, g)
                cols = slice(s * SEQ, (s + 1) * SEQ)
                dve.wait_ge(z_hi[i], m_ + 1)
                dve.tensor_tensor(Zlo[:, g, cols], bank(key)[:, 0:SEQ], Zhi[:, g, cols].bitcast(F32),
                                  ALU.subtract).then_inc(free_dve, 1)

        def route(i):
            t0, nt = tiles[i][0], len(tiles[i])
            v = lambda t_: t_[:, t0:]
            g4 = lambda t_: v(t_).rearrange("p t (g e) -> p t g e", g=4)
            key_e = cs(C_KE, NE).unsqueeze(1)
            key_g = cs(C_KG, 4).unsqueeze(1)
            row = lambda t_, n_: spread(v(t_).unsqueeze(2), [P, nt, n_])

            def first_max(src, n_, keys_, work, onehot):
                link(dve.tensor_reduce(v(tm), v(src), AX.X, ALU.max))
                link(dve.tensor_tensor(v(work), v(src), row(tm, n_), ALU.is_equal))
                link(dve.tensor_tensor(v(work), v(work), spread(keys_, [P, nt, n_]), ALU.mult))
                link(dve.tensor_reduce(v(tm), v(work), AX.X, ALU.max))
                link(dve.tensor_tensor(v(onehot), v(work), row(tm, n_), ALU.is_equal))

            key = (i, "aff")
            wait_tile(dve, key)
            dve.tensor_copy(v(aff).rearrange("p t e -> p (t e)"), bank(key)[:, NE * t0:4 * NE]).then_inc(free_dve, 1)
            wait_emptied(dve, key)
            link(dve.tensor_tensor(v(sel), v(aff), spread(brb[:, :].unsqueeze(1), [P, nt, NE]), ALU.add))
            s4 = g4(sel)
            dve.tensor_scalar(asg[:, 4, :], sel[:, 3, :], 0.0, None, ALU.mult)
            for m_, (a_, b_) in enumerate([(0, 1), (0, 2), (0, 3), (1, 2), (1, 3), (2, 3)]):
                ins = dve.tensor_tensor(v(pr)[:, :, :, m_], s4[:, :, :, a_], s4[:, :, :, b_], ALU.add)
            link(ins)
            link(dve.tensor_reduce(v(gsc), v(pr), AX.X, ALU.max))
            first_max(gsc, 4, key_g, geq, ing)
            inb = spread(v(ing).unsqueeze(3), [P, nt, 4, 4])
            link(dve.tensor_scalar(v(geq), v(ing), BIG, -BIG, ALU.mult, ALU.add))
            link(dve.tensor_tensor(g4(msk), s4, inb, ALU.mult))
            link(dve.tensor_tensor(g4(msk), g4(msk), spread(v(geq).unsqueeze(3), [P, nt, 4, 4]), ALU.add))
            first_max(msk, NE, key_e, ta, oh1)
            link(dve.tensor_scalar(v(tb), v(oh1), -BIG, None, ALU.mult))
            link(dve.tensor_tensor(v(msk), v(msk), v(tb), ALU.add))
            first_max(msk, NE, key_e, ta, oh2)
            dve.tensor_tensor(asg[:, t0:4, :], v(oh1), v(oh2), ALU.add).then_inc(rt_asg[i], 1)
            dve.wait_ge(rt_asg[i], 1)
            link(dve.tensor_scalar(v(off), asg[:, t0:4, :], -2.0 * T, 2.0 * T, ALU.mult, ALU.add))
            for s, oh in enumerate((oh1, oh2)):
                link(dve.tensor_tensor(v(ta), v(oh), v(aff), ALU.mult))
                link(dve.tensor_reduce(w12[:, s, t0:], v(ta), AX.X, ALU.add))
            link(dve.tensor_tensor(v(wsum), w12[:, 0, t0:], w12[:, 1, t0:], ALU.add))
            link(dve.reciprocal(v(wsum), v(wsum)))
            for s in range(2):
                link(dve.tensor_tensor(gates[:, s, t0:], w12[:, s, t0:], v(wsum), ALU.mult))

        def experts_tokens(i):
            t0, nt = tiles[i][0], len(tiles[i])
            v = lambda t_: t_[:, t0:]
            key = (i, "rank")
            wait_tile(dve, key)
            dve.tensor_copy(rank[:, t0:5, :].rearrange("p t e -> p (t e)"), bank(key)[:, NE * t0:5 * NE]).then_inc(free_dve, 1)
            wait_emptied(dve, key)
            link(dve.tensor_tensor(v(mrank), rank[:, t0:4, :], v(off), ALU.add))
            cap = CAP[i]
            iota = spread(cs(C_IOTA, cap).unsqueeze(1).unsqueeze(1), [P, nt, 4, cap])
            for g in range(5):
                if g < 4:
                    ex = slice(4 * g, 4 * g + 4)
                    dve.tensor_tensor(pick[:, t0:, ex, 0:cap], spread(mrank[:, t0:, ex].unsqueeze(3), [P, nt, 4, cap]), iota,
                                      ALU.is_equal).then_inc(picked, 1)
                if g >= 1:
                    key = (i, "ids", g - 1)
                    wait_tile(dve, key)
                    dve.tensor_copy(ids[0:cap, 4 * g - 4:4 * g], bank(key)[0:cap, 0:8:2]).then_inc(free_dve, 1)
                    split_lo(dve, exp0[i] + g - 1)

        def places(i):
            t0, nt = tiles[i][0], len(tiles[i])
            v = lambda t_: t_[:, t0:]
            count = rank[:, 4, :]
            link(dve.tensor_reduce(most_f[:, :], count, AX.X, ALU.max))
            link(dve.tensor_copy(cum[:, 0, :], count))
            for m_, sh in enumerate((1, 2, 4, 8)):
                a_, b_ = cum[:, m_ % 2, :], cum[:, (m_ + 1) % 2, :]
                link(dve.tensor_copy(b_[:, 0:sh], a_[:, 0:sh]))
                link(dve.tensor_tensor(b_[:, sh:NE], a_[:, sh:NE], a_[:, 0:NE - sh], ALU.add))
            link(dve.tensor_tensor(start_f[:, :], cum[:, 0, :], count, ALU.subtract))
            link(dve.tensor_tensor(v(pos), rank[:, t0:4, :], spread(start_f[:, :].unsqueeze(1), [P, nt, NE]), ALU.add))
            for s, oh in enumerate((oh1, oh2)):
                link(dve.tensor_tensor(v(ta), v(oh), v(pos), ALU.mult))
                link(dve.tensor_reduce(loc_f[:, s, t0:], v(ta), AX.X, ALU.add))
            dve.tensor_copy(loc[:, :, t0:], loc_f[:, :, t0:])
            dve.tensor_copy(starts[:, :], start_f[:, :])
            dve.tensor_copy(most[:, :], most_f[:, :]).then_inc(rt_loc[i], 1)

        def empty_vectors(i):
            wait_tile(dve, ("vec", i))
            dve.tensor_copy(vec[i][:, :], bank(("vec", i))[:, 0:V_ROWS]).then_inc(free_dve, 1)

        for k in range(0, KT, 2):
            wait_tile(dve, ("x0", k))
            dve.tensor_copy(X[:, k, :], bank(("x0", k))).then_inc(free_dve, 1)
        empty_vectors(0)
        wait_emptied(dve, ("vec", 0))
        dve.wait_ge(cond_sig, 1)
        dve.tensor_tensor(csil[:, :], csig[:, :], vec[0][:, V_C:V_C + 16], ALU.mult).then_inc(cond_sil, 1)
        dve.wait_ge(cond_hi, 1)
        cond4 = cond[:, :, AR - 4:AR].rearrange("p k (s u) -> p s k u", u=2)
        dve.tensor_tensor(cond4[:, :, :, 1], csil[:, :].rearrange("p (s k) -> p s k", s=2),
                          cond4[:, :, :, 0].bitcast(F32), ALU.subtract).then_inc(cond_ready, 1)
        for n in range(ADA_A):
            split_lo(dve, n)
            if n == ADA_A // 2:
                dve.wait_ge(lam_in, 16)
                pairs = lamv[:, :, :].rearrange("p (a b) d -> p a b d", b=2)
                link(dve.tensor_tensor(lprod[:, :, :], pairs[:, :, 0, :], pairs[:, :, 1, :], ALU.mult))
                dve.tensor_reduce(lsum[:, :], lprod[:, :, :], AX.X, ALU.add).then_inc(lam_s, 1)
                norm_inverse("n1_0", 0)
        dve.wait_ge(lam_e, 1)
        link(dve.tensor_tensor(nlam[:, :], lexp[:, 1::2], lexp[:, 0::2], ALU.subtract))
        for i in range(DEPTH):
            link(dve.tensor_scalar(nlam[:, i:i + 1], nlam[:, i:i + 1], -lam_init[i], None, ALU.add))
        adaln(0, 0, 0, ADA_A // 4, mod_a)

        for i in range(DEPTH):
            n0 = mix0[i]
            for ch in range(ahead[i]):
                split_lo(dve, n0 + ch)
            if i:
                norm_inverse(f"n1_{i}", 0)
            if i == 0:
                empty_vectors(1)
            norm(f"n1_{i}", 0, True, {2 * ch - 1: n0 + ch for ch in range(ahead[i], 4)})
            at_chunk = {n: sc for sc, n in place_of[i].items()}
            for n in range(n0 + 4, exp0[i] + SPL):
                s, ch = at_chunk.get(n - SPL, (None, 0))
                if ch == 3:
                    empty_step(i, s)
                elif ch == 1 and s == ("WF", 0):
                    empty_step(i, s, 0)
                if n - 3 == place_of[i][(("GF", 1), 0)]:
                    dft_tokens(i)
                if n - SPL == place_of[i][(("WA", 0), 0)]:
                    attention(i)
                for s_, part in ADA_TURN.items():
                    if i == 0 and n - SPL == place_of[0][(s_, 0)]:
                        adaln(part, part - 1, 0 if part == 2 else ADA_A // 4, AG, mod_b)
                if n < exp0[i]:
                    split_lo(dve, n)
            norm_inverse(f"n2_{i}", col0[i])
            norm(f"n2_{i}", col0[i], False)
            route(i)
            experts_tokens(i)

            nb, cb, cap = exp0[i], NE * i, CAP[i]

            def tokens_lo(e):
                dve.wait_ge(e_xh, cb + e + 1)
                dve.tensor_tensor(turned(xlo, cap), turned_ps(4, 2, cap), turned(xhi, cap).bitcast(F32), ALU.subtract).then_inc(e_xl, 1)

            def splits(n, count, it=None):
                for ch in range(count):
                    split_lo(dve, n + ch, it, 24)

            def gated(e, first=False):
                if not first:
                    dve.wait_ge(e_he, cb + e)
                dve.wait_ge(e_sig, cb + e + 1)
                dve.tensor_tensor(gu[0:cap, :], ps[0:cap, 0, :], sg[0:cap, :], ALU.mult).then_inc(e_gu, 1)

            def hidden(n, e, it=None):
                dve.wait_ge(w_used, scaled(n, it, 24))
                dve.wait_ge(e_gu, cb + e + 1)
                dve.tensor_tensor(he[0:cap, :], ps[0:cap, 1, :], gu[0:cap, :], ALU.mult).then_inc(e_he, 1)

            def hidden_lo(e):
                dve.wait_ge(e_hh, cb + e + 1)
                dve.tensor_tensor(turned(helo, cap), turned_ps(6, 1, cap), turned(hehi, cap).bitcast(F32), ALU.subtract).then_inc(e_hl, 1)

            def result(n, e, j, it=None):
                dve.wait_ge(w_used, scaled(n, it, 24))
                dve.wait_ge(y_free[i], e + 1)
                dve.tensor_copy(ytile[0:cap, j, CW:D], ps[0:cap, 3, :]).then_inc(e_yd, 1)

            tokens_lo(0)
            splits(nb + 4, 3)
            places(i)
            splits(nb + 7, 1)
            gated(0, first=True)
            splits(nb + 8, 4)
            tokens_lo(1)
            hidden(nb + 8, 0)
            splits(nb + 12, 4)
            with dve.Fori(0, NE // 2 - 1) as it:
                for j in range(2):
                    n = nb + 16 + 12 * j
                    splits(n, 4, it)
                    gated(2 * it + 1 + j)
                    hidden_lo(2 * it + j)
                    splits(n + 4, 4, it)
                    hidden(n, 2 * it + 1 + j, it)
                    tokens_lo(2 * it + 2 + j)
                    splits(n + 8, 3, it)
                    result(n + 4, 2 * it + j, j, it)
                    splits(n + 11, 1, it)
            n = nb + NE * EXP_CHUNKS - 8
            splits(n, 4)
            gated(NE - 1)
            hidden_lo(NE - 2)
            splits(n + 4, 4)
            hidden(n, NE - 1)
            result(n + 4, NE - 2, 0)
            hidden_lo(NE - 1)
            result(n + 8, NE - 1, 1)

            if i == DEPTH - 1:
                for k in range(0, KT, 2):
                    wait_tile(dve, ("last", k))
                    dve.tensor_copy(token_major[:, k // 2, 0:CW], bank(("last", k))).then_inc(free_dve, 1)

            over = dve.value_load(most[0:1, 0:1], min_val=0, max_val=T)
            with dve.If(over > CAP[i]):
                with dve.Fori(0, NE * len(tiles[i])) as r:
                    dve.wait_ge(f_pe[i], r * 4 + 1)
                    dve.tensor_copy(xT32[:, :, :].rearrange("p k t -> p (k t)"),
                                    ps[:, 4:6, :].rearrange("p b n -> p (b n)")).then_inc(f_dve[i], 1)
                    dve.wait_ge(f_act[i], r + 1)
                    dve.tensor_tensor(gu[:, :], ps[:, 0, :], sg[:, :], ALU.mult).then_inc(f_dve[i], 1)
                    dve.wait_ge(f_dve[i], r * 5 + 2)
                    dve.tensor_tensor(he[:, :], ps[:, 1, :], gu[:, :], ALU.mult).then_inc(f_dve[i], 1)
                    dve.wait_ge(f_pe[i], r * 4 + 3)
                    dve.tensor_copy(hT32[:, :, :].rearrange("p k t -> p (k t)"), ps[:, 6, :]).then_inc(f_dve[i], 1)
                    dve.wait_ge(f_pe[i], r * 4 + 4)
                    dve.tensor_copy(ytile[:, 0, :], ps[:, 2:4, :].rearrange("p b n -> p (b n)")).then_inc(f_dve[i], 1)

            if i == DEPTH - 1:
                continue
            for t in tiles[i]:
                dve.wait_ge(y_in[t], 32 * (i + 1 if t >= 2 else 1))
                link(dve.tensor_scalar(y1[:, t, :], y1[:, t, :], gates[:, 0, t:t + 1], None, ALU.mult))
                stt(y2[:, t, :], y2[:, t, :], gates[:, 1, t:t + 1], y1[:, t, :], ALU.mult, ALU.add).then_inc(y_sum[i], 1)
            parts = [p for p in streams if p[0] >= col0[i]]
            for k in range(KT):
                key = (i, "yT", k)
                wait_tile(dve, key)
                for a_, b_, cd in parts:
                    m = stt(X[:, k, a_:b_], bank(key)[:, a_:b_], mod[i][:, 40 + k, cd:cd + 1], X[:, k, a_:b_],
                            ALU.mult, ALU.add)
                m.then_inc(free_dve, 1)
        wait_all_emptied(dve, ("last", KT - 1))
        for t in range(2):
            z = y2[:, 2 + t, :]
            dve.wait_ge(z_first, t + 1)
            link(stt(z, z, gates[:, 1, 2 + t:3 + t], y1[:, 2 + t, :], ALU.mult, ALU.add))
            link(dve.tensor_tensor(z, z, token_major[:, 2, :], ALU.mult))
            dve.tensor_tensor(z, z, token_major[:, t, :], ALU.add).then_inc(z_sum, 1)
        for t in range(2):
            dve.wait_ge(z_std, t + 1)
            link(dve.reciprocal(zss[:, 2, t:t + 1], zss[:, 1, t:t + 1]))
            stt(outt[:, t, :], y2[:, 2 + t, :], zss[:, 2, t:t + 1], token_major[:, 3, :], ALU.mult, ALU.mult).then_inc(out_ready, 1)

    es.close()


_INS = ["x", "c", "ctx", "c_ctx", "w_ada", "b_ada", "g_norm1", "w_in", "lam_qk", "g_subln", "w_attn_out",
        "w_four_out", "w_gate", "b_gate", "w_out", "g_norm2", "w_router", "b_router", "w_e_gate", "w_e_up",
        "w_e_down", "g_final"]


def kernel(**inputs):
    import concourse.bacc as bacc
    from concourse.bass_utils import run_bass_kernel_spmd

    nc = bacc.Bacc("TRN2", target_bir_lowering=False, num_devices=1)
    arrays, args = {}, []
    for name in _INS:
        a = np.ascontiguousarray(inputs[name])
        arrays[f"in_{name}"] = a
        args.append(nc.dram_tensor(f"in_{name}", a.shape, mybir.dt.from_np(a.dtype), kind="ExternalInput").ap())
    arrays["in_consts"] = constants()
    args.append(nc.dram_tensor("in_consts", (P, C_COLS), F32, kind="ExternalInput").ap())
    o = nc.dram_tensor("out_x", (1, SEQ, D), F32, kind="ExternalOutput").ap()
    build(nc, *args, o)
    r = run_bass_kernel_spmd(nc, [arrays], core_ids=[0])
    return r.results[0]["out_x"]
```
